# Optimizing a Trainium2 kernel written in Bass

```python
import math
import jax, jax.numpy as jnp
from jax import lax
import numpy as np

D_MODEL = 1024
BATCH = 1
SEQ = 256
DEPTH = 1

N_BRANCH = 4
BRANCH_W = D_MODEL // 4
HEAD_DIM = 64
POOL_WINDOWS = (2, 4, 8, 16)
POOL_GROUP = BRANCH_W // len(POOL_WINDOWS)
FOX_HEADS = BRANCH_W // HEAD_DIM
DSA_HEADS = BRANCH_W // HEAD_DIM
IDX_HEADS = 4
IDX_DIM = 64
DSA_TOPK = 256
CONV_W = 31
CONV_CH = BRANCH_W
N_GROUPS = 4
EXPERTS_PER_GROUP = 4
N_EXPERTS = N_GROUPS * EXPERTS_PER_GROUP
TOP_K_INNER = 2
D_FF_EXPERT = D_MODEL // 2

Q_BLOCK = 128
LN_EPS = 1e-5
NEG_INF = -1e30
DEEPNORM_ALPHA = (2.0 * DEPTH) ** 0.25
DEEPNORM_BETA = (8.0 * DEPTH) ** -0.25

SPLIT_SIZES = (
    BRANCH_W,
    FOX_HEADS * HEAD_DIM,
    FOX_HEADS * HEAD_DIM,
    FOX_HEADS * HEAD_DIM,
    FOX_HEADS,
    DSA_HEADS * HEAD_DIM,
    HEAD_DIM,
    HEAD_DIM,
    IDX_HEADS * IDX_DIM,
    IDX_DIM,
    IDX_HEADS,
    2 * CONV_CH,
    N_BRANCH * D_MODEL,
)
P_TOTAL = sum(SPLIT_SIZES)

kernel_name = "hybrid_pool_fox_dsa_conv_hmoe_deepnorm"

def layer_norm(x, g, b):
    xf = x.astype(jnp.float32)
    mu = jnp.mean(xf, axis=-1, keepdims=True)
    var = jnp.mean(jnp.square(xf - mu), axis=-1, keepdims=True)
    return ((xf - mu) * lax.rsqrt(var + LN_EPS) * g + b).astype(x.dtype)

def split_columns(p):
    outs, off = [], 0
    for n in SPLIT_SIZES:
        outs.append(p[..., off:off + n])
        off += n
    return outs

def pool_mixer(v, pool_w, pool_scale):
    B, S, C = v.shape
    vf = v.astype(jnp.float32)
    cs = jnp.cumsum(vf, axis=1)
    pos = jnp.arange(1, S + 1, dtype=jnp.float32)
    outs = []
    for g, w in enumerate(POOL_WINDOWS):
        sl = slice(g * POOL_GROUP, (g + 1) * POOL_GROUP)
        csg = cs[..., sl]
        lag = jnp.pad(csg, ((0, 0), (w, 0), (0, 0)))[:, :S]
        cnt = jnp.minimum(pos, float(w))[None, :, None]
        outs.append((csg - lag) / cnt - vf[..., sl])
    pooled = jnp.stack(outs, axis=2).astype(v.dtype)
    mixed = jnp.einsum('bsgc,gcd->bsgd', pooled, pool_w).reshape(B, S, C)
    return mixed * pool_scale

def fox_attention(q, k, v, f_logit):
    B, S, H, Dh = q.shape
    nb = S // Q_BLOCK
    scale = HEAD_DIM ** -0.5
    c = jnp.cumsum(jax.nn.log_sigmoid(f_logit.astype(jnp.float32)), axis=1)
    c_k = c.transpose(0, 2, 1)
    qb = q.reshape(B, nb, Q_BLOCK, H, Dh).swapaxes(0, 1)
    cb = c.reshape(B, nb, Q_BLOCK, H).swapaxes(0, 1)
    kpos = jnp.arange(S)

    def block(args):
        qi, ci, start = args
        qpos = start + jnp.arange(Q_BLOCK)
        s = jnp.einsum('bqhd,bkhd->bhqk', qi, k).astype(jnp.float32) * scale
        s = s + ci.transpose(0, 2, 1)[..., None] - c_k[:, :, None, :]
        s = jnp.where(kpos[None, :] <= qpos[:, None], s, NEG_INF)
        p = jax.nn.softmax(s, axis=-1).astype(v.dtype)
        return jnp.einsum('bhqk,bkhd->bqhd', p, v)

    out = lax.map(block, (qb, cb, jnp.arange(nb) * Q_BLOCK))
    return out.swapaxes(0, 1).reshape(B, S, H * Dh)

def dsa_attention(q, k, v, q_idx, k_idx, w_idx):
    B, S, H, Dh = q.shape
    nb = S // Q_BLOCK
    topk = min(DSA_TOPK, S // 4)
    scale = HEAD_DIM ** -0.5
    slopes = jnp.asarray([2.0 ** (-8.0 * (h + 1) / DSA_HEADS) for h in range(DSA_HEADS)],
                         dtype=jnp.float32)
    qb = q.reshape(B, nb, Q_BLOCK, H, Dh).swapaxes(0, 1)
    qib = q_idx.reshape(B, nb, Q_BLOCK, IDX_HEADS, IDX_DIM).swapaxes(0, 1)
    wib = w_idx.reshape(B, nb, Q_BLOCK, IDX_HEADS).swapaxes(0, 1)
    kpos = jnp.arange(S)
    gather = jax.vmap(lambda a, i: a[i])

    def block(args):
        qi, qii, wi, start = args
        qpos = start + jnp.arange(Q_BLOCK)
        rel = jax.nn.relu(jnp.einsum('bqhd,bkd->bqhk', qii, k_idx).astype(jnp.float32))
        score = jnp.einsum('bqhk,bqh->bqk', rel, wi.astype(jnp.float32))
        score = jnp.where(kpos[None, None, :] <= qpos[None, :, None], score, NEG_INF)
        _, idx = lax.top_k(score, topk)
        k_sel = gather(k, idx)
        v_sel = gather(v, idx)
        logits = jnp.einsum('bqhd,bqkd->bhqk', qi, k_sel).astype(jnp.float32) * scale
        dist = (qpos[None, :, None] - idx).astype(jnp.float32)
        logits = logits - slopes[None, :, None, None] * dist[:, None]
        valid = (idx <= qpos[None, :, None])[:, None]
        logits = jnp.where(valid, logits, NEG_INF)
        p = jax.nn.softmax(logits, axis=-1).astype(v.dtype)
        return jnp.einsum('bhqk,bqkd->bqhd', p, v_sel)

    out = lax.map(block, (qb, qib, wib, jnp.arange(nb) * Q_BLOCK))
    return out.swapaxes(0, 1).reshape(B, S, H * Dh)

def conv_module(a, conv_dw, conv_b, ln_g, ln_b):
    C = CONV_CH
    h = a[..., :C] * jax.nn.sigmoid(a[..., C:])
    y = lax.conv_general_dilated(h, conv_dw[:, None, :].astype(h.dtype), window_strides=(1,),
                                 padding=((CONV_W - 1, 0),),
                                 dimension_numbers=('NWC', 'WIO', 'NWC'),
                                 feature_group_count=C) + conv_b
    return jax.nn.silu(layer_norm(y, ln_g, ln_b))

def hier_moe(x, rg, rg_b, re, re_b, wg, wu, wd):
    B, S, D = x.shape
    t = x.reshape(-1, D)
    pg = jax.nn.softmax((t @ rg).astype(jnp.float32) + rg_b, axis=-1)
    pg_top, g_idx = lax.top_k(pg, 1)
    le = ((t @ re).astype(jnp.float32) + re_b).reshape(-1, N_GROUPS, EXPERTS_PER_GROUP)
    le = jnp.take_along_axis(le, g_idx[:, :, None], axis=1)[:, 0]
    pe_top, e_idx = lax.top_k(jax.nn.softmax(le, axis=-1), TOP_K_INNER)
    pe_top = pe_top / jnp.sum(pe_top, axis=-1, keepdims=True)
    gate = pg_top * pe_top
    expert_id = g_idx * EXPERTS_PER_GROUP + e_idx
    combine = jnp.sum(jax.nn.one_hot(expert_id, N_EXPERTS, dtype=jnp.float32) * gate[..., None],
                      axis=1)
    out = jnp.zeros(t.shape, jnp.float32)
    for e in range(N_EXPERTS):
        h = jax.nn.silu(t @ wg[e]) * (t @ wu[e])
        out = out + combine[:, e:e + 1] * (h @ wd[e]).astype(jnp.float32)
    return out.astype(x.dtype).reshape(B, S, D)

def setup_inputs(seed: int = 0) -> dict:
    key = jax.random.key(seed)
    ks = jax.random.split(key, 32)
    L, D = DEPTH, D_MODEL
    f32 = jnp.float32
    nrm = lambda k, shape, s: (jax.random.normal(k, shape, f32) * s)
    return {
        "x": nrm(ks[0], (BATCH, SEQ, D), 1.0),
        "ln_in_g": 1.0 + nrm(ks[1], (D,), 0.05),
        "ln_in_b": nrm(ks[2], (D,), 0.05),
        "w_in": nrm(ks[3], (L, D, P_TOTAL), D ** -0.5),
        "b_forget": 3.0 + nrm(ks[4], (L, FOX_HEADS), 0.5),
        "b_gate": nrm(ks[5], (L, N_BRANCH * D), 0.1),
        "pool_w": nrm(ks[6], (L, len(POOL_WINDOWS), POOL_GROUP, POOL_GROUP), POOL_GROUP ** -0.5),
        "pool_scale": 1.0 + nrm(ks[7], (L, BRANCH_W), 0.1),
        "conv_dw": nrm(ks[8], (L, CONV_W, CONV_CH), CONV_W ** -0.5),
        "conv_b": nrm(ks[9], (L, CONV_CH), 0.02),
        "conv_ln_g": 1.0 + nrm(ks[10], (L, CONV_CH), 0.05),
        "conv_ln_b": nrm(ks[11], (L, CONV_CH), 0.05),
        "w_branch": nrm(ks[12], (L, N_BRANCH, BRANCH_W, D), BRANCH_W ** -0.5),
        "w_out": nrm(ks[13], (L, D, D), D ** -0.5 * DEEPNORM_BETA),
        "ln1_g": 1.0 + nrm(ks[14], (L, D), 0.05),
        "ln1_b": nrm(ks[15], (L, D), 0.05),
        "router_g": nrm(ks[16], (L, D, N_GROUPS), D ** -0.5),
        "router_g_b": nrm(ks[17], (L, N_GROUPS), 0.01),
        "router_e": nrm(ks[18], (L, D, N_EXPERTS), D ** -0.5),
        "router_e_b": nrm(ks[19], (L, N_EXPERTS), 0.01),
        "expert_w_gate": nrm(ks[20], (L, N_EXPERTS, D, D_FF_EXPERT), D ** -0.5),
        "expert_w_up": nrm(ks[21], (L, N_EXPERTS, D, D_FF_EXPERT), D ** -0.5),
        "expert_w_down": nrm(ks[22], (L, N_EXPERTS, D_FF_EXPERT, D), D_FF_EXPERT ** -0.5 * DEEPNORM_BETA),
        "ln2_g": 1.0 + nrm(ks[23], (L, D), 0.05),
        "ln2_b": nrm(ks[24], (L, D), 0.05),
    }

def reference(x, ln_in_g, ln_in_b, w_in, b_forget, b_gate, pool_w, pool_scale, conv_dw, conv_b,
              conv_ln_g, conv_ln_b, w_branch, w_out, ln1_g, ln1_b, router_g, router_g_b,
              router_e, router_e_b, expert_w_gate, expert_w_up, expert_w_down, ln2_g, ln2_b):
    B, S, D = x.shape
    h = layer_norm(x, ln_in_g, ln_in_b)
    for l in range(DEPTH):
        (pool_v, fq, fk, fv, ff, dq, dk, dv, iq, ik, iw, conv_in, gate) = split_columns(h @ w_in[l])
        br_a = pool_mixer(pool_v, pool_w[l], pool_scale[l])
        br_b = fox_attention(fq.reshape(B, S, FOX_HEADS, HEAD_DIM),
                             fk.reshape(B, S, FOX_HEADS, HEAD_DIM),
                             fv.reshape(B, S, FOX_HEADS, HEAD_DIM),
                             ff + b_forget[l])
        br_c = dsa_attention(dq.reshape(B, S, DSA_HEADS, HEAD_DIM), dk, dv,
                             iq.reshape(B, S, IDX_HEADS, IDX_DIM), ik, iw)
        br_d = conv_module(conv_in, conv_dw[l], conv_b[l], conv_ln_g[l], conv_ln_b[l])
        branches = jnp.stack([br_a, br_b.astype(br_a.dtype), br_c.astype(br_a.dtype),
                              br_d.astype(br_a.dtype)], axis=2)
        up = jnp.einsum('bsnc,ncd->bsnd', branches, w_branch[l])
        g = jax.nn.sigmoid(gate.reshape(B, S, N_BRANCH, D) + b_gate[l].reshape(N_BRANCH, D))
        mixed = jnp.sum(g * up, axis=2) @ w_out[l]
        h = layer_norm(DEEPNORM_ALPHA * h + mixed, ln1_g[l], ln1_b[l])
        moe = hier_moe(h, router_g[l], router_g_b[l], router_e[l], router_e_b[l],
                       expert_w_gate[l], expert_w_up[l], expert_w_down[l])
        h = layer_norm(DEEPNORM_ALPHA * h + moe, ln2_g[l], ln2_b[l])
    return h


_drawn_inputs = setup_inputs


def setup_inputs(seed=0):
    import zlib

    import numpy as np

    out = dict(_drawn_inputs(seed))
    spreads = {}
    factors = {'b_forget': 37.096,
     'b_gate': 3.403,
     'conv_b': 5.38,
     'conv_ln_g': 3.383,
     'conv_ln_b': 5.323,
     'router_g_b': 24.32,
     'router_e_b': 24.201}
    for name, (base, spread) in spreads.items():
        noise = np.random.default_rng([zlib.crc32(name.encode()), seed]).standard_normal(out[name].shape)
        drawn = base * np.exp(spread * noise) if base else spread * noise
        out[name] = __import__('jax').numpy.asarray(drawn.astype(out[name].dtype))
    for name, factor in factors.items():
        out[name] = (out[name] * factor).astype(out[name].dtype)
    return out
```

```python
import concourse.bass as bass
from concourse import mybir
from contextlib import ExitStack


def hybrid_trunk_kernel(nc: bass.Bass, a: dict, out: bass.AP):
    F32 = mybir.dt.float32
    I32 = mybir.dt.int32
    ALU = mybir.AluOpType
    ACT = mybir.ActivationFunctionType
    AX = mybir.AxisListType

    P = 128
    T, D = a["x"].shape[1], a["x"].shape[2]
    TB = T // P
    KC = D // P
    HALF = 512
    BW = D // 4
    DH = 64
    NH = BW // DH
    CONV_W = a["conv_dw"].shape[1]
    PADC = CONV_W - 1
    PADP = 16
    NB = 4
    NG = a["router_g"].shape[2]
    NE = a["router_e"].shape[2]
    EPG = NE // NG
    DFF = a["expert_w_gate"].shape[3]
    FC = DFF // P
    PAIRS = NE // 2
    CAP = 64
    PASSES = T // CAP
    TOPK = min(256, T // 4)
    ROUNDS = TOPK // 8
    NEG = -1e30
    TAKEN = -3e38
    EPS = 1e-5
    ALPHA = 2.0 ** 0.25
    SCALE = float(DH) ** -0.5
    SLOPES = [2.0 ** (-8.0 * (h + 1) / NH) for h in range(NH)]
    WINDOWS = (2, 4, 8, 16)

    sizes = dict(pool=BW, fq=BW, fk=BW, fv=BW, ff=NH, dq=BW, dk=DH, dv=DH, iq=BW, ik=DH, iw=NH,
                 conv=2 * BW, gate=NB * D)
    col, at = {}, 0
    for name, n in sizes.items():
        col[name] = at
        at += n

    x_v = a["x"][0].rearrange("(t p) d -> p t d", p=P)
    w_in = a["w_in"][0].rearrange("(k p) n -> p k n", p=P)
    w_br = a["w_branch"][0].rearrange("n (k p) d -> p (n k) d", p=P)
    w_out = a["w_out"][0].rearrange("(k p) d -> p k d", p=P)
    e_gate = a["expert_w_gate"][0].rearrange("e (k p) f -> p e k f", p=P)
    e_up = a["expert_w_up"][0].rearrange("e (k p) f -> p e k f", p=P)
    e_down = a["expert_w_down"][0].rearrange("e (k p) d -> p e k d", p=P)
    out_v = out[0].rearrange("(t p) d -> p t d", p=P)

    vec_src, ROW, at = [], {}, 0
    for name, src in (("conv_dw", a["conv_dw"][0].rearrange("w (c p) -> (w c) p", p=P)),
                      ("pool_scale", a["pool_scale"][0].rearrange("(c p) -> c p", p=P)),
                      ("conv_b", a["conv_b"][0].rearrange("(c p) -> c p", p=P)),
                      ("conv_ln_g", a["conv_ln_g"][0].rearrange("(c p) -> c p", p=P)),
                      ("conv_ln_b", a["conv_ln_b"][0].rearrange("(c p) -> c p", p=P)),
                      ("ln_in_g", a["ln_in_g"].rearrange("(c p) -> c p", p=P)),
                      ("ln_in_b", a["ln_in_b"].rearrange("(c p) -> c p", p=P)),
                      ("ln1_g", a["ln1_g"][0].rearrange("(c p) -> c p", p=P)),
                      ("ln1_b", a["ln1_b"][0].rearrange("(c p) -> c p", p=P))):
        ROW[name] = at
        vec_src.append((at, src))
        at += src.shape[0]
    NROW = at

    ctx = ExitStack()
    with ctx:
        def sb(name, shape, dt=F32):
            return ctx.enter_context(nc.sbuf_tensor(name, shape, dt))

        def sem(name):
            return ctx.enter_context(nc.semaphore(name))

        SLOTS = 6
        ring = sb("ring", [P, SLOTS, KC * HALF])
        gates = sb("gates", [P, 2, KC * HALF])
        gflat = gates[:, :, :].rearrange("p a n -> p (a n)")
        place = {0: 0, 1: KC * HALF, 2: 0}

        def early(part, shape, rows=P):
            n = 1
            for d in shape:
                n *= d
            at = place[part]
            place[part] += n
            assert place[part] <= (1 if part == 0 else 2) * KC * HALF
            v = gflat[0:rows, at:at + n]
            if len(shape) == 2:
                v = v.rearrange("p (a b) -> p a b", b=shape[1])
            if len(shape) == 3:
                v = v.rearrange("p (a b c) -> p a b c", b=shape[1], c=shape[2])
            return v

        hT = sb("hT", [P, KC, T])
        hn = sb("hn", [P, TB, D])
        work = sb("work", [P, TB, D])
        lnp = sb("lnp", [P, 2, D])
        bgate = sb("bgate", [P, 2, HALF])
        vrows = early(0, [P], NROW)
        vcol = sb("vcol", [P, NROW])
        ident = sb("ident", [P, P])
        tri = sb("tri", [P, 3 * P])
        causal = sb("causal", [P, T])
        dist = sb("dist", [P, T])
        disti = early(0, [T]).bitcast(I32)
        rcnt = sb("rcnt", [P, 2, T])
        slot_no = sb("slot_no", [P, CAP])
        desc4 = sb("desc4", [P, NG])
        bforget = sb("bforget", [P, NH])
        rbias = sb("rbias", [P, NG + NE])
        rw = sb("rw", [P, KC, NG + NE])
        poolw = sb("poolw", [P, 2, DH])
        iqT = early(0, [2, T])
        ikT = early(0, [T])
        dqT = sb("dqT", [P, 2, T])
        dkT = sb("dkT", [P, T])
        fqT = early(0, [2, T])
        fkT = early(1, [2, T])
        fv = early(1, [TB, BW])
        misc = sb("misc", [P, TB, DH + 2 * NH])
        wflat = work[:, :, :].rearrange("p a n -> p (a n)")
        poolv, *pooled = [wflat[:, i * 2 * (PADP + T):(i + 1) * 2 * (PADP + T)]
                          .rearrange("p (c t) -> p c t", c=2) for i in range(3)]
        glu = sb("glu", [P, 2, T])
        hpad = sb("hpad", [P, 2, PADC + T])
        convy = sb("convy", [P, 2, T])
        brT = sb("brT", [P, NB, 2, T])
        fs = sb("fs", [P, 6, TB, NH])
        lsb = early(0, [TB, NH, P])
        cq = sb("cq", [P, TB, NH])
        fbias0 = early(1, [NH, P])
        fbias1 = early(1, [NH, T])
        rel = early(0, [NH, T])
        score = [sb(f"score{b}", [P, (b + 1) * P]) for b in range(TB)]
        top8 = sb("top8", [P, 8])
        logit = [sb("logit0", [P, NH, P]), sb("logit1", [P, NH, T])]
        alibi = sb("alibi", [P, NH, T])
        probT = sb("probT", [P, 2, NH * P])
        tmp = probT
        smx = sb("smx", [P, 2, TB, 3, NH])
        stats = sb("stats", [P, TB, 2, 6])
        mv = sb("mv", [P, TB, 5])
        lg = early(2, [TB, NG + NE])
        xg = early(2, [KC, P])
        rt = early(2, [16, TB, NE])
        rankp = early(2, [PASSES * PAIRS + 1, TB, 2])
        wpair = early(2, [PASSES * PAIRS, TB, 2])
        disp = early(2, [TB, 2, CAP])
        dispw = early(2, [TB, 2, CAP])
        comb = early(2, [TB * P])
        silu_g = early(2, [DFF])
        hexp = early(2, [DFF])
        hexT = early(2, [FC * P])
        yexp = early(2, [D])
        npass_f = sb("npass_f", [P, 8])
        npass_i = sb("npass_i", [P, 1], I32)
        acc = hn

        bank = ctx.enter_context(nc.psum_tensor("bank", [P, 8, HALF], F32))

        def pair_bank(i):
            return bank[:, i:i + 2, :].rearrange("p a (j k) -> p (a j) k", j=2)

        s_x = [sem(f"x_loaded{t}") for t in range(TB)]
        s_vr = sem("vector_rows_loaded")
        s_small = sem("small_params_loaded")
        s_slot = [sem(f"slot{i}_loaded") for i in range(SLOTS)]
        s_lnp = sem("ln_params_loaded")
        s_bg = [sem(f"bgate{i}_loaded") for i in range(2)]
        s_wout = [sem(f"w_out{i}_loaded") for i in range(2)]
        s_const = sem("constants_built")
        s_ppad = sem("pool_rows_padded")
        s_idf = sem("identity_built")
        s_vT = sem("vector_rows_turned")
        s_vcol = sem("vector_columns_ready")
        s_var = sem("row_variance_ready")
        s_std = sem("row_std_ready")
        s_z = sem("x_normalised")
        s_xT = sem("x_turned")
        s_hTa = sem("hT_by_scalar")
        s_hTd = sem("hT_by_vector")
        s_hn = sem("hn_ready")
        UNITS = ["iq", "ik", "misc", "dq", "dk", "fq", "fk", "fv", "pool", "convb", "conva"]
        s_unit = sem("unit_projected")
        s_uout = {u: sem(f"{u}_out_of_psum") for u in UNITS}
        s_gate = sem("gate_projected")
        s_gout = sem("gate_out_of_psum")
        s_gbias = sem("gate_biased")
        s_gsig = sem("gate_sigmoid_done")
        s_idx = sem("indexer_scores_in_psum")
        s_rel = sem("indexer_relu_done")
        s_relu_used = sem("indexer_relu_used")
        s_sel = sem("selection_done")
        s_ls = sem("log_sigmoid_steps")
        s_lsa = sem("log_sigmoid_by_scalar")
        s_lsb = sem("log_sigmoid_spread")
        s_cum = sem("cumulated_in_psum")
        s_cumo = sem("cumulated_out_of_psum")
        s_s = sem("attention_scores_in_psum")
        s_lg = sem("logits_ready")
        s_exp = sem("exponentials_done")
        s_prob = sem("probabilities_ready")
        s_pT = sem("probabilities_turned")
        s_pTo = sem("turned_probabilities_out")
        s_pv = sem("values_weighted")
        s_att = sem("attention_branch_ready")
        s_poolin = sem("pool_means_ready")
        s_poolmm = sem("pool_mixed")
        s_poolo = sem("pool_branch_ready")
        s_glu = sem("glu_padded")
        s_conv = sem("convolution_done")
        s_cT = sem("convolution_turned")
        s_cz = sem("convolution_normalised")
        s_czT = sem("convolution_turned_back")
        s_cbr = sem("convolution_branch_ready")
        s_up = sem("branch_projected")
        s_mix = sem("branch_merged")
        s_mT = sem("merged_turned")
        s_mTo = sem("merged_turned_out")
        s_o = sem("output_projected")
        s_y1 = sem("residual_added")
        s_z1 = sem("layer1_normalised")
        s_zT = sem("layer1_turned")
        s_h1Ta = sem("layer1_turned_by_scalar")
        s_h1Td = sem("layer1_turned_by_vector")
        s_h1 = sem("layer1_output_ready")
        s_rt = sem("router_logits_in_psum")
        s_re = sem("router_exp_argument")
        s_rex = sem("router_exp_done")
        s_mask = sem("expert_mask_ready")
        s_rank = sem("ranks_in_psum")
        s_tab = sem("tables_ready")
        s_np = sem("passes_known")
        m_disp = sem("dispatch_ready")
        m_dispw = sem("weighted_dispatch_ready")
        m_xg = sem("tokens_gathered")
        m_xgo = sem("gathered_out_of_psum")
        m_g = sem("expert_gate_in_psum")
        m_u = sem("expert_up_in_psum")
        m_silu = sem("expert_silu_done")
        m_h = sem("expert_hidden_ready")
        m_hT = sem("expert_hidden_turned")
        m_hTo = sem("expert_hidden_turned_out")
        m_cT = sem("combine_turned")
        m_cTo = sem("combine_turned_out")
        m_y = sem("expert_output_in_psum")
        m_ya = sem("expert_output_out_by_scalar")
        m_yd = sem("expert_output_out_by_vector")
        m_c = sem("combined_in_psum")
        m_acc = sem("combined_added")
        s_acc0 = sem("residual_sum_started")
        s_dch = sem("vector_chain")
        s_pch = sem("gpsimd_chain")
        s_ach = sem("scalar_chain")
        s_fin = sem("output_rows_ready")
        s_out = sem("output_stored")

        block = ctx.enter_context(nc.Block())

        FRONT = ["s_idx", "s_dsa", "s_fox", "s_val", "s_conv"] + [f"g{t}" for t in range(8)] + ["wb0", "wb1"]
        SLOT = {name: n % SLOTS for n, name in enumerate(FRONT)}
        LOAD = {name: n // SLOTS + 1 for n, name in enumerate(FRONT)}
        FIRST = [sum(1 for n in range(len(FRONT)) if n % SLOTS == s) for s in range(SLOTS)]

        def slot(name, cols=HALF):
            return ring[:, SLOT[name], 0:KC * cols].rearrange("p (k n) -> p k n", n=cols)

        def loaded(eng, name):
            eng.wait_ge(s_slot[SLOT[name]], 16 * LOAD[name])

        IDXC, DSAC = BW + DH, BW + 2 * DH + 2 * NH

        USED = {"s_idx": (s_unit, 2), "s_dsa": (s_unit, 5), "s_fox": (s_unit, 7), "s_val": (s_unit, 9),
                "s_conv": (s_unit, 11)}
        USED.update({f"g{t}": (s_gate, 2 * t + 2) for t in range(8)})
        USED.update({f"wb{q}": (s_up, 8 * q + 8) for q in range(2)})

        def slot_free(eng, n):
            if n >= SLOTS:
                eng.wait_ge(*USED[FRONT[n - SLOTS]])

        def expert_slot(s, n):
            return ring[:, s, :].rearrange("p (k n) -> p k n", n=n)

        @block.sync
        def _(sp):
            for t in range(TB):
                sp.dma_start(work[:, t, :], x_v[:, t, :]).then_inc(s_x[t], 16)
            sp.dma_start(slot("s_idx", IDXC), w_in[:, :, col["iq"]:col["iq"] + IDXC])\
                .then_inc(s_slot[0], 16)
            d = slot("s_dsa", DSAC)
            n = BW + 2 * DH
            sp.dma_start(d[:, :, 0:n], w_in[:, :, col["dq"]:col["dq"] + n]).then_inc(s_slot[1], 16)
            sp.dma_start(d[:, :, n:n + NH], w_in[:, :, col["iw"]:col["iw"] + NH]).then_inc(s_slot[1], 16)
            sp.dma_start(d[:, :, n + NH:n + 2 * NH], w_in[:, :, col["ff"]:col["ff"] + NH])\
                .then_inc(s_slot[1], 16)
            sp.dma_start(slot("s_fox"), w_in[:, :, col["fq"]:col["fq"] + 2 * BW]).then_inc(s_slot[2], 16)
            v = slot("s_val")
            sp.dma_start(v[:, :, 0:BW], w_in[:, :, col["pool"]:col["pool"] + BW]).then_inc(s_slot[3], 16)
            sp.dma_start(v[:, :, BW:2 * BW], w_in[:, :, col["fv"]:col["fv"] + BW]).then_inc(s_slot[3], 16)
            sp.dma_start(slot("s_conv"), w_in[:, :, col["conv"]:col["conv"] + 2 * BW])\
                .then_inc(s_slot[4], 16)
            for t in range(8):
                dq, n = divmod(t, NB)
                if t >= 2:
                    sp.wait_ge(s_gbias, t - 1)
                c = n * D + dq * HALF
                sp.dma_start(bgate[:, t % 2, :],
                             a["b_gate"][0][c:c + HALF].partition_broadcast(P)).then_inc(s_bg[t % 2], 16)
                slot_free(sp, 5 + t)
                c += col["gate"]
                sp.dma_start(slot(f"g{t}"), w_in[:, :, c:c + HALF]).then_inc(s_slot[SLOT[f"g{t}"]], 16)
            for dq in range(2):
                slot_free(sp, 13 + dq)
                sp.dma_start(slot(f"wb{dq}"), w_br[:, :, dq * HALF:(dq + 1) * HALF])\
                    .then_inc(s_slot[SLOT[f"wb{dq}"]], 16)
            sources = [e_gate[:, 0], e_gate[:, 1], e_up[:, 0], e_up[:, 1], e_down[:, 0], e_down[:, 1]]
            widths = [DFF, DFF, DFF, DFF, D, D]
            order = [(len(FRONT) + i) % SLOTS for i in range(SLOTS)]
            for i, s in enumerate(order):
                slot_free(sp, len(FRONT) + i)
                if i == 4:
                    sp.wait_ge(s_mix, 4 * NB // 2)
                    sp.dma_start(gates[:, 0, :].rearrange("p (k n) -> p k n", n=HALF),
                                 w_out[:, :, 0:HALF]).then_inc(s_wout[0], 16)
                sp.dma_start(expert_slot(s, widths[s]), sources[s]).then_inc(s_slot[s], 16)
            sp.wait_ge(s_mix, 4 * NB)
            sp.dma_start(gates[:, 1, :].rearrange("p (k n) -> p k n", n=HALF),
                         w_out[:, :, HALF:D]).then_inc(s_wout[1], 16)

            def load_pair(it, pair):
                for s, (src, used, w) in enumerate(((e_gate, m_g, DFF), (e_gate, m_g, DFF),
                                                    (e_up, m_u, DFF), (e_up, m_u, DFF),
                                                    (e_down, m_y, D), (e_down, m_y, D))):
                    if s % 2 == 0:
                        sp.wait_ge(used, it)
                    sp.dma_start(expert_slot(s, w),
                                 src[:, bass.ds(2 * pair + s % 2, 1)].rearrange("p e k f -> p (e k) f"))\
                        .then_inc(s_slot[s], 16)

            with sp.Fori(1, PAIRS) as pair:
                load_pair(pair, pair)
            sp.wait_ge(s_np, 1)
            npass = sp.value_load(npass_i[0:1, 0:1], min_val=1, max_val=PASSES)
            with sp.If(npass > 1):
                with sp.Fori(1, npass) as again:
                    with sp.Fori(0, PAIRS) as pair:
                        load_pair(sp.snap(again * PAIRS + pair), pair)
            sp.wait_ge(s_fin, TB)
            for t in range(TB):
                sp.dma_start(out_v[:, t, :], work[:, t, :]).then_inc(s_out, 16)
            sp.wait_ge(s_out, 16 * TB)

        @block.gpsimd
        def _(pool):
            n = [0]

            def link(ins):
                n[0] += 1
                ins.then_inc(s_pch, 1)
                pool.wait_ge(s_pch, n[0])

            link(pool.memset(ident[:, :], 0.0))
            pool.affine_select(out=ident[:, :], in_=ident[:, :], compare_op=ALU.not_equal, fill=1.0, base=0,
                               pattern=[[-1, P]], channel_multiplier=1).then_inc(s_idf, 1)
            link(pool.memset(causal[:, :], 0.0))
            link(pool.affine_select(out=causal[:, :], in_=causal[:, :], compare_op=ALU.is_ge, fill=NEG,
                                    base=P, pattern=[[-1, T]], channel_multiplier=1))
            link(pool.iota(disti[:, :], [[-1, T]], base=P, channel_multiplier=1))
            link(pool.tensor_copy(dist[:, :], disti[:, :]))
            link(pool.memset(tri[:, :], 1.0))
            link(pool.affine_select(out=tri[:, :], in_=tri[:, :], compare_op=ALU.is_ge, fill=0.0,
                                    base=-P, pattern=[[1, 3 * P]], channel_multiplier=-1))
            link(pool.iota(disti[:, :], [[1, T]], base=1, channel_multiplier=0))
            for g, w in enumerate(WINDOWS):
                r = slice(DH * (g % 2), DH * (g % 2) + DH)
                link(pool.tensor_scalar(rcnt[r, g // 2, :], disti[r, :], float(w), None, ALU.min))
            link(pool.iota(disti[:, 0:CAP], [[1, CAP]], base=0, channel_multiplier=0))
            link(pool.tensor_copy(slot_no[:, :], disti[:, 0:CAP]))
            link(pool.iota(disti[:, 0:NG], [[-1, NG]], base=NG, channel_multiplier=0))
            link(pool.tensor_copy(desc4[:, :], disti[:, 0:NG]))
            pool.memset(hpad[:, :, 0:PADC], 0.0).then_inc(s_const, 1)

            def affine(t, ready, done):
                pool.wait_ge(ready, t + 1)
                link(pool.tensor_tensor(hn[:, t, :], work[:, t, :], lnp[:, 0, :], ALU.mult))
                pool.tensor_tensor(hn[:, t, :], hn[:, t, :], lnp[:, 1, :], ALU.add).then_inc(done, 1)

            pool.wait_ge(s_lnp, 32)
            for t in range(TB):
                affine(t, s_z, s_hn)
            pool.wait_ge(s_xT, 4)
            pool.wait_ge(s_hn, TB)
            pool.memset(poolv[:, :, 0:PADP], 0.0)
            pool.memset(pooled[0][:, :, 0:PADP], 0.0)
            pool.memset(pooled[1][:, :, 0:PADP], 0.0).then_inc(s_ppad, 1)
            for t in range(8):
                dq, nb = divmod(t, NB)
                pool.wait_ge(s_bg[t % 2], 16 * (t // 2 + 1))
                pool.wait_ge(s_gout, 2 * (t + 1))
                g = gates[:, dq, :].rearrange("p (t n c) -> p t n c", t=TB, n=NB)[:, :, nb, :]
                pool.tensor_tensor(g, g, bgate[:, t % 2, :].unsqueeze(1).broadcast_to([P, TB, HALF]),
                                   ALU.add).then_inc(s_gbias, 1)

        @block.scalar
        def _(act):
            for r, src in vec_src:
                act.dma_start(vrows[r:r + src.shape[0], :], src).then_inc(s_vr, 16)
            act.dma_start(bforget[:, :], a["b_forget"][0].partition_broadcast(P)).then_inc(s_small, 16)
            act.dma_start(rbias[:, 0:NG], a["router_g_b"][0].partition_broadcast(P)).then_inc(s_small, 16)
            act.dma_start(rbias[:, NG:NG + NE], a["router_e_b"][0].partition_broadcast(P)).then_inc(s_small, 16)
            pw = a["pool_w"][0]
            for g in range(4):
                act.dma_start(poolw[DH * (g % 2):DH * (g % 2) + DH, g // 2, :], pw[g]).then_inc(s_small, 16)
            act.dma_start(lnp[:, 0, :], a["ln_in_g"].partition_broadcast(P)).then_inc(s_lnp, 16)
            act.dma_start(lnp[:, 1, :], a["ln_in_b"].partition_broadcast(P)).then_inc(s_lnp, 16)
            act.dma_start(rw[:, :, 0:NG], a["router_g"][0].rearrange("(k p) n -> p k n", p=P)).then_inc(s_small, 16)
            act.dma_start(rw[:, :, NG:NG + NE], a["router_e"][0].rearrange("(k p) n -> p k n", p=P))\
                .then_inc(s_small, 16)

            nln = [0]

            def root():
                nln[0] += 1
                act.wait_ge(s_var, TB * nln[0])
                act.activation(mv[:, :, 3:4], mv[:, :, 2:3], ACT.Sqrt).then_inc(s_std, 1)

            root()
            act.wait_ge(s_vcol, 1)
            act.wait_ge(s_xT, 4)
            for k in range(4):
                act.activation(hT[:, k, :], bank[:, k // 2, (k % 2) * T:(k % 2 + 1) * T], ACT.Identity,
                               bias=vcol[:, ROW["ln_in_b"] + k:ROW["ln_in_b"] + k + 1],
                               scale=vcol[:, ROW["ln_in_g"] + k:ROW["ln_in_g"] + k + 1]).then_inc(s_hTa, 1)

            unit_bank = {u: 2 + i % 2 for i, u in enumerate(UNITS)}

            def unit(name):
                act.wait_ge(s_unit, UNITS.index(name) + 1)
                return bank[:, unit_bank[name], :].rearrange("p (c t) -> p c t", c=2)

            def relu(b):
                act.wait_ge(s_idx, b + 1)
                if b:
                    act.wait_ge(s_relu_used, b)
                n = (b + 1) * P
                act.activation(rel[:, :, 0:n], pair_bank(4)[:, :, 0:n], ACT.Relu).then_inc(s_rel, 1)

            u = unit("iq")
            act.activation(iqT[:, :, :], u, ACT.Copy).then_inc(s_uout["iq"], 1)
            for name, dst in (("ik", ikT),):
                u = unit(name)
                act.activation(dst[0:DH, :], u[0:DH, 0, :], ACT.Copy)
                act.activation(dst[DH:P, :], u[0:DH, 0, :], ACT.Copy).then_inc(s_uout[name], 1)
            u = unit("misc")
            act.activation(misc[:, :, :], u[:, :, 0:DH + 2 * NH], ACT.Copy).then_inc(s_uout["misc"], 1)
            relu(0)
            act.wait_ge(s_ls, 1)
            act.activation(fs[:, 2], fs[:, 1], ACT.Exp, scale=-1.0).then_inc(s_lsa, 1)
            u = unit("dq")
            act.activation(dqT[:, :, :], u, ACT.Copy, scale=SCALE).then_inc(s_uout["dq"], 1)
            act.wait_ge(s_ls, 2)
            act.activation(fs[:, 4], fs[:, 3], ACT.Ln).then_inc(s_lsa, 1)
            relu(1)
            u = unit("dk")
            act.activation(dkT[0:DH, :], u[0:DH, 0, :], ACT.Copy)
            act.activation(dkT[DH:P, :], u[0:DH, 0, :], ACT.Copy).then_inc(s_uout["dk"], 1)
            u = unit("fq")
            act.activation(fqT[:, :, :], u, ACT.Copy, scale=SCALE).then_inc(s_uout["fq"], 1)
            u = unit("fk")
            act.activation(fkT[:, :, :], u, ACT.Copy).then_inc(s_uout["fk"], 1)
            u = unit("fv")
            act.activation(fv[:, :, :], u, ACT.Copy).then_inc(s_uout["fv"], 1)

            def exps(i):
                b = i % TB
                n = (b + 1) * P
                act.wait_ge(s_lg, i + 1)
                for hh in range(NH):
                    last = act.activation(logit[b][:, hh, 0:n], logit[b][:, hh, 0:n], ACT.Exp,
                                          bias=smx[:, i // TB, b, 0, hh:hh + 1],
                                          accum_out=smx[:, i // TB, b, 1, hh:hh + 1])
                last.then_inc(s_exp, 1)

            nturn = [0]

            def turned(kc):
                i = nturn[0]
                nturn[0] += 1
                act.wait_ge(s_pT, i + 1)
                need = {1: 1, 2: 1, 3: 2, 4: 3, 5: 3}.get(i)
                if need:
                    act.wait_ge(s_pv, need)
                act.activation(probT[:, kc, :], bank[:, 6, :], ACT.Copy).then_inc(s_pTo, 1)

            def branch(i):
                act.wait_ge(s_pv, 2 * (i + 1))
                act.activation(brT[:, 1 + i], bank[:, 7, :].rearrange("p (j t) -> p j t", j=2),
                               ACT.Copy).then_inc(s_att, 1)

            def gate_out(t):
                dq, nb = divmod(t, NB)
                g = gates[:, dq, :].rearrange("p (t n c) -> p t n c", t=TB, n=NB)
                for b in range(TB):
                    act.wait_ge(s_gate, 2 * t + b + 1)
                    act.activation(g[:, b, nb, :], bank[:, b, :], ACT.Copy).then_inc(s_gout, 1)

            exps(0)
            act.wait_ge(s_ppad, 1)
            u = unit("pool")
            act.activation(poolv[:, :, PADP:PADP + T], u, ACT.Copy).then_inc(s_uout["pool"], 1)
            exps(1)
            u = unit("convb")
            act.activation(glu[:, :, :], u, ACT.Sigmoid).then_inc(s_uout["convb"], 1)
            gate_out(0)
            turned(0)
            gate_out(1)
            turned(0)
            turned(1)
            branch(0)
            gate_out(2)
            gate_out(3)
            exps(2)
            turned(0)
            gate_out(4)
            exps(3)
            turned(0)
            turned(1)
            branch(1)
            gate_out(5)
            act.wait_ge(s_poolmm, 1)
            for q in range(2):
                r = slice(DH * q, DH * q + DH)
                for j in range(2):
                    c = ROW["pool_scale"] + j
                    last = act.activation(brT[r, 0, j, :], bank[r, 2 + q, j * T:(j + 1) * T],
                                          ACT.Copy, scale=vcol[r, c:c + 1])
            last.then_inc(s_poolo, 1)
            gate_out(6)
            gate_out(7)

            root()

            def sig(t):
                dq, nb = divmod(t, NB)
                act.wait_ge(s_gbias, t + 1)
                g = gates[:, dq, :].rearrange("p (t n c) -> p t n c", t=TB, n=NB)[:, :, nb, :]
                act.activation(g, g, ACT.Sigmoid).then_inc(s_gsig, 1)

            for t in range(8):
                sig(t)
            act.wait_ge(s_czT, 1)
            for c in range(2):
                last = act.activation(brT[:, 3, c, :], bank[:, 7, c * T:(c + 1) * T], ACT.Silu,
                                      bias=vcol[:, ROW["conv_ln_b"] + c:ROW["conv_ln_b"] + c + 1],
                                      scale=vcol[:, ROW["conv_ln_g"] + c:ROW["conv_ln_g"] + c + 1])
            last.then_inc(s_cbr, 1)
            act.wait_ge(s_hn, TB)
            act.dma_start(lnp[:, 0, :], a["ln1_g"][0].partition_broadcast(P)).then_inc(s_lnp, 16)
            act.dma_start(lnp[:, 1, :], a["ln1_b"][0].partition_broadcast(P)).then_inc(s_lnp, 16)
            for i in range(4):
                act.wait_ge(s_mT, i + 1)
                act.activation(hT[:, 2 * i:2 * i + 2, :],
                               bank[:, 4 + i % 2, :].rearrange("p (c t) -> p c t", c=2), ACT.Copy)\
                    .then_inc(s_mTo, 1)
            root()
            act.wait_ge(s_zT, 4)
            for k in range(4):
                act.activation(hT[:, k, :], bank[:, 4 + k // 2, (k % 2) * T:(k % 2 + 1) * T], ACT.Identity,
                               bias=vcol[:, ROW["ln1_b"] + k:ROW["ln1_b"] + k + 1],
                               scale=vcol[:, ROW["ln1_g"] + k:ROW["ln1_g"] + k + 1]).then_inc(s_h1Ta, 1)
            act.wait_ge(s_re, 1)
            act.activation(rt[:, 8, :, 0:NG + 1], rt[:, 7, :, 0:NG + 1], ACT.Exp).then_inc(s_rex, 1)
            act.wait_ge(s_h1, TB)
            act.dma_start(lnp[:, 0, :], a["ln2_g"][0].partition_broadcast(P)).then_inc(s_lnp, 16)
            act.dma_start(lnp[:, 1, :], a["ln2_b"][0].partition_broadcast(P)).then_inc(s_lnp, 16)
            act.wait_ge(s_np, 1)
            npass = act.value_load(npass_i[0:1, 0:1], min_val=1, max_val=PASSES)
            with act.Fori(0, act.snap(npass * PAIRS)) as it:
                act.wait_ge(m_g, it + 1)
                act.activation(silu_g[:, :], bank[:, 0, :], ACT.Silu).then_inc(m_silu, 1)
                act.wait_ge(m_y, it + 1)
                act.activation(yexp[:, HALF:D], bank[:, 6, :], ACT.Copy).then_inc(m_ya, 1)
            root()

        @block.tensor
        def _(pe):
            pe.wait_ge(s_idf, 1)
            pe.wait_ge(s_vr, 16 * len(vec_src))
            pe.transpose(bank[:, 4, 0:NROW], vrows[:, :], ident[0:NROW, 0:NROW]).then_inc(s_vT, 1)
            for t in range(TB):
                pe.wait_ge(s_z, t + 1)
                for k in range(KC):
                    last = pe.transpose(bank[:, k // 2, (k % 2) * T + t * P:(k % 2) * T + (t + 1) * P],
                                        work[:, t, k * P:(k + 1) * P], ident[:, :])
            last.then_inc(s_xT, 4)

            nunit = [0]

            def start_unit():
                i = nunit[0]
                if i >= 2:
                    pe.wait_ge(s_uout[UNITS[i - 2]], 1)
                nunit[0] += 1
                return bank[:, 2 + i % 2, :].rearrange("p (c t) -> p c t", c=2)

            def by_channel(w, c0, width):
                o = start_unit()
                m = min(P, width)
                for c in range((width + P - 1) // P):
                    for k in range(KC):
                        last = pe.matmul(o[0:m, c, :], w[:, k, c0 + c * P:c0 + c * P + m], hT[:, k, :],
                                         start=(k == 0), stop=(k == KC - 1))
                last.then_inc(s_unit, 1)

            def by_token(w, c0, width):
                o = start_unit()
                for t in range(TB):
                    for k in range(KC):
                        last = pe.matmul(o[:, t, 0:width], hT[:, k, t * P:(t + 1) * P],
                                         w[:, k, c0:c0 + width], start=(k == 0), stop=(k == KC - 1))
                last.then_inc(s_unit, 1)

            def scores(qT, kT, shared, b, done):
                n = (b + 1) * P
                o = pair_bank(4)
                for j in range(2):
                    for par in range(2):
                        r = slice(DH * par, DH * par + DH)
                        k = kT[r, 0:n] if shared else kT[r, j, 0:n]
                        last = pe.matmul(o[:, 2 * par + j, 0:n], qT[r, j, b * P:(b + 1) * P], k,
                                         start=True, stop=True)
                last.then_inc(done, 1)

            pe.wait_ge(s_hTa, 4)
            pe.wait_ge(s_hTd, 4)
            loaded(pe, "s_idx")
            w = slot("s_idx", IDXC)
            by_channel(w, 0, BW)
            by_channel(w, BW, DH)
            pe.wait_ge(s_slot[1], 48)
            w = slot("s_dsa", DSAC)
            by_token(w, BW + DH, DH + 2 * NH)
            pe.wait_ge(s_uout["iq"], 1)
            pe.wait_ge(s_uout["ik"], 1)
            scores(iqT, ikT, True, 0, s_idx)
            by_channel(w, 0, BW)
            pe.wait_ge(s_rel, 1)
            scores(iqT, ikT, True, 1, s_idx)
            by_channel(w, BW, DH)
            loaded(pe, "s_fox")
            w = slot("s_fox")
            by_channel(w, 0, BW)
            by_channel(w, BW, BW)
            pe.wait_ge(s_lsb, 2)
            pe.wait_ge(s_const, 1)
            o = pair_bank(0)
            for hh in range(NH):
                h = 2 * (hh % 2) + hh // 2
                pe.matmul(o[:, hh, :], lsb[:, 0, h, :], tri[:, P:P + T], start=True, stop=False)
                pe.matmul(o[:, hh, :], lsb[:, 1, h, :], tri[:, 0:T], start=False, stop=True)
            pe.matmul(bank[:, 6, 0:NH], tri[:, P:2 * P], fs[:, 5, 0, :], start=True, stop=True)
            pe.matmul(bank[:, 6, NH:2 * NH], tri[:, 2 * P:3 * P], fs[:, 5, 0, :], start=True, stop=False)
            pe.matmul(bank[:, 6, NH:2 * NH], tri[:, P:2 * P], fs[:, 5, 1, :], start=False, stop=True)\
                .then_inc(s_cum, 1)
            loaded_val = 32
            pe.wait_ge(s_slot[3], loaded_val)
            w = slot("s_val")
            by_token(w, BW, BW)
            pe.wait_ge(s_uout["fq"], 1)
            pe.wait_ge(s_uout["fk"], 1)
            pe.wait_ge(s_rel, 2)
            scores(fqT, fkT, False, 0, s_s)
            by_channel(w, 0, BW)
            pe.wait_ge(s_lg, 1)
            scores(fqT, fkT, False, 1, s_s)
            loaded(pe, "s_conv")
            w = slot("s_conv")
            by_channel(w, BW, BW)
            by_channel(w, 0, BW)

            def gate(t):
                loaded_gate(t)
                w = slot(f"g{t}")
                for b in range(TB):
                    if t:
                        pe.wait_ge(s_gout, 2 * (t - 1) + b + 1)
                    elif b == 0:
                        pe.wait_ge(s_cumo, 1)
                    for k in range(KC):
                        last = pe.matmul(bank[:, b, :], hT[:, k, b * P:(b + 1) * P], w[:, k, :],
                                         start=(k == 0), stop=(k == KC - 1))
                    last.then_inc(s_gate, 1)

            def loaded_gate(t):
                n = f"g{t}"
                extra = {1: 32, 3: 16}.get(SLOT[n], 0)
                pe.wait_ge(s_slot[SLOT[n]], 16 * LOAD[n] + extra)

            nturn = [0]

            def turn(i, kc):
                if nturn[0] == 0:
                    pe.wait_ge(s_cumo, 1)
                else:
                    pe.wait_ge(s_pTo, nturn[0])
                nturn[0] += 1
                pe.wait_ge(s_prob, i + 1)
                b = i % TB
                for hh in range(NH):
                    last = pe.transpose(bank[:, 6, hh * P:(hh + 1) * P],
                                        logit[b][:, hh, kc * P:(kc + 1) * P], ident[:, :])
                last.then_inc(s_pT, 1)

            def weigh(i, value):
                b = i % TB
                pe.wait_ge(s_pTo, nturn[0])
                if i == TB:
                    pe.wait_ge(s_att, 1)
                for hh in range(NH):
                    par, j = hh // 2, hh % 2
                    for kc in range(b + 1):
                        last = pe.matmul(bank[DH * par:DH * par + DH, 7, j * T + b * P:j * T + (b + 1) * P],
                                         value(kc, 2 * j + par), probT[:, kc, hh * P:(hh + 1) * P],
                                         start=(kc == 0), stop=(kc == b))
                last.then_inc(s_pv, 1)

            def fox_v(kc, h):
                return fv[:, kc, h * DH:(h + 1) * DH]

            def dsa_v(kc, h):
                return misc[:, kc, 0:DH]

            gate(0)
            turn(0, 0)
            weigh(0, fox_v)
            gate(1)
            turn(1, 0)
            turn(1, 1)
            weigh(1, fox_v)
            gate(2)
            pe.wait_ge(s_lg, 2)
            scores(dqT, dkT, True, 0, s_s)
            gate(3)
            turn(2, 0)
            weigh(2, dsa_v)
            pe.wait_ge(s_lg, 3)
            scores(dqT, dkT, True, 1, s_s)
            gate(4)
            turn(3, 0)
            turn(3, 1)
            weigh(3, dsa_v)
            gate(5)
            pe.wait_ge(s_poolin, 1)
            pe.wait_ge(s_small, 16 * 9)
            pe.wait_ge(s_uout["conva"], 1)
            for g in range(4):
                r = slice(DH * (g % 2), DH * (g % 2) + DH)
                last = pe.matmul(bank[r, 2 + g % 2, (g // 2) * T:(g // 2 + 1) * T], poolw[r, g // 2, :],
                                 pooled[0][r, g // 2, PADP:PADP + T], start=True, stop=True)
            last.then_inc(s_poolmm, 1)
            gate(6)
            pe.wait_ge(s_conv, 1)
            pe.wait_ge(s_pTo, 6)
            for t in range(TB):
                for c in range(2):
                    last = pe.transpose(bank[:, 6, t * T + c * P:t * T + (c + 1) * P],
                                        convy[:, c, t * P:(t + 1) * P], ident[:, :])
            last.then_inc(s_cT, 1)
            gate(7)
            pe.wait_ge(s_cz, 1)
            pe.wait_ge(s_att, 2)
            for c in range(2):
                for t in range(TB):
                    last = pe.transpose(bank[:, 7, c * T + t * P:c * T + (t + 1) * P],
                                        glu[:, t, c * P:(c + 1) * P], ident[:, :])
            last.then_inc(s_czT, 1)

            pe.wait_ge(s_att, 2)
            pe.wait_ge(s_poolo, 1)
            i = 0
            for dq in range(2):
                pe.wait_ge(s_slot[SLOT[f"wb{dq}"]],
                           16 * LOAD[f"wb{dq}"] + {1: 32, 3: 16}.get(SLOT[f"wb{dq}"], 0))
                w = slot(f"wb{dq}")
                for t in range(TB):
                    for n in range(NB):
                        if i < 2:
                            pe.wait_ge(s_gout, 16)
                        if n == 3:
                            pe.wait_ge(s_cbr, 1)
                        if i >= 4:
                            pe.wait_ge(s_mix, i - 3)
                        for kc in range(2):
                            last = pe.matmul(bank[:, i % 4, :], brT[:, n, kc, t * P:(t + 1) * P],
                                             w[:, 2 * n + kc, :], start=(kc == 0), stop=(kc == 1))
                        last.then_inc(s_up, 1)
                        i += 1
            for i in range(4):
                pe.wait_ge(s_mix, 8 * (i // 2 + 1))
                if i < 2:
                    pe.wait_ge(s_lg, 4)
                else:
                    pe.wait_ge(s_mTo, i - 1)
                for kk in range(2):
                    for t in range(TB):
                        k = 2 * i + kk
                        last = pe.transpose(bank[:, 4 + i % 2, kk * T + t * P:kk * T + (t + 1) * P],
                                            work[:, t, k * P:(k + 1) * P], ident[:, :])
                last.then_inc(s_mT, 1)
            pe.wait_ge(s_mTo, 4)
            for j in range(2):
                pe.wait_ge(s_wout[j], 16)
                w = gates[:, j, :].rearrange("p (k n) -> p k n", n=HALF)
                for t in range(TB):
                    for k in range(KC):
                        last = pe.matmul(bank[:, 2 * t + j, :], hT[:, k, t * P:(t + 1) * P], w[:, k, :],
                                         start=(k == 0), stop=(k == KC - 1))
                    last.then_inc(s_o, 1)
            for t in range(TB):
                pe.wait_ge(s_z1, t + 1)
                for k in range(KC):
                    last = pe.transpose(bank[:, 4 + k // 2, (k % 2) * T + t * P:(k % 2) * T + (t + 1) * P],
                                        work[:, t, k * P:(k + 1) * P], ident[:, :])
            last.then_inc(s_zT, 4)
            pe.wait_ge(s_h1Ta, 4)
            pe.wait_ge(s_h1Td, 4)
            for t in range(TB):
                for k in range(KC):
                    last = pe.matmul(bank[:, 0, t * 32:t * 32 + NG + NE], hT[:, k, t * P:(t + 1) * P],
                                     rw[:, k, :], start=(k == 0), stop=(k == KC - 1))
            last.then_inc(s_rt, 1)
            pe.wait_ge(s_mask, 1)
            mask = [rt[:, 12, t, :] for t in range(TB)]
            o = bank[:, 1, 0:3 * NE]
            pe.matmul(o[:, 0:NE], tri[:, P:2 * P], mask[0], start=True, stop=True)
            pe.matmul(o[:, NE:2 * NE], tri[:, 2 * P:3 * P], mask[0], start=True, stop=False)
            pe.matmul(o[:, NE:2 * NE], tri[:, P:2 * P], mask[1], start=False, stop=True)
            pe.matmul(o[:, 2 * NE:3 * NE], tri[:, 2 * P:3 * P], mask[0], start=True, stop=False)
            pe.matmul(o[:, 2 * NE:3 * NE], tri[:, 2 * P:3 * P], mask[1], start=False, stop=True)\
                .then_inc(s_rank, 1)

            def gather():
                for k in range(KC):
                    for t in range(TB):
                        last = pe.matmul(bank[:, 2 + k // 4, (k % 4) * P:(k % 4 + 1) * P],
                                         work[:, t, k * P:(k + 1) * P],
                                         disp[:, t].rearrange("p e s -> p (e s)"),
                                         start=(t == 0), stop=(t == TB - 1))
                last.then_inc(m_xg, 1)

            pe.wait_ge(m_disp, 1)
            pe.wait_ge(s_h1, TB)
            gather()
            pe.wait_ge(s_np, 1)
            npass = pe.value_load(npass_i[0:1, 0:1], min_val=1, max_val=PASSES)
            base = [16 * FIRST[s] + {1: 32, 3: 16}.get(s, 0) for s in range(SLOTS)]
            with pe.Fori(0, pe.snap(npass * PAIRS)) as it:
                pe.wait_ge(m_xgo, it + 1)
                for first, bk, done in ((0, 0, m_g), (2, 1, m_u)):
                    for e in range(2):
                        pe.wait_ge(s_slot[first + e], it * 16 + base[first + e] + 16)
                    for k in range(KC):
                        for e in range(2):
                            last = pe.matmul(bank[CAP * e:CAP * e + CAP, bk, :],
                                             xg[:, k, CAP * e:CAP * e + CAP],
                                             expert_slot(first + e, DFF)[:, k, :],
                                             start=(k == 0), stop=(k == KC - 1))
                    last.then_inc(done, 1)
                pe.wait_ge(m_disp, it + 2)
                gather()
                pe.wait_ge(m_dispw, it + 1)
                for t in range(TB):
                    last = pe.transpose(bank[:, 7, t * P:(t + 1) * P],
                                        dispw[:, t].rearrange("p e s -> p (e s)"), ident[:, :])
                last.then_inc(m_cT, 1)
                pe.wait_ge(m_h, it + 1)
                for f in range(FC):
                    last = pe.transpose(bank[:, 4, f * P:(f + 1) * P], hexp[:, f * P:(f + 1) * P], ident[:, :])
                last.then_inc(m_hT, 1)
                pe.wait_ge(m_hTo, it + 1)
                for e in range(2):
                    pe.wait_ge(s_slot[4 + e], it * 16 + base[4 + e] + 16)
                for half in range(2):
                    for f in range(FC):
                        for e in range(2):
                            last = pe.matmul(bank[CAP * e:CAP * e + CAP, 5 + half, :],
                                             hexT[:, f * P + CAP * e:f * P + CAP * e + CAP],
                                             expert_slot(4 + e, D)[:, f, half * HALF:(half + 1) * HALF],
                                             start=(f == 0), stop=(f == FC - 1))
                last.then_inc(m_y, 1)
                pe.wait_ge(m_cTo, it + 1)
                pe.wait_ge(m_yd, it + 1)
                pe.wait_ge(m_ya, it + 1)
                for i in range(4):
                    t, half = divmod(i, 2)
                    if i >= 2:
                        pe.wait_ge(m_acc, it * 4 + i - 1)
                    pe.matmul(bank[:, 7 if i % 2 == 0 else 4, :], comb[:, t * P:(t + 1) * P],
                              yexp[:, half * HALF:(half + 1) * HALF], start=True, stop=True).then_inc(m_c, 1)
                pe.wait_ge(m_acc, it * 4 + 4)

        @block.vector
        def _(dve):
            n = [0]

            def chain(ins):
                n[0] += 1
                ins.then_inc(s_dch, 1)
                return n[0]

            def link(ins):
                dve.wait_ge(s_dch, chain(ins))

            nln = [0]

            def row_stats(t, src, width):
                parts = (width + HALF - 1) // HALF
                for i in range(parts):
                    w = width // parts
                    last = dve.bn_stats(stats[:, t, i, :], src[:, i * w:(i + 1) * w])
                link(last)
                link(dve.bn_aggr(mv[:, t, 0:2], stats[:, t, 0:parts, :]))
                dve.tensor_scalar(mv[:, t, 2:3], mv[:, t, 1:2], EPS, None, ALU.add).then_inc(s_var, 1)

            def inverse_std():
                nln[0] += 1
                dve.wait_ge(s_std, nln[0])
                link(dve.reciprocal(mv[:, :, 4:5], mv[:, :, 3:4]))

            def normalise(t, src, dst):
                return dve.tensor_scalar(dst, src, mv[:, t, 0:1], mv[:, t, 4:5], ALU.subtract, ALU.mult)

            for t in range(TB):
                dve.wait_ge(s_x[t], 16)
                row_stats(t, work[:, t, :], D)
            inverse_std()
            for t in range(TB):
                normalise(t, work[:, t, :], work[:, t, :]).then_inc(s_z, 1)
            dve.wait_ge(s_vT, 1)
            dve.tensor_copy(vcol[:, :], bank[:, 4, 0:NROW]).then_inc(s_vcol, 1)
            dve.wait_ge(s_vcol, 1)
            dve.wait_ge(s_xT, 4)
            for k in range(4, KC):
                dve.tensor_scalar(hT[:, k, :], bank[:, k // 2, (k % 2) * T:(k % 2 + 1) * T],
                                  vcol[:, ROW["ln_in_g"] + k:ROW["ln_in_g"] + k + 1],
                                  vcol[:, ROW["ln_in_b"] + k:ROW["ln_in_b"] + k + 1],
                                  ALU.mult, ALU.add).then_inc(s_hTd, 1)
            dve.wait_ge(s_const, 1)
            link(dve.reciprocal(rcnt[:, :, :], rcnt[:, :, :]))
            dve.wait_ge(s_uout["misc"], 1)
            dve.wait_ge(s_small, 16 * 9)
            link(dve.tensor_tensor(fs[:, 0], misc[:, :, DH + NH:DH + 2 * NH],
                                   bforget[:, :].unsqueeze(1).broadcast_to([P, TB, NH]), ALU.add))
            link(dve.tensor_scalar(fs[:, 1], fs[:, 0], -1.0, None, ALU.mult))
            dve.tensor_tensor(fs[:, 1], fs[:, 0], fs[:, 1], ALU.max).then_inc(s_ls, 1)
            dve.wait_ge(s_lsa, 1)
            dve.tensor_scalar(fs[:, 3], fs[:, 2], 1.0, None, ALU.add).then_inc(s_ls, 1)

            def index_score(b):
                m = (b + 1) * P
                dve.wait_ge(s_rel, b + 1)
                for h in range(NH):
                    hh = 2 * (h % 2) + h // 2
                    w = misc[:, b, DH + h:DH + h + 1]
                    if h == 0:
                        ins = dve.tensor_scalar(score[b][:, :], rel[:, hh, 0:m], w, None, ALU.mult)
                    else:
                        ins = dve.scalar_tensor_tensor(out=score[b][:, :], in0=rel[:, hh, 0:m], scalar=w,
                                                       in1=score[b][:, :], op0=ALU.mult, op1=ALU.add)
                    link(ins)
                dve.tensor_tensor(score[b][:, :], score[b][:, :], causal[:, T - m:T], ALU.add)\
                    .then_inc(s_relu_used, 1)
                dve.wait_ge(s_relu_used, b + 1)

            index_score(0)
            dve.wait_ge(s_lsa, 2)
            dve.scalar_tensor_tensor(out=fs[:, 5], in0=fs[:, 0], scalar=0.0, in1=fs[:, 4],
                                     op0=ALU.min, op1=ALU.subtract).then_inc(s_lsb, 1)
            dve.wait_ge(s_lsb, 1)
            dve.tensor_copy(lsb[:, :, :, :], fs[:, 5].unsqueeze(3).broadcast_to([P, TB, NH, P]))\
                .then_inc(s_lsb, 1)
            index_score(1)
            dve.wait_ge(s_cum, 1)
            dve.tensor_copy(cq[:, :, :], bank[:, 6, 0:TB * NH].rearrange("p (t h) -> p t h", t=TB))
            dve.scalar_tensor_tensor(out=fbias0[:, :, :], in0=pair_bank(0)[:, :, 0:P], scalar=-1.0,
                                     in1=causal[:, P:T].unsqueeze(1).broadcast_to([P, NH, P]),
                                     op0=ALU.mult, op1=ALU.add)
            dve.scalar_tensor_tensor(out=fbias1[:, :, :], in0=pair_bank(0), scalar=-1.0,
                                     in1=causal[:, :].unsqueeze(1).broadcast_to([P, NH, T]),
                                     op0=ALU.mult, op1=ALU.add).then_inc(s_cumo, 1)
            dve.wait_ge(s_cumo, 1)

            def negmax(i):
                b = i % TB
                dve.tensor_reduce(smx[:, i // TB, b, 0, :], logit[b][:, :, :], AX.X, ALU.max,
                                  negate=True).then_inc(s_lg, 1)

            def probs(i):
                b = i % TB
                s = smx[:, i // TB, b]
                dve.wait_ge(s_exp, i + 1)
                link(dve.reciprocal(s[:, 2, :], s[:, 1, :]))
                for hh in range(NH):
                    last = dve.tensor_scalar(logit[b][:, hh, :], logit[b][:, hh, :], s[:, 2, hh:hh + 1],
                                             None, ALU.mult)
                last.then_inc(s_prob, 1)

            def fox(b):
                fb = fbias1 if b else fbias0
                m = (b + 1) * P
                dve.wait_ge(s_s, b + 1)
                for hh in range(NH):
                    h = 2 * (hh % 2) + hh // 2
                    last = dve.scalar_tensor_tensor(out=logit[b][:, hh, :], in0=pair_bank(4)[:, hh, 0:m],
                                                    scalar=cq[:, b, h:h + 1], in1=fb[:, hh, :],
                                                    op0=ALU.add, op1=ALU.add)
                link(last)
                negmax(b)

            def select(b):
                s = score[b][:, :]
                for r in range(ROUNDS):
                    link(dve.max(top8[:, :], s))
                    link(dve.match_replace(s, top8[:, :], s, TAKEN))
                link(dve.tensor_scalar(s, s, TAKEN / 2, NEG, ALU.is_gt, ALU.mult))
                link(dve.tensor_tensor(s, s, causal[:, T - (b + 1) * P:T], ALU.add))

            def dsa(b):
                m = (b + 1) * P
                for hh in range(NH):
                    h = 2 * (hh % 2) + hh // 2
                    last = dve.scalar_tensor_tensor(out=alibi[:, hh, 0:m], in0=dist[:, T - m:T],
                                                    scalar=-SLOPES[h], in1=score[b][:, :],
                                                    op0=ALU.mult, op1=ALU.add)
                link(last)
                dve.wait_ge(s_s, TB + b + 1)
                dve.wait_ge(s_pT, 1 if b == 0 else 3)
                link(dve.tensor_tensor(logit[b][:, :, :], pair_bank(4)[:, :, 0:m], alibi[:, :, 0:m], ALU.add))
                negmax(TB + b)

            fox(0)
            probs(0)
            fox(1)
            probs(1)
            dve.wait_ge(s_unit, len(UNITS))
            dve.wait_ge(s_uout["convb"], 1)
            dve.tensor_tensor(hpad[:, :, PADC:PADC + T], bank[:, 2, :].rearrange("p (c t) -> p c t", c=2),
                              glu[:, :, :], ALU.mult).then_inc(s_uout["conva"], 1)
            select(0)
            select(1)
            dsa(0)
            probs(2)
            dsa(1)
            dve.wait_ge(s_uout["pool"], 1)
            src = poolv
            for g, w in enumerate(WINDOWS):
                dst = pooled[g % 2]
                j0 = g // 2
                link(dve.tensor_tensor(dst[:, j0:2, PADP:], src[:, j0:2, PADP:],
                                       src[:, j0:2, PADP - w // 2:PADP + T - w // 2], ALU.add))
                r = slice(DH * (g % 2), DH * (g % 2) + DH)
                link(dve.tensor_tensor(convy[r, g // 2, :], dst[r, g // 2, PADP:], rcnt[r, g // 2, :], ALU.mult))
                src = dst
            dve.tensor_tensor(pooled[0][:, :, PADP:], convy[:, :, :], poolv[:, :, PADP:], ALU.subtract)\
                .then_inc(s_poolin, 1)
            probs(3)
            dve.wait_ge(s_poolin, 1)
            dve.wait_ge(s_uout["conva"], 1)
            done = [0, 0]
            for j in range(CONV_W):
                for c in range(2):
                    w = vcol[:, ROW["conv_dw"] + 2 * j + c:ROW["conv_dw"] + 2 * j + c + 1]
                    src = hpad[:, c, j:j + T]
                    if j == 0:
                        b = ROW["conv_b"] + c
                        ins = dve.tensor_scalar(convy[:, c, :], src, w, vcol[:, b:b + 1], ALU.mult, ALU.add)
                    else:
                        dve.wait_ge(s_dch, done[c])
                        ins = dve.scalar_tensor_tensor(out=convy[:, c, :], in0=src, scalar=w,
                                                       in1=convy[:, c, :], op0=ALU.mult, op1=ALU.add)
                    if j == CONV_W - 1 and c == 1:
                        ins.then_inc(s_conv, 1)
                    else:
                        done[c] = chain(ins)
            dve.wait_ge(s_cT, 1)
            for t in range(TB):
                row_stats(t, bank[:, 6, t * T:(t + 1) * T], BW)
            inverse_std()
            for t in range(TB):
                last = normalise(t, bank[:, 6, t * T:(t + 1) * T], glu[:, t, :])
            last.then_inc(s_cz, 1)

            i = 0
            for dq in range(2):
                g = gates[:, dq, :].rearrange("p (t n c) -> p t n c", t=TB, n=NB)
                for t in range(TB):
                    o = work[:, t, dq * HALF:(dq + 1) * HALF]
                    if i == 0:
                        dve.wait_ge(s_hn, TB)
                    for nb in range(NB):
                        dve.wait_ge(s_up, i + 1)
                        dve.wait_ge(s_gsig, 4 * dq + nb + 1)
                        dst = o if nb == 0 else tmp[:, nb % 2, :]
                        ins = dve.tensor_tensor(dst, bank[:, i % 4, :], g[:, t, nb, :], ALU.mult)
                        if nb:
                            link(ins)
                            dve.tensor_tensor(o, o, tmp[:, nb % 2, :], ALU.add).then_inc(s_mix, 1)
                        else:
                            ins.then_inc(s_mix, 1)
                        i += 1
                        dve.wait_ge(s_mix, i)
            dve.wait_ge(s_mT, 4)
            for t in range(TB):
                for j in range(2):
                    dve.wait_ge(s_o, 2 * j + t + 1)
                    c = slice(j * HALF, (j + 1) * HALF)
                    link(dve.scalar_tensor_tensor(out=work[:, t, c], in0=hn[:, t, c], scalar=ALPHA,
                                                  in1=bank[:, 2 * t + j, :], op0=ALU.mult, op1=ALU.add))
                row_stats(t, work[:, t, :], D)
            inverse_std()
            for t in range(TB):
                normalise(t, work[:, t, :], work[:, t, :]).then_inc(s_z1, 1)
            dve.wait_ge(s_zT, 4)
            for k in range(4, KC):
                dve.tensor_scalar(hT[:, k, :], bank[:, 4 + k // 2, (k % 2) * T:(k % 2 + 1) * T],
                                  vcol[:, ROW["ln1_g"] + k:ROW["ln1_g"] + k + 1],
                                  vcol[:, ROW["ln1_b"] + k:ROW["ln1_b"] + k + 1],
                                  ALU.mult, ALU.add).then_inc(s_h1Td, 1)
            dve.wait_ge(s_lnp, 64)
            for t in range(TB):
                link(dve.tensor_tensor(work[:, t, :], work[:, t, :], lnp[:, 0, :], ALU.mult))
                dve.tensor_tensor(work[:, t, :], work[:, t, :], lnp[:, 1, :], ALU.add).then_inc(s_h1, 1)
            dve.wait_ge(s_rt, 1)
            R = [rt[:, i] for i in range(16)]
            link(dve.tensor_tensor(lg, bank[:, 0, 0:TB * 32].rearrange("p (t n) -> p t n", t=TB)[:, :, 0:NG + NE],
                                   rbias[:, :].unsqueeze(1).broadcast_to([P, TB, NG + NE]), ALU.add))
            order = desc4[:, :].unsqueeze(1).broadcast_to([P, TB, NG])

            def first_max(v, val, hot, s):
                link(dve.tensor_reduce(val, v, AX.X, ALU.max))
                link(dve.tensor_tensor(s, v, val.unsqueeze(2).broadcast_to([P, TB, NG]), ALU.is_equal))
                link(dve.tensor_tensor(s, s, order, ALU.mult))
                link(dve.tensor_reduce(R[15][:, :, 0], s, AX.X, ALU.max))
                link(dve.tensor_tensor(hot, s, R[15][:, :, 0:1].broadcast_to([P, TB, NG]), ALU.is_equal))

            gmax, hotg, le = R[0][:, :, 0], R[1][:, :, 0:NG], R[3][:, :, 0:EPG]
            first_max(lg[:, :, 0:NG], gmax, hotg, R[2][:, :, 0:NG])
            link(dve.tensor_tensor(R[7][:, :, 0:NG], lg[:, :, 0:NG],
                                   R[0][:, :, 0:1].broadcast_to([P, TB, NG]), ALU.subtract))
            hotg4 = hotg.unsqueeze(3).broadcast_to([P, TB, NG, EPG])
            prod = R[2].rearrange("p t (g j) -> p t g j", g=NG)
            link(dve.tensor_tensor(prod, lg[:, :, NG:].rearrange("p t (g j) -> p t g j", g=NG), hotg4, ALU.mult))
            link(dve.tensor_reduce(le, R[2].rearrange("p t (g j) -> p t j g", g=NG), AX.X, ALU.add))
            hot1, hot2 = R[4][:, :, 0:EPG], R[5][:, :, 0:EPG]
            first_max(le, R[0][:, :, 1], hot1, R[6][:, :, 0:EPG])
            link(dve.scalar_tensor_tensor(out=R[6][:, :, 4:8], in0=hot1, scalar=TAKEN, in1=le,
                                          op0=ALU.mult, op1=ALU.add))
            first_max(R[6][:, :, 4:8], R[0][:, :, 2], hot2, R[6][:, :, 0:EPG])
            dve.tensor_tensor(R[7][:, :, NG:NG + 1], R[0][:, :, 2:3], R[0][:, :, 1:2], ALU.subtract)\
                .then_inc(s_re, 1)
            link(dve.tensor_tensor(R[9][:, :, 0:EPG], hot1, hot2, ALU.add))
            dve.tensor_tensor(R[12].rearrange("p t (g j) -> p t g j", g=NG), hotg4,
                              R[9][:, :, 0:EPG].unsqueeze(2).broadcast_to([P, TB, NG, EPG]), ALU.mult)\
                .then_inc(s_mask, 1)
            dve.wait_ge(s_rex, 1)
            link(dve.tensor_reduce(R[10][:, :, 0], R[8][:, :, 0:NG], AX.X, ALU.add))
            link(dve.tensor_scalar(R[10][:, :, 1], R[8][:, :, NG], 1.0, None, ALU.add))
            link(dve.reciprocal(R[10][:, :, 2:4], R[10][:, :, 0:2]))
            link(dve.tensor_tensor(R[10][:, :, 4], R[10][:, :, 2], R[10][:, :, 3], ALU.mult))
            link(dve.tensor_tensor(R[10][:, :, 5], R[10][:, :, 4], R[8][:, :, NG], ALU.mult))
            link(dve.tensor_tensor(R[11][:, :, 0:EPG], hot1, R[10][:, :, 4:5].broadcast_to([P, TB, EPG]), ALU.mult))
            link(dve.tensor_tensor(R[11][:, :, 4:8], hot2, R[10][:, :, 5:6].broadcast_to([P, TB, EPG]), ALU.mult))
            link(dve.tensor_tensor(R[11][:, :, 0:EPG], R[11][:, :, 0:EPG], R[11][:, :, 4:8], ALU.add))
            link(dve.tensor_tensor(R[13].rearrange("p t (g j) -> p t g j", g=NG), hotg4,
                                   R[11][:, :, 0:EPG].unsqueeze(2).broadcast_to([P, TB, NG, EPG]), ALU.mult))
            dve.wait_ge(s_rank, 1)
            ranks = bank[:, 1, 0:2 * NE].rearrange("p (t e) -> p t e", t=TB)
            link(dve.tensor_tensor(R[14], ranks, R[12], ALU.mult))
            dve.memset(rankp[:, PASSES * PAIRS], -1.0)
            for q in range(PASSES):
                for t in range(TB):
                    dve.tensor_scalar(rankp[:, q * PAIRS:(q + 1) * PAIRS, t, :],
                                      R[14][:, t].rearrange("p (i e) -> p i e", e=2),
                                      -1.0 - CAP * q, None, ALU.add)
                    last = dve.tensor_copy(wpair[:, q * PAIRS:(q + 1) * PAIRS, t, :],
                                           R[13][:, t].rearrange("p (i e) -> p i e", e=2))
            link(last)
            dve.memset(npass_f[:, 0:1], 1.0)
            link(dve.tensor_reduce(npass_f[:, 6:7], bank[:, 1, 2 * NE:3 * NE], AX.X, ALU.max))
            for q in range(1, PASSES):
                last = dve.tensor_scalar(npass_f[:, q:q + 1], npass_f[:, 6:7], CAP * q + 0.5, None, ALU.is_gt)
            link(last)
            link(dve.tensor_reduce(npass_f[:, PASSES:PASSES + 1], npass_f[:, 0:PASSES], AX.X, ALU.add))
            dve.tensor_copy(npass_i[:, :], npass_f[:, PASSES:PASSES + 1]).then_inc(s_np, 1)

            slots = slot_no[:, :].unsqueeze(1).broadcast_to([P, 2, CAP])

            def dispatch(it):
                for t in range(TB):
                    r = rankp[:, bass.ds(it, 1), t, :].rearrange("p o e -> p (o e)")
                    last = dve.tensor_tensor(disp[:, t], slots, r.unsqueeze(2).broadcast_to([P, 2, CAP]),
                                             ALU.is_equal)
                last.then_inc(m_disp, 1)

            dispatch(0)
            for t in range(TB):
                last = dve.tensor_scalar(acc[:, t, :], work[:, t, :], ALPHA, None, ALU.mult)
            last.then_inc(s_acc0, 1)

            def gathered():
                dve.tensor_copy(xg[:, :, :].rearrange("p (b k) s -> p b (k s)", b=2), bank[:, 2:4, :])\
                    .then_inc(m_xgo, 1)

            dve.wait_ge(m_xg, 1)
            gathered()
            dve.wait_ge(s_acc0, 1)
            dve.wait_ge(s_np, 1)
            npass = dve.value_load(npass_i[0:1, 0:1], min_val=1, max_val=PASSES)
            with dve.Fori(0, dve.snap(npass * PAIRS)) as it:
                dve.wait_ge(m_disp, it + 1)
                for t in range(TB):
                    w = wpair[:, bass.ds(it, 1), t, :].rearrange("p o e -> p (o e)")
                    last = dve.tensor_tensor(dispw[:, t], disp[:, t],
                                             w.unsqueeze(2).broadcast_to([P, 2, CAP]), ALU.mult)
                last.then_inc(m_dispw, 1)
                dve.wait_ge(m_dispw, it + 1)
                dve.wait_ge(m_xg, it + 1)
                dispatch(it + 1)
                dve.wait_ge(m_u, it + 1)
                dve.wait_ge(m_silu, it + 1)
                dve.tensor_tensor(hexp[:, :], silu_g[:, :], bank[:, 1, :], ALU.mult).then_inc(m_h, 1)
                dve.wait_ge(m_xg, it + 2)
                gathered()
                dve.wait_ge(m_cT, it + 1)
                dve.tensor_copy(comb[:, :], bank[:, 7, 0:TB * P]).then_inc(m_cTo, 1)
                dve.wait_ge(m_hT, it + 1)
                dve.tensor_copy(hexT[:, :], bank[:, 4, :]).then_inc(m_hTo, 1)
                dve.wait_ge(m_y, it + 1)
                dve.tensor_copy(yexp[:, 0:HALF], bank[:, 5, :]).then_inc(m_yd, 1)
                for i in range(4):
                    t, half = divmod(i, 2)
                    dve.wait_ge(m_c, it * 4 + i + 1)
                    o = acc[:, t, half * HALF:(half + 1) * HALF]
                    dve.tensor_tensor(o, o, bank[:, 7 if i % 2 == 0 else 4, :], ALU.add).then_inc(m_acc, 1)
                dve.wait_ge(m_acc, it * 4 + 4)
            dve.wait_ge(s_lnp, 96)
            for t in range(TB):
                row_stats(t, acc[:, t, :], D)
            inverse_std()
            for t in range(TB):
                link(normalise(t, acc[:, t, :], work[:, t, :]))
                link(dve.tensor_tensor(work[:, t, :], work[:, t, :], lnp[:, 0, :], ALU.mult))
                dve.tensor_tensor(work[:, t, :], work[:, t, :], lnp[:, 1, :], ALU.add).then_inc(s_fin, 1)


_INS = ["x", "ln_in_g", "ln_in_b", "w_in", "b_forget", "b_gate", "pool_w", "pool_scale", "conv_dw", "conv_b",
        "conv_ln_g", "conv_ln_b", "w_branch", "w_out", "ln1_g", "ln1_b", "router_g", "router_g_b",
        "router_e", "router_e_b", "expert_w_gate", "expert_w_up", "expert_w_down", "ln2_g", "ln2_b"]


def kernel(**inputs):
    import numpy as _np
    import concourse.bacc as _bacc
    from concourse import mybir as _mybir
    from concourse.bass_utils import run_bass_kernel_spmd as _run

    nc = _bacc.Bacc("TRN2", target_bir_lowering=False, num_devices=1)
    arrays, aps = {}, {}
    for name in _INS:
        v = _np.ascontiguousarray(inputs[name])
        arrays[f"in_{name}_dram"] = v
        aps[name] = nc.dram_tensor(f"in_{name}_dram", v.shape, _mybir.dt.from_np(v.dtype),
                                   kind="ExternalInput").ap()
    shape = arrays["in_x_dram"].shape
    out = nc.dram_tensor("out_0_dram", shape, _mybir.dt.float32, kind="ExternalOutput").ap()
    hybrid_trunk_kernel(nc, aps, out)
    r = _run(nc, [arrays], core_ids=[0])
    return r.results[0]["out_0_dram"]
```

```python
import concourse.bass as bass
from concourse import mybir
from contextlib import ExitStack


def hybrid_trunk_kernel(nc: bass.Bass, a: dict, out: bass.AP):
    F32 = mybir.dt.float32
    I32 = mybir.dt.int32
    ALU = mybir.AluOpType
    ACT = mybir.ActivationFunctionType
    AX = mybir.AxisListType

    P = 128
    T, D = a["x"].shape[1], a["x"].shape[2]
    TB = T // P
    KC = D // P
    HALF = 512
    BW = D // 4
    DH = 64
    NH = BW // DH
    CONV_W = a["conv_dw"].shape[1]
    PADC = CONV_W - 1
    PADP = 16
    NB = 4
    NG = a["router_g"].shape[2]
    NE = a["router_e"].shape[2]
    EPG = NE // NG
    DFF = a["expert_w_gate"].shape[3]
    FC = DFF // P
    PAIRS = NE // 2
    BODY = 4
    CAP = 64
    PASSES = T // CAP
    TOPK = min(256, T // 4)
    ROUNDS = TOPK // 8
    NEG = -1e30
    TAKEN = -3e38
    EPS = 1e-5
    ALPHA = 2.0 ** 0.25
    SCALE = float(DH) ** -0.5
    SLOPES = [2.0 ** (-8.0 * (h + 1) / NH) for h in range(NH)]
    WINDOWS = (2, 4, 8, 16)

    sizes = dict(pool=BW, fq=BW, fk=BW, fv=BW, ff=NH, dq=BW, dk=DH, dv=DH, iq=BW, ik=DH, iw=NH,
                 conv=2 * BW, gate=NB * D)
    col, at = {}, 0
    for name, n in sizes.items():
        col[name] = at
        at += n

    x_v = a["x"][0].rearrange("(t p) d -> p t d", p=P)
    w_in = a["w_in"][0].rearrange("(k p) n -> p k n", p=P)
    w_br = a["w_branch"][0].rearrange("n (k p) d -> p (n k) d", p=P)
    w_out = a["w_out"][0].rearrange("(k p) d -> p k d", p=P)
    e_gate = a["expert_w_gate"][0].rearrange("e (k p) f -> p e k f", p=P)
    e_up = a["expert_w_up"][0].rearrange("e (k p) f -> p e k f", p=P)
    e_down = a["expert_w_down"][0].rearrange("e (k p) d -> p e k d", p=P)
    out_v = out[0].rearrange("(t p) d -> p t d", p=P)

    vec_src, ROW, at = [], {}, 0
    for name, src in (("ln_in_g", a["ln_in_g"].rearrange("(c p) -> c p", p=P)),
                      ("ln_in_b", a["ln_in_b"].rearrange("(c p) -> c p", p=P)),
                      ("conv_dw", a["conv_dw"][0].rearrange("w (c p) -> (w c) p", p=P)),
                      ("pool_scale", a["pool_scale"][0].rearrange("(c p) -> c p", p=P)),
                      ("conv_b", a["conv_b"][0].rearrange("(c p) -> c p", p=P)),
                      ("conv_ln_g", a["conv_ln_g"][0].rearrange("(c p) -> c p", p=P)),
                      ("conv_ln_b", a["conv_ln_b"][0].rearrange("(c p) -> c p", p=P)),
                      ("ln1_g", a["ln1_g"][0].rearrange("(c p) -> c p", p=P)),
                      ("ln1_b", a["ln1_b"][0].rearrange("(c p) -> c p", p=P))):
        ROW[name] = at
        vec_src.append((at, src))
        at += src.shape[0]
    NROW = at
    NIN = 2 * KC

    ctx = ExitStack()
    with ctx:
        def sb(name, shape, dt=F32):
            return ctx.enter_context(nc.sbuf_tensor(name, shape, dt))

        def sem(name):
            return ctx.enter_context(nc.semaphore(name))

        SLOTS = 6
        RING = 8
        ring = sb("ring", [P, RING, KC * HALF])
        gates = sb("gates", [P, 2, KC * HALF])
        gflat = gates[:, :, :].rearrange("p a n -> p (a n)")
        xflat = ring[:, SLOTS:RING, :].rearrange("p a n -> p (a n)")
        place = {0: 0, 1: KC * HALF, 2: 0, 3: 0}

        def early(part, shape, rows=P):
            n = 1
            for d in shape:
                n *= d
            at = place[part]
            place[part] += n
            assert place[part] <= (1 if part == 0 else 2) * KC * HALF
            v = (xflat if part == 3 else gflat)[0:rows, at:at + n]
            if len(shape) == 2:
                v = v.rearrange("p (a b) -> p a b", b=shape[1])
            if len(shape) == 3:
                v = v.rearrange("p (a b c) -> p a b c", b=shape[1], c=shape[2])
            return v

        hT = sb("hT", [P, KC, T])
        hn = sb("hn", [P, TB, D])
        work = sb("work", [P, TB, D])
        lnp = sb("lnp", [P, 2, D])
        bgate = early(3, [2, HALF])
        vrows = early(0, [P], NROW)
        vcol = sb("vcol", [P, NROW])
        ident = sb("ident", [P, P])
        tri = sb("tri", [P, 3 * P])
        causal = sb("causal", [P, T])
        dist = sb("dist", [P, T])
        disti = early(0, [T]).bitcast(I32)
        rcnt = early(3, [2, T])
        slot_no = sb("slot_no", [P, CAP])
        desc4 = sb("desc4", [P, NG])
        bforget = sb("bforget", [P, NH])
        rbias = sb("rbias", [P, NG + NE])
        rw = sb("rw", [P, KC, NG + NE])
        poolw = sb("poolw", [P, 2, DH])
        iqT = early(0, [2, T])
        ikT = early(0, [T])
        dqT = early(3, [2, T])
        dkT = early(3, [T])
        fqT = early(0, [2, T])
        fkT = early(1, [2, T])
        fv = early(1, [TB, BW])
        misc = sb("misc", [P, TB, DH + 2 * NH])
        wflat = work[:, :, :].rearrange("p a n -> p (a n)")
        poolv, *pooled = [wflat[:, i * 2 * (PADP + T):(i + 1) * 2 * (PADP + T)]
                          .rearrange("p (c t) -> p c t", c=2) for i in range(3)]
        glu = early(3, [2, T])
        hpad = early(3, [2, PADC + T])
        convy = early(3, [2, T])
        brT = early(3, [NB, 2, T])
        fs = sb("fs", [P, 6, TB, NH])
        lsb = early(0, [TB, NH, P])
        cq = sb("cq", [P, TB, NH])
        fbias0 = early(1, [NH, P])
        fbias1 = early(1, [NH, T])
        rel = early(0, [NH, T])
        score = [sb(f"score{b}", [P, (b + 1) * P]) for b in range(TB)]
        top8 = sb("top8", [P, 8])
        logit = [sb("logit0", [P, NH, P]), early(3, [NH, T])]
        alibi = sb("alibi", [P, NH, T])
        probT = early(3, [2, NH * P])
        tmp = probT
        smx = sb("smx", [P, 2, TB, 3, NH])
        stats = sb("stats", [P, TB, 2, 6])
        mv = sb("mv", [P, TB, 5])
        lg = early(2, [TB, NG + NE])
        xg = early(2, [KC, P])
        rt = early(2, [16, TB, NE])
        rankp = early(2, [PASSES * PAIRS + 1, TB, 2])
        wpair = early(2, [PASSES * PAIRS, TB, 2])
        disp = early(2, [TB, 2, CAP])
        dispw = early(2, [TB, 2, CAP])
        comb = early(2, [TB * P])
        silu_g = early(2, [DFF])
        hexp = early(2, [DFF])
        hexT = early(2, [FC * P])
        yexp = early(2, [D])
        npass_f = sb("npass_f", [P, 8])
        npass_i = sb("npass_i", [P, 1], I32)
        acc = hn

        bank = ctx.enter_context(nc.psum_tensor("bank", [P, 8, HALF], F32))

        def pair_bank(i):
            return bank[:, i:i + 2, :].rearrange("p a (j k) -> p (a j) k", j=2)

        s_x = [sem(f"x_loaded{t}") for t in range(TB)]
        s_vin = sem("ln_in_rows_loaded")
        s_vr = sem("other_vector_rows_loaded")
        s_bf = sem("forget_bias_loaded")
        s_small = sem("small_params_loaded")
        s_slot = [sem(f"slot{i}_loaded") for i in range(RING)]
        s_lnp = sem("ln_params_loaded")
        s_bg = [sem(f"bgate{i}_loaded") for i in range(2)]
        s_wout = [sem(f"w_out{i}_loaded") for i in range(2)]
        s_const = sem("constants_built")
        s_ppad = sem("pool_rows_padded")
        s_idf = sem("identity_built")
        s_vT = sem("vector_rows_turned")
        s_vcol = sem("vector_columns_ready")
        s_var = sem("row_variance_ready")
        s_std = sem("row_std_ready")
        s_z = sem("x_normalised")
        s_xT = sem("x_turned")
        s_hTa = sem("hT_by_scalar")
        s_hTd = sem("hT_by_vector")
        s_hn = sem("hn_ready")
        UNITS = ["iq", "ik", "misc", "dq", "dk", "fq", "fk", "fv", "pool", "convb", "conva"]
        s_unit = sem("unit_projected")
        s_uout = {u: sem(f"{u}_out_of_psum") for u in UNITS}
        s_gate = sem("gate_projected")
        s_gout = sem("gate_out_of_psum")
        s_gbias = sem("gate_biased")
        s_gsig = sem("gate_sigmoid_done")
        s_idx = sem("indexer_scores_in_psum")
        s_rel = sem("indexer_relu_done")
        s_relu_used = sem("indexer_relu_used")
        s_sel = sem("selection_done")
        s_ls = sem("log_sigmoid_steps")
        s_lsa = sem("log_sigmoid_by_scalar")
        s_lsb = sem("log_sigmoid_spread")
        s_cum = sem("cumulated_in_psum")
        s_cumo = sem("cumulated_out_of_psum")
        s_s = sem("attention_scores_in_psum")
        s_lg = sem("logits_ready")
        s_exp = sem("exponentials_done")
        s_prob = sem("probabilities_ready")
        s_pT = sem("probabilities_turned")
        s_pTo = sem("turned_probabilities_out")
        s_pv = sem("values_weighted")
        s_att = sem("attention_branch_ready")
        s_poolin = sem("pool_means_ready")
        s_poolmm = sem("pool_mixed")
        s_poolo = sem("pool_branch_ready")
        s_glu = sem("glu_padded")
        s_conv = sem("convolution_done")
        s_cT = sem("convolution_turned")
        s_cz = sem("convolution_normalised")
        s_czT = sem("convolution_turned_back")
        s_cbr = sem("convolution_branch_ready")
        s_up = sem("branch_projected")
        s_mix = sem("branch_merged")
        s_mT = sem("merged_turned")
        s_mTo = sem("merged_turned_out")
        s_o = sem("output_projected")
        s_y1 = sem("residual_added")
        s_z1 = sem("layer1_normalised")
        s_zT = sem("layer1_turned")
        s_h1Ta = sem("layer1_turned_by_scalar")
        s_h1Td = sem("layer1_turned_by_vector")
        s_h1 = sem("layer1_output_ready")
        s_rt = sem("router_logits_in_psum")
        s_re = sem("router_exp_argument")
        s_rex = sem("router_exp_done")
        s_mask = sem("expert_mask_ready")
        s_rank = sem("ranks_in_psum")
        s_tab = sem("tables_ready")
        s_np = sem("passes_known")
        m_disp = sem("dispatch_ready")
        m_dispw = sem("weighted_dispatch_ready")
        m_xg = sem("tokens_gathered")
        m_xga = sem("gathered_out_by_scalar")
        m_xgd = sem("gathered_out_by_vector")
        m_g = sem("expert_gate_in_psum")
        m_u = sem("expert_up_in_psum")
        m_silu = sem("expert_silu_done")
        m_h = sem("expert_hidden_ready")
        m_hT = sem("expert_hidden_turned")
        m_hTo = sem("expert_hidden_turned_out")
        m_cT = sem("combine_turned")
        m_cTo = sem("combine_turned_out")
        m_y = sem("expert_output_in_psum")
        m_ya = sem("expert_output_out_by_scalar")
        m_yd = sem("expert_output_out_by_vector")
        m_c = sem("combined_in_psum")
        m_acc = sem("residual_sum_begun_or_added_to")
        s_dch = sem("vector_chain")
        s_pch = sem("gpsimd_chain")
        s_ach = sem("scalar_chain")
        s_fin = sem("output_rows_ready")
        s_out = sem("output_stored")

        block = ctx.enter_context(nc.Block())

        FRONT = ["s_idx", "s_dsa", "s_fox", "s_val", "s_conv"] + [f"g{t}" for t in range(8)] + ["wb0", "wb1"]
        SLOT = {name: n % SLOTS for n, name in enumerate(FRONT)}
        LOAD = {name: n // SLOTS + 1 for n, name in enumerate(FRONT)}
        FIRST = [16 * sum(1 for n in range(len(FRONT)) if n % SLOTS == s) + {1: 32, 3: 16}.get(s, 0)
                 for s in range(RING)]
        FIRST[SLOTS:] = [0] * (RING - SLOTS)

        def slot(name, cols=HALF):
            return ring[:, SLOT[name], 0:KC * cols].rearrange("p (k n) -> p k n", n=cols)

        def loaded(eng, name):
            eng.wait_ge(s_slot[SLOT[name]], 16 * LOAD[name])

        IDXC, DSAC = BW + DH, BW + 2 * DH + 2 * NH

        USED = {"s_idx": (s_unit, 2), "s_dsa": (s_unit, 5), "s_fox": (s_unit, 7), "s_val": (s_unit, 9),
                "s_conv": (s_unit, 11)}
        USED.update({f"g{t}": (s_gate, 2 * t + 2) for t in range(8)})
        USED.update({f"wb{q}": (s_up, 8 * q + 8) for q in range(2)})

        def slot_free(eng, n):
            if n >= SLOTS:
                eng.wait_ge(*USED[FRONT[n - SLOTS]])

        def expert_slot(s, n):
            return ring[:, s, :].rearrange("p (k n) -> p k n", n=n)

        @block.sync
        def _(sp):
            for t in range(TB):
                sp.dma_start(work[:, t, :], x_v[:, t, :]).then_inc(s_x[t], 16)
            sp.dma_start(slot("s_idx", IDXC), w_in[:, :, col["iq"]:col["iq"] + IDXC])\
                .then_inc(s_slot[0], 16)
            d = slot("s_dsa", DSAC)
            n = BW + 2 * DH
            sp.dma_start(d[:, :, 0:n], w_in[:, :, col["dq"]:col["dq"] + n]).then_inc(s_slot[1], 16)
            sp.dma_start(d[:, :, n:n + NH], w_in[:, :, col["iw"]:col["iw"] + NH]).then_inc(s_slot[1], 16)
            sp.dma_start(d[:, :, n + NH:n + 2 * NH], w_in[:, :, col["ff"]:col["ff"] + NH])\
                .then_inc(s_slot[1], 16)
            sp.dma_start(slot("s_fox"), w_in[:, :, col["fq"]:col["fq"] + 2 * BW]).then_inc(s_slot[2], 16)
            v = slot("s_val")
            sp.dma_start(v[:, :, 0:BW], w_in[:, :, col["pool"]:col["pool"] + BW]).then_inc(s_slot[3], 16)
            sp.dma_start(v[:, :, BW:2 * BW], w_in[:, :, col["fv"]:col["fv"] + BW]).then_inc(s_slot[3], 16)
            sp.dma_start(slot("s_conv"), w_in[:, :, col["conv"]:col["conv"] + 2 * BW])\
                .then_inc(s_slot[4], 16)
            for t in range(8):
                dq, n = divmod(t, NB)
                if t >= 2:
                    sp.wait_ge(s_gbias, t - 1)
                c = n * D + dq * HALF
                sp.dma_start(bgate[:, t % 2, :],
                             a["b_gate"][0][c:c + HALF].partition_broadcast(P)).then_inc(s_bg[t % 2], 16)
                slot_free(sp, 5 + t)
                c += col["gate"]
                sp.dma_start(slot(f"g{t}"), w_in[:, :, c:c + HALF]).then_inc(s_slot[SLOT[f"g{t}"]], 16)
            for dq in range(2):
                slot_free(sp, 13 + dq)
                sp.dma_start(slot(f"wb{dq}"), w_br[:, :, dq * HALF:(dq + 1) * HALF])\
                    .then_inc(s_slot[SLOT[f"wb{dq}"]], 16)
            sources = [e_gate[:, 0], e_gate[:, 1], e_up[:, 0], e_up[:, 1], e_down[:, 0], e_down[:, 1]]
            widths = [DFF, DFF, DFF, DFF, D, D]
            order = [(len(FRONT) + i) % SLOTS for i in range(SLOTS)]
            for i, s in enumerate(order):
                slot_free(sp, len(FRONT) + i)
                if i == 4:
                    sp.wait_ge(s_mix, 4 * NB // 2)
                    sp.dma_start(gates[:, 0, :].rearrange("p (k n) -> p k n", n=HALF),
                                 w_out[:, :, 0:HALF]).then_inc(s_wout[0], 16)
                sp.dma_start(expert_slot(s, widths[s]), sources[s]).then_inc(s_slot[s], 16)
            sp.wait_ge(s_mix, 4 * NB)
            sp.dma_start(gates[:, 1, :].rearrange("p (k n) -> p k n", n=HALF),
                         w_out[:, :, HALF:D]).then_inc(s_wout[1], 16)

            for e in range(RING - SLOTS):
                sp.dma_start(expert_slot(SLOTS + e, DFF), e_gate[:, 2 + e]).then_inc(s_slot[SLOTS + e], 16)

            def load_pairs(body, half, first):
                for n in range(first, BODY * 6):
                    pair, part = divmod(n, 6)
                    before, bpart = divmod(n - RING + BODY * 6, 6)
                    sp.wait_ge((m_g, m_u, m_y)[bpart // 2], body * BODY + before - BODY + 1)
                    src, w = ((e_gate, DFF), (e_up, DFF), (e_down, D))[part // 2]
                    e = 2 * (half * BODY + pair) + part % 2
                    sp.dma_start(expert_slot(n % RING, w), src[:, e]).then_inc(s_slot[n % RING], 16)

            load_pairs(0, 0, RING)
            load_pairs(1, 1, 0)
            sp.wait_ge(s_np, 1)
            npass = sp.value_load(npass_i[0:1, 0:1], min_val=1, max_val=PASSES)
            with sp.If(npass > 1):
                with sp.Fori(1, npass) as again:
                    for half in range(2):
                        load_pairs(sp.snap(again * 2 + half), half, 0)
            for t in range(TB):
                sp.wait_ge(s_fin, t + 1)
                sp.dma_start(out_v[:, t, :], work[:, t, :]).then_inc(s_out, 16)
            sp.wait_ge(s_out, 16 * TB)

        @block.gpsimd
        def _(pool):
            n = [0]

            def link(ins):
                n[0] += 1
                ins.then_inc(s_pch, 1)
                pool.wait_ge(s_pch, n[0])

            link(pool.memset(ident[:, :], 0.0))
            pool.affine_select(out=ident[:, :], in_=ident[:, :], compare_op=ALU.not_equal, fill=1.0, base=0,
                               pattern=[[-1, P]], channel_multiplier=1).then_inc(s_idf, 1)
            for r, src in vec_src[2:]:
                pool.dma_start(vrows[r:r + src.shape[0], :], src).then_inc(s_vr, 16)
            link(pool.memset(causal[:, :], 0.0))
            link(pool.affine_select(out=causal[:, :], in_=causal[:, :], compare_op=ALU.is_ge, fill=NEG,
                                    base=P, pattern=[[-1, T]], channel_multiplier=1))
            link(pool.iota(disti[:, :], [[-1, T]], base=P, channel_multiplier=1))
            link(pool.tensor_copy(dist[:, :], disti[:, :]))
            link(pool.memset(tri[:, :], 1.0))
            link(pool.affine_select(out=tri[:, :], in_=tri[:, :], compare_op=ALU.is_ge, fill=0.0,
                                    base=-P, pattern=[[1, 3 * P]], channel_multiplier=-1))
            link(pool.iota(disti[:, :], [[1, T]], base=1, channel_multiplier=0))
            for g, w in enumerate(WINDOWS):
                r = slice(DH * (g % 2), DH * (g % 2) + DH)
                link(pool.tensor_scalar(rcnt[r, g // 2, :], disti[r, :], float(w), None, ALU.min))
            link(pool.iota(disti[:, 0:CAP], [[1, CAP]], base=0, channel_multiplier=0))
            link(pool.tensor_copy(slot_no[:, :], disti[:, 0:CAP]))
            link(pool.iota(disti[:, 0:NG], [[-1, NG]], base=NG, channel_multiplier=0))
            link(pool.tensor_copy(desc4[:, :], disti[:, 0:NG]))
            pool.memset(hpad[:, :, 0:PADC], 0.0).then_inc(s_const, 1)

            def affine(t, dst, done):
                link(pool.tensor_tensor(dst[:, t, :], work[:, t, :], lnp[:, 0, :], ALU.mult))
                pool.tensor_tensor(dst[:, t, :], dst[:, t, :], lnp[:, 1, :], ALU.add).then_inc(done, 1)

            pw = a["pool_w"][0]
            for g in range(4):
                pool.dma_start(poolw[DH * (g % 2):DH * (g % 2) + DH, g // 2, :], pw[g]).then_inc(s_small, 16)
            pool.dma_start(rbias[:, 0:NG], a["router_g_b"][0].partition_broadcast(P)).then_inc(s_small, 16)
            pool.dma_start(rbias[:, NG:NG + NE], a["router_e_b"][0].partition_broadcast(P)).then_inc(s_small, 16)
            pool.dma_start(rw[:, :, 0:NG], a["router_g"][0].rearrange("(k p) n -> p k n", p=P)).then_inc(s_small, 16)
            pool.dma_start(rw[:, :, NG:NG + NE], a["router_e"][0].rearrange("(k p) n -> p k n", p=P))\
                .then_inc(s_small, 16)

            pool.wait_ge(s_lnp, 32)
            for t in range(TB):
                pool.wait_ge(s_z, t + 1)
                affine(t, hn, s_hn)
            pool.wait_ge(s_xT, TB)
            pool.wait_ge(s_hn, TB)
            pool.memset(poolv[:, :, 0:PADP], 0.0)
            pool.memset(pooled[0][:, :, 0:PADP], 0.0)
            pool.memset(pooled[1][:, :, 0:PADP], 0.0).then_inc(s_ppad, 1)
            for t in range(8):
                dq, nb = divmod(t, NB)
                pool.wait_ge(s_bg[t % 2], 16 * (t // 2 + 1))
                pool.wait_ge(s_gout, 2 * (t + 1))
                g = gates[:, dq, :].rearrange("p (t n c) -> p t n c", t=TB, n=NB)[:, :, nb, :]
                pool.tensor_tensor(g, g, bgate[:, t % 2, :].unsqueeze(1).broadcast_to([P, TB, HALF]),
                                   ALU.add).then_inc(s_gbias, 1)
            pool.wait_ge(s_lnp, 64)
            for t in range(TB):
                pool.wait_ge(s_zT, t + 1)
                affine(t, work, s_h1)

        @block.scalar
        def _(act):
            nln = [0]

            def root(t):
                nln[0] += 1
                act.wait_ge(s_var, nln[0])
                act.activation(mv[:, t, 3:4], mv[:, t, 2:3], ACT.Sqrt).then_inc(s_std, 1)

            def turned_rows(t, turned, bk, gain, bias, done):
                act.wait_ge(turned, t + 1)
                for k in range(KC // 2):
                    last = act.activation(hT[:, k, t * P:(t + 1) * P], bank[:, bk + 2 * t, k * P:(k + 1) * P],
                                          ACT.Identity, bias=vcol[:, ROW[bias] + k:ROW[bias] + k + 1],
                                          scale=vcol[:, ROW[gain] + k:ROW[gain] + k + 1])
                last.then_inc(done, 1)

            for r, src in vec_src[:2]:
                act.dma_start(vrows[r:r + src.shape[0], :], src).then_inc(s_vin, 16)
            act.dma_start(bforget[:, :], a["b_forget"][0].partition_broadcast(P)).then_inc(s_bf, 16)
            act.dma_start(lnp[:, 0, :], a["ln_in_g"].partition_broadcast(P)).then_inc(s_lnp, 16)
            act.dma_start(lnp[:, 1, :], a["ln_in_b"].partition_broadcast(P)).then_inc(s_lnp, 16)
            root(0)
            root(1)
            act.wait_ge(s_vcol, 1)
            for t in range(TB):
                turned_rows(t, s_xT, 0, "ln_in_g", "ln_in_b", s_hTa)
            unit_bank = {u: 2 + i % 2 for i, u in enumerate(UNITS)}

            def unit(name):
                act.wait_ge(s_unit, UNITS.index(name) + 1)
                return bank[:, unit_bank[name], :].rearrange("p (c t) -> p c t", c=2)

            def relu(b):
                act.wait_ge(s_idx, b + 1)
                if b:
                    act.wait_ge(s_relu_used, b)
                n = (b + 1) * P
                act.activation(rel[:, :, 0:n], pair_bank(4)[:, :, 0:n], ACT.Relu).then_inc(s_rel, 1)

            u = unit("iq")
            act.activation(iqT[:, :, :], u, ACT.Copy).then_inc(s_uout["iq"], 1)
            for name, dst in (("ik", ikT),):
                u = unit(name)
                act.activation(dst[0:DH, :], u[0:DH, 0, :], ACT.Copy)
                act.activation(dst[DH:P, :], u[0:DH, 0, :], ACT.Copy).then_inc(s_uout[name], 1)
            u = unit("misc")
            act.activation(misc[:, :, :], u[:, :, 0:DH + 2 * NH], ACT.Copy).then_inc(s_uout["misc"], 1)
            relu(0)
            act.wait_ge(s_ls, 1)
            act.activation(fs[:, 2], fs[:, 1], ACT.Exp, scale=-1.0).then_inc(s_lsa, 1)
            u = unit("dq")
            act.activation(dqT[:, :, :], u, ACT.Copy, scale=SCALE).then_inc(s_uout["dq"], 1)
            act.wait_ge(s_ls, 2)
            act.activation(fs[:, 4], fs[:, 3], ACT.Ln).then_inc(s_lsa, 1)
            relu(1)
            u = unit("dk")
            act.activation(dkT[0:DH, :], u[0:DH, 0, :], ACT.Copy)
            act.activation(dkT[DH:P, :], u[0:DH, 0, :], ACT.Copy).then_inc(s_uout["dk"], 1)
            u = unit("fq")
            act.activation(fqT[:, :, :], u, ACT.Copy, scale=SCALE).then_inc(s_uout["fq"], 1)
            u = unit("fk")
            act.activation(fkT[:, :, :], u, ACT.Copy).then_inc(s_uout["fk"], 1)
            u = unit("fv")
            act.activation(fv[:, :, :], u, ACT.Copy).then_inc(s_uout["fv"], 1)

            def exps(i):
                b = i % TB
                n = (b + 1) * P
                act.wait_ge(s_lg, i + 1)
                for hh in range(NH):
                    last = act.activation(logit[b][:, hh, 0:n], logit[b][:, hh, 0:n], ACT.Exp,
                                          bias=smx[:, i // TB, b, 0, hh:hh + 1],
                                          accum_out=smx[:, i // TB, b, 1, hh:hh + 1])
                last.then_inc(s_exp, 1)

            nturn = [0]

            def turned(kc):
                i = nturn[0]
                nturn[0] += 1
                act.wait_ge(s_pT, i + 1)
                need = {1: 1, 2: 1, 3: 2, 4: 3, 5: 3}.get(i)
                if need:
                    act.wait_ge(s_pv, need)
                act.activation(probT[:, kc, :], bank[:, 6, :], ACT.Copy).then_inc(s_pTo, 1)

            def branch(i):
                act.wait_ge(s_pv, 2 * (i + 1))
                act.activation(brT[:, 1 + i], bank[:, 7, :].rearrange("p (j t) -> p j t", j=2),
                               ACT.Copy).then_inc(s_att, 1)

            def gate_out(t, b):
                act.wait_ge(s_gate, 2 * t + b + 1)
                dq, nb = divmod(t, NB)
                g = gates[:, dq, :].rearrange("p (t n c) -> p t n c", t=TB, n=NB)
                act.activation(g[:, b, nb, :], bank[:, b, :], ACT.Copy).then_inc(s_gout, 1)

            exps(0)
            act.wait_ge(s_ppad, 1)
            u = unit("pool")
            act.activation(poolv[:, :, PADP:PADP + T], u, ACT.Copy).then_inc(s_uout["pool"], 1)
            exps(1)
            u = unit("convb")
            act.activation(glu[:, :, :], u, ACT.Sigmoid).then_inc(s_uout["convb"], 1)
            gate_out(0, 0)
            gate_out(0, 1)
            turned(0)
            gate_out(1, 0)
            turned(0)
            gate_out(1, 1)
            turned(1)
            gate_out(2, 0)
            branch(0)
            exps(2)
            gate_out(2, 1)
            gate_out(3, 0)
            turned(0)
            gate_out(3, 1)
            exps(3)
            gate_out(4, 0)
            gate_out(4, 1)
            turned(0)
            gate_out(5, 0)
            turned(1)
            gate_out(5, 1)
            branch(1)
            act.wait_ge(s_poolmm, 1)
            for q in range(2):
                r = slice(DH * q, DH * q + DH)
                for j in range(2):
                    c = ROW["pool_scale"] + j
                    last = act.activation(brT[r, 0, j, :], bank[r, 2 + q, j * T:(j + 1) * T],
                                          ACT.Copy, scale=vcol[r, c:c + 1])
            last.then_inc(s_poolo, 1)
            gate_out(6, 0)
            gate_out(6, 1)
            root(0)
            root(1)

            def sig(t):
                dq, nb = divmod(t, NB)
                act.wait_ge(s_gbias, t + 1)
                g = gates[:, dq, :].rearrange("p (t n c) -> p t n c", t=TB, n=NB)[:, :, nb, :]
                act.activation(g, g, ACT.Sigmoid).then_inc(s_gsig, 1)

            for t in range(3):
                sig(t)
            gate_out(7, 0)
            for t in range(3, 6):
                sig(t)
            gate_out(7, 1)
            for t in range(6, 8):
                sig(t)
            act.wait_ge(s_czT, 1)
            for c in range(2):
                last = act.activation(brT[:, 3, c, :], bank[:, 7, c * T:(c + 1) * T], ACT.Silu,
                                      bias=vcol[:, ROW["conv_ln_b"] + c:ROW["conv_ln_b"] + c + 1],
                                      scale=vcol[:, ROW["conv_ln_g"] + c:ROW["conv_ln_g"] + c + 1])
            last.then_inc(s_cbr, 1)
            act.wait_ge(s_hn, TB)
            act.dma_start(lnp[:, 0, :], a["ln1_g"][0].partition_broadcast(P)).then_inc(s_lnp, 16)
            act.dma_start(lnp[:, 1, :], a["ln1_b"][0].partition_broadcast(P)).then_inc(s_lnp, 16)
            for i in range(4):
                act.wait_ge(s_mT, i + 1)
                act.activation(hT[:, 2 * i:2 * i + 2, :],
                               bank[:, 4 + i % 2, :].rearrange("p (c t) -> p c t", c=2), ACT.Copy)\
                    .then_inc(s_mTo, 1)
            root(0)
            root(1)
            for t in range(TB):
                turned_rows(t, s_zT, 4, "ln1_g", "ln1_b", s_h1Ta)
            act.wait_ge(s_re, 1)
            act.activation(rt[:, 8, :, 0:NG + 1], rt[:, 7, :, 0:NG + 1], ACT.Exp).then_inc(s_rex, 1)
            act.wait_ge(s_h1, TB)
            act.dma_start(lnp[:, 0, :], a["ln2_g"][0].partition_broadcast(P)).then_inc(s_lnp, 16)
            act.dma_start(lnp[:, 1, :], a["ln2_b"][0].partition_broadcast(P)).then_inc(s_lnp, 16)
            act.wait_ge(s_np, 1)
            npass = act.value_load(npass_i[0:1, 0:1], min_val=1, max_val=PASSES)
            act.wait_ge(m_xg, 1)
            act.activation(xg[:, 0:KC // 2, :].rearrange("p k s -> p (k s)"), bank[:, 2, :], ACT.Copy)\
                .then_inc(m_xga, 1)
            with act.Fori(0, act.snap(npass * PAIRS)) as it:
                act.wait_ge(m_g, it + 1)
                act.activation(silu_g[:, :], bank[:, 0, :], ACT.Silu).then_inc(m_silu, 1)
                act.wait_ge(m_y, it + 1)
                act.activation(yexp[:, HALF:D], bank[:, 6, :], ACT.Copy).then_inc(m_ya, 1)
                act.wait_ge(m_xg, it + 2)
                act.activation(xg[:, 0:KC // 2, :].rearrange("p k s -> p (k s)"), bank[:, 2, :], ACT.Copy)\
                    .then_inc(m_xga, 1)
            root(0)
            root(1)

        @block.tensor
        def _(pe):
            pe.wait_ge(s_idf, 1)
            pe.wait_ge(s_vin, 32)
            pe.transpose(bank[:, 4, 0:NIN], vrows[0:NIN, :], ident[0:NIN, 0:NIN]).then_inc(s_vT, 1)

            def turn_rows(ready, bk, done):
                for t in range(TB):
                    pe.wait_ge(ready, t + 1)
                    for k in range(KC):
                        c = k % (KC // 2)
                        last = pe.transpose(bank[:, bk + 2 * t + k // (KC // 2), c * P:(c + 1) * P],
                                            work[:, t, k * P:(k + 1) * P], ident[:, :])
                    last.then_inc(done, 1)

            turn_rows(s_z, 0, s_xT)

            nunit = [0]

            def start_unit():
                i = nunit[0]
                if i >= 2:
                    pe.wait_ge(s_uout[UNITS[i - 2]], 1)
                nunit[0] += 1
                return bank[:, 2 + i % 2, :].rearrange("p (c t) -> p c t", c=2)

            def by_channel(w, c0, width):
                o = start_unit()
                m = min(P, width)
                for c in range((width + P - 1) // P):
                    for k in range(KC):
                        last = pe.matmul(o[0:m, c, :], w[:, k, c0 + c * P:c0 + c * P + m], hT[:, k, :],
                                         start=(k == 0), stop=(k == KC - 1))
                last.then_inc(s_unit, 1)

            def by_token(w, c0, width):
                o = start_unit()
                for t in range(TB):
                    for k in range(KC):
                        last = pe.matmul(o[:, t, 0:width], hT[:, k, t * P:(t + 1) * P],
                                         w[:, k, c0:c0 + width], start=(k == 0), stop=(k == KC - 1))
                last.then_inc(s_unit, 1)

            def scores(qT, kT, shared, b, done):
                n = (b + 1) * P
                o = pair_bank(4)
                for j in range(2):
                    for par in range(2):
                        r = slice(DH * par, DH * par + DH)
                        k = kT[r, 0:n] if shared else kT[r, j, 0:n]
                        last = pe.matmul(o[:, 2 * par + j, 0:n], qT[r, j, b * P:(b + 1) * P], k,
                                         start=True, stop=True)
                last.then_inc(done, 1)

            pe.wait_ge(s_hTa, TB)
            pe.wait_ge(s_hTd, TB)
            loaded(pe, "s_idx")
            w = slot("s_idx", IDXC)
            by_channel(w, 0, BW)
            by_channel(w, BW, DH)
            pe.wait_ge(s_slot[1], 48)
            w = slot("s_dsa", DSAC)
            by_token(w, BW + DH, DH + 2 * NH)
            pe.wait_ge(s_uout["iq"], 1)
            pe.wait_ge(s_uout["ik"], 1)
            scores(iqT, ikT, True, 0, s_idx)
            by_channel(w, 0, BW)
            pe.wait_ge(s_rel, 1)
            scores(iqT, ikT, True, 1, s_idx)
            by_channel(w, BW, DH)
            loaded(pe, "s_fox")
            w = slot("s_fox")
            by_channel(w, 0, BW)
            by_channel(w, BW, BW)
            pe.wait_ge(s_vr, 16 * (len(vec_src) - 2))
            pe.transpose(bank[:, 7, 0:NROW], vrows[:, :], ident[0:NROW, 0:NROW]).then_inc(s_vT, 1)
            pe.wait_ge(s_lsb, 2)
            pe.wait_ge(s_const, 1)
            o = pair_bank(0)
            for hh in range(NH):
                h = 2 * (hh % 2) + hh // 2
                pe.matmul(o[:, hh, :], lsb[:, 0, h, :], tri[:, P:P + T], start=True, stop=False)
                pe.matmul(o[:, hh, :], lsb[:, 1, h, :], tri[:, 0:T], start=False, stop=True)
            pe.matmul(bank[:, 6, 0:NH], tri[:, P:2 * P], fs[:, 5, 0, :], start=True, stop=True)
            pe.matmul(bank[:, 6, NH:2 * NH], tri[:, 2 * P:3 * P], fs[:, 5, 0, :], start=True, stop=False)
            pe.matmul(bank[:, 6, NH:2 * NH], tri[:, P:2 * P], fs[:, 5, 1, :], start=False, stop=True)\
                .then_inc(s_cum, 1)
            loaded_val = 32
            pe.wait_ge(s_slot[3], loaded_val)
            w = slot("s_val")
            by_token(w, BW, BW)
            pe.wait_ge(s_uout["fq"], 1)
            pe.wait_ge(s_uout["fk"], 1)
            pe.wait_ge(s_rel, 2)
            scores(fqT, fkT, False, 0, s_s)
            by_channel(w, 0, BW)
            pe.wait_ge(s_lg, 1)
            scores(fqT, fkT, False, 1, s_s)
            loaded(pe, "s_conv")
            w = slot("s_conv")
            by_channel(w, BW, BW)
            by_channel(w, 0, BW)

            def gate(t, b):
                if b == 0:
                    loaded_gate(t)
                w = slot(f"g{t}")
                if t:
                    pe.wait_ge(s_gout, 2 * (t - 1) + b + 1)
                elif b == 0:
                    pe.wait_ge(s_cumo, 1)
                for k in range(KC):
                    last = pe.matmul(bank[:, b, :], hT[:, k, b * P:(b + 1) * P], w[:, k, :],
                                     start=(k == 0), stop=(k == KC - 1))
                last.then_inc(s_gate, 1)

            def loaded_gate(t):
                n = f"g{t}"
                extra = {1: 32, 3: 16}.get(SLOT[n], 0)
                pe.wait_ge(s_slot[SLOT[n]], 16 * LOAD[n] + extra)

            nturn = [0]

            def turn(i, kc):
                if nturn[0] == 0:
                    pe.wait_ge(s_cumo, 1)
                else:
                    pe.wait_ge(s_pTo, nturn[0])
                nturn[0] += 1
                pe.wait_ge(s_prob, i + 1)
                b = i % TB
                for hh in range(NH):
                    last = pe.transpose(bank[:, 6, hh * P:(hh + 1) * P],
                                        logit[b][:, hh, kc * P:(kc + 1) * P], ident[:, :])
                last.then_inc(s_pT, 1)

            def weigh(i, value):
                b = i % TB
                pe.wait_ge(s_pTo, nturn[0])
                if i == 0:
                    pe.wait_ge(s_vcol, 2)
                if i == TB:
                    pe.wait_ge(s_att, 1)
                for hh in range(NH):
                    par, j = hh // 2, hh % 2
                    for kc in range(b + 1):
                        last = pe.matmul(bank[DH * par:DH * par + DH, 7, j * T + b * P:j * T + (b + 1) * P],
                                         value(kc, 2 * j + par), probT[:, kc, hh * P:(hh + 1) * P],
                                         start=(kc == 0), stop=(kc == b))
                last.then_inc(s_pv, 1)

            def fox_v(kc, h):
                return fv[:, kc, h * DH:(h + 1) * DH]

            def dsa_v(kc, h):
                return misc[:, kc, 0:DH]

            gate(0, 0)
            gate(0, 1)
            turn(0, 0)
            gate(1, 0)
            weigh(0, fox_v)
            turn(1, 0)
            gate(1, 1)
            turn(1, 1)
            gate(2, 0)
            weigh(1, fox_v)
            pe.wait_ge(s_lg, 2)
            scores(dqT, dkT, True, 0, s_s)
            gate(2, 1)
            gate(3, 0)
            turn(2, 0)
            gate(3, 1)
            weigh(2, dsa_v)
            pe.wait_ge(s_lg, 3)
            scores(dqT, dkT, True, 1, s_s)
            gate(4, 0)
            gate(4, 1)
            turn(3, 0)
            gate(5, 0)
            turn(3, 1)
            gate(5, 1)
            weigh(3, dsa_v)
            pe.wait_ge(s_poolin, 1)
            pe.wait_ge(s_small, 16 * 8)
            pe.wait_ge(s_uout["conva"], 1)
            for g in range(4):
                r = slice(DH * (g % 2), DH * (g % 2) + DH)
                last = pe.matmul(bank[r, 2 + g % 2, (g // 2) * T:(g // 2 + 1) * T], poolw[r, g // 2, :],
                                 pooled[0][r, g // 2, PADP:PADP + T], start=True, stop=True)
            last.then_inc(s_poolmm, 1)
            gate(6, 0)
            gate(6, 1)
            pe.wait_ge(s_conv, 1)
            pe.wait_ge(s_pTo, 6)
            for t in range(TB):
                for c in range(2):
                    last = pe.transpose(bank[:, 6, t * T + c * P:t * T + (c + 1) * P],
                                        convy[:, c, t * P:(t + 1) * P], ident[:, :])
            last.then_inc(s_cT, 1)
            gate(7, 0)
            gate(7, 1)
            pe.wait_ge(s_cz, 1)
            pe.wait_ge(s_att, 2)
            for c in range(2):
                for t in range(TB):
                    last = pe.transpose(bank[:, 7, c * T + t * P:c * T + (t + 1) * P],
                                        glu[:, t, c * P:(c + 1) * P], ident[:, :])
            last.then_inc(s_czT, 1)

            pe.wait_ge(s_att, 2)
            pe.wait_ge(s_poolo, 1)
            i = 0
            for dq in range(2):
                pe.wait_ge(s_slot[SLOT[f"wb{dq}"]],
                           16 * LOAD[f"wb{dq}"] + {1: 32, 3: 16}.get(SLOT[f"wb{dq}"], 0))
                w = slot(f"wb{dq}")
                for t in range(TB):
                    for n in range(NB):
                        if i < 2:
                            pe.wait_ge(s_gout, 16)
                        if n == 3:
                            pe.wait_ge(s_cbr, 1)
                        if i >= 4:
                            pe.wait_ge(s_mix, i - 3)
                        for kc in range(2):
                            last = pe.matmul(bank[:, i % 4, :], brT[:, n, kc, t * P:(t + 1) * P],
                                             w[:, 2 * n + kc, :], start=(kc == 0), stop=(kc == 1))
                        last.then_inc(s_up, 1)
                        i += 1
            for i in range(4):
                pe.wait_ge(s_mix, 8 * (i // 2 + 1))
                if i < 2:
                    pe.wait_ge(s_lg, 4)
                else:
                    pe.wait_ge(s_mTo, i - 1)
                for kk in range(2):
                    for t in range(TB):
                        k = 2 * i + kk
                        last = pe.transpose(bank[:, 4 + i % 2, kk * T + t * P:kk * T + (t + 1) * P],
                                            work[:, t, k * P:(k + 1) * P], ident[:, :])
                last.then_inc(s_mT, 1)
            pe.wait_ge(s_mTo, 4)
            for j in range(2):
                pe.wait_ge(s_wout[j], 16)
                w = gates[:, j, :].rearrange("p (k n) -> p k n", n=HALF)
                for t in range(TB):
                    for k in range(KC):
                        last = pe.matmul(bank[:, 2 * t + j, :], hT[:, k, t * P:(t + 1) * P], w[:, k, :],
                                         start=(k == 0), stop=(k == KC - 1))
                    last.then_inc(s_o, 1)
            turn_rows(s_z1, 4, s_zT)
            for t in range(TB):
                pe.wait_ge(s_h1Ta, t + 1)
                pe.wait_ge(s_h1Td, t + 1)
                for k in range(KC):
                    last = pe.matmul(bank[:, 0, t * 32:t * 32 + NG + NE], hT[:, k, t * P:(t + 1) * P],
                                     rw[:, k, :], start=(k == 0), stop=(k == KC - 1))
            last.then_inc(s_rt, 1)
            pe.wait_ge(s_mask, 1)
            mask = [rt[:, 12, t, :] for t in range(TB)]
            o = bank[:, 1, 0:3 * NE]
            pe.matmul(o[:, 0:NE], tri[:, P:2 * P], mask[0], start=True, stop=True)
            pe.matmul(o[:, NE:2 * NE], tri[:, 2 * P:3 * P], mask[0], start=True, stop=False)
            pe.matmul(o[:, NE:2 * NE], tri[:, P:2 * P], mask[1], start=False, stop=True)
            pe.matmul(o[:, 2 * NE:3 * NE], tri[:, 2 * P:3 * P], mask[0], start=True, stop=False)
            pe.matmul(o[:, 2 * NE:3 * NE], tri[:, 2 * P:3 * P], mask[1], start=False, stop=True)\
                .then_inc(s_rank, 1)

            def gather(chunks):
                for k in chunks:
                    for t in range(TB):
                        last = pe.matmul(bank[:, 2 + k // 4, (k % 4) * P:(k % 4 + 1) * P],
                                         work[:, t, k * P:(k + 1) * P],
                                         disp[:, t].rearrange("p e s -> p (e s)"),
                                         start=(t == 0), stop=(t == TB - 1))
                if k == KC - 1:
                    last.then_inc(m_xg, 1)

            pe.wait_ge(m_disp, 1)
            pe.wait_ge(s_h1, TB)
            gather(range(KC))
            pe.wait_ge(s_np, 1)
            npass = pe.value_load(npass_i[0:1, 0:1], min_val=1, max_val=PASSES)
            with pe.Fori(0, pe.snap(npass * (PAIRS // BODY))) as body:
                for j in range(BODY):
                    it = body * BODY + j

                    def weights(part, n):
                        load = 6 * j + part
                        s = load % RING
                        each = BODY * 6 // RING
                        pe.wait_ge(s_slot[s], body * (16 * each) + FIRST[s] + 16 * (load // RING + 1))
                        return expert_slot(s, n)

                    pe.wait_ge(m_xga, it + 1)
                    pe.wait_ge(m_xgd, it + 1)
                    for first, bk, done in ((0, 0, m_g), (2, 1, m_u)):
                        w = [weights(first + e, DFF) for e in range(2)]
                        for k in range(KC):
                            for e in range(2):
                                last = pe.matmul(bank[CAP * e:CAP * e + CAP, bk, :],
                                                 xg[:, k, CAP * e:CAP * e + CAP], w[e][:, k, :],
                                                 start=(k == 0), stop=(k == KC - 1))
                        last.then_inc(done, 1)
                    pe.wait_ge(m_dispw, it + 1)
                    pe.wait_ge(m_acc, it * 4 + 1)
                    for t in range(TB):
                        last = pe.transpose(bank[:, 7, t * P:(t + 1) * P],
                                            dispw[:, t].rearrange("p e s -> p (e s)"), ident[:, :])
                    last.then_inc(m_cT, 1)
                    pe.wait_ge(m_disp, it + 2)
                    gather(range(0, 2))
                    pe.wait_ge(m_h, it + 1)
                    for f in range(FC):
                        last = pe.transpose(bank[:, 4, f * P:(f + 1) * P], hexp[:, f * P:(f + 1) * P],
                                            ident[:, :])
                    last.then_inc(m_hT, 1)
                    gather(range(2, 4))
                    pe.wait_ge(m_hTo, it + 1)
                    w = [weights(4 + e, D) for e in range(2)]
                    for half in range(2):
                        for f in range(FC):
                            for e in range(2):
                                last = pe.matmul(bank[CAP * e:CAP * e + CAP, 5 + half, :],
                                                 hexT[:, f * P + CAP * e:f * P + CAP * e + CAP],
                                                 w[e][:, f, half * HALF:(half + 1) * HALF],
                                                 start=(f == 0), stop=(f == FC - 1))
                    last.then_inc(m_y, 1)
                    gather(range(4, KC))
                    pe.wait_ge(m_cTo, it + 1)
                    pe.wait_ge(m_yd, it + 1)
                    pe.wait_ge(m_ya, it + 1)
                    for i in range(4):
                        t, half = divmod(i, 2)
                        if i >= 2:
                            pe.wait_ge(m_acc, it * 4 + i)
                        pe.matmul(bank[:, 7 if i % 2 == 0 else 4, :], comb[:, t * P:(t + 1) * P],
                                  yexp[:, half * HALF:(half + 1) * HALF], start=True, stop=True)\
                            .then_inc(m_c, 1)

        @block.vector
        def _(dve):
            n = [0]

            def chain(ins):
                n[0] += 1
                ins.then_inc(s_dch, 1)
                return n[0]

            def link(ins):
                dve.wait_ge(s_dch, chain(ins))

            nln = [0]

            def row_stats(t, src, width):
                parts = (width + HALF - 1) // HALF
                for i in range(parts):
                    w = width // parts
                    last = dve.bn_stats(stats[:, t, i, :], src[:, i * w:(i + 1) * w])
                link(last)
                link(dve.bn_aggr(mv[:, t, 0:2], stats[:, t, 0:parts, :]))
                dve.tensor_scalar(mv[:, t, 2:3], mv[:, t, 1:2], EPS, None, ALU.add).then_inc(s_var, 1)

            def inverse_std(t):
                nln[0] += 1
                dve.wait_ge(s_std, nln[0])
                link(dve.reciprocal(mv[:, t, 4:5], mv[:, t, 3:4]))

            def normalise(t, src, dst):
                return dve.tensor_scalar(dst, src, mv[:, t, 0:1], mv[:, t, 4:5], ALU.subtract, ALU.mult)

            for t in range(TB):
                dve.wait_ge(s_x[t], 16)
                row_stats(t, work[:, t, :], D)
            for t in range(TB):
                inverse_std(t)
                normalise(t, work[:, t, :], work[:, t, :]).then_inc(s_z, 1)
            dve.wait_ge(s_vT, 1)
            dve.tensor_copy(vcol[:, 0:NIN], bank[:, 4, 0:NIN]).then_inc(s_vcol, 1)
            dve.wait_ge(s_vcol, 1)

            def turned_rows(t, turned, bk, gain, bias, done):
                dve.wait_ge(turned, t + 1)
                for k in range(KC // 2, KC):
                    c = k - KC // 2
                    last = dve.tensor_scalar(hT[:, k, t * P:(t + 1) * P],
                                             bank[:, bk + 2 * t + 1, c * P:(c + 1) * P],
                                             vcol[:, ROW[gain] + k:ROW[gain] + k + 1],
                                             vcol[:, ROW[bias] + k:ROW[bias] + k + 1], ALU.mult, ALU.add)
                last.then_inc(done, 1)

            for t in range(TB):
                turned_rows(t, s_xT, 0, "ln_in_g", "ln_in_b", s_hTd)
            dve.wait_ge(s_uout["misc"], 1)
            dve.wait_ge(s_bf, 16)
            link(dve.tensor_tensor(fs[:, 0], misc[:, :, DH + NH:DH + 2 * NH],
                                   bforget[:, :].unsqueeze(1).broadcast_to([P, TB, NH]), ALU.add))
            link(dve.tensor_scalar(fs[:, 1], fs[:, 0], -1.0, None, ALU.mult))
            dve.tensor_tensor(fs[:, 1], fs[:, 0], fs[:, 1], ALU.max).then_inc(s_ls, 1)
            dve.wait_ge(s_lsa, 1)
            dve.tensor_scalar(fs[:, 3], fs[:, 2], 1.0, None, ALU.add).then_inc(s_ls, 1)

            def index_score(b):
                m = (b + 1) * P
                dve.wait_ge(s_rel, b + 1)
                for h in range(NH):
                    hh = 2 * (h % 2) + h // 2
                    w = misc[:, b, DH + h:DH + h + 1]
                    if h == 0:
                        ins = dve.tensor_scalar(score[b][:, :], rel[:, hh, 0:m], w, None, ALU.mult)
                    else:
                        ins = dve.scalar_tensor_tensor(out=score[b][:, :], in0=rel[:, hh, 0:m], scalar=w,
                                                       in1=score[b][:, :], op0=ALU.mult, op1=ALU.add)
                    link(ins)
                dve.tensor_tensor(score[b][:, :], score[b][:, :], causal[:, T - m:T], ALU.add)\
                    .then_inc(s_relu_used, 1)
                dve.wait_ge(s_relu_used, b + 1)

            dve.wait_ge(s_const, 1)
            index_score(0)
            dve.wait_ge(s_lsa, 2)
            dve.scalar_tensor_tensor(out=fs[:, 5], in0=fs[:, 0], scalar=0.0, in1=fs[:, 4],
                                     op0=ALU.min, op1=ALU.subtract).then_inc(s_lsb, 1)
            dve.wait_ge(s_lsb, 1)
            dve.tensor_copy(lsb[:, :, :, :], fs[:, 5].unsqueeze(3).broadcast_to([P, TB, NH, P]))\
                .then_inc(s_lsb, 1)
            index_score(1)
            dve.wait_ge(s_vT, 2)
            dve.tensor_copy(vcol[:, NIN:NROW], bank[:, 7, NIN:NROW]).then_inc(s_vcol, 1)
            dve.wait_ge(s_cum, 1)
            dve.tensor_copy(cq[:, :, :], bank[:, 6, 0:TB * NH].rearrange("p (t h) -> p t h", t=TB))
            dve.scalar_tensor_tensor(out=fbias0[:, :, :], in0=pair_bank(0)[:, :, 0:P], scalar=-1.0,
                                     in1=causal[:, P:T].unsqueeze(1).broadcast_to([P, NH, P]),
                                     op0=ALU.mult, op1=ALU.add)
            dve.scalar_tensor_tensor(out=fbias1[:, :, :], in0=pair_bank(0), scalar=-1.0,
                                     in1=causal[:, :].unsqueeze(1).broadcast_to([P, NH, T]),
                                     op0=ALU.mult, op1=ALU.add).then_inc(s_cumo, 1)
            dve.wait_ge(s_cumo, 1)

            def negmax(i):
                b = i % TB
                dve.tensor_reduce(smx[:, i // TB, b, 0, :], logit[b][:, :, :], AX.X, ALU.max,
                                  negate=True).then_inc(s_lg, 1)

            def probs(i):
                b = i % TB
                s = smx[:, i // TB, b]
                dve.wait_ge(s_exp, i + 1)
                link(dve.reciprocal(s[:, 2, :], s[:, 1, :]))
                for hh in range(NH):
                    last = dve.tensor_scalar(logit[b][:, hh, :], logit[b][:, hh, :], s[:, 2, hh:hh + 1],
                                             None, ALU.mult)
                last.then_inc(s_prob, 1)

            def fox(b):
                fb = fbias1 if b else fbias0
                m = (b + 1) * P
                dve.wait_ge(s_s, b + 1)
                for hh in range(NH):
                    h = 2 * (hh % 2) + hh // 2
                    last = dve.scalar_tensor_tensor(out=logit[b][:, hh, :], in0=pair_bank(4)[:, hh, 0:m],
                                                    scalar=cq[:, b, h:h + 1], in1=fb[:, hh, :],
                                                    op0=ALU.add, op1=ALU.add)
                link(last)
                negmax(b)

            def select(b):
                s = score[b][:, :]
                for r in range(ROUNDS):
                    link(dve.max(top8[:, :], s))
                    link(dve.match_replace(s, top8[:, :], s, TAKEN))
                link(dve.tensor_scalar(s, s, TAKEN / 2, NEG, ALU.is_gt, ALU.mult))
                link(dve.tensor_tensor(s, s, causal[:, T - (b + 1) * P:T], ALU.add))

            def dsa(b):
                m = (b + 1) * P
                for hh in range(NH):
                    h = 2 * (hh % 2) + hh // 2
                    last = dve.scalar_tensor_tensor(out=alibi[:, hh, 0:m], in0=dist[:, T - m:T],
                                                    scalar=-SLOPES[h], in1=score[b][:, :],
                                                    op0=ALU.mult, op1=ALU.add)
                link(last)
                dve.wait_ge(s_s, TB + b + 1)
                dve.wait_ge(s_pT, 1 if b == 0 else 3)
                link(dve.tensor_tensor(logit[b][:, :, :], pair_bank(4)[:, :, 0:m], alibi[:, :, 0:m], ALU.add))
                negmax(TB + b)

            done = [0, 0]

            def tap(taps):
                for j in taps:
                    for c in range(2):
                        w = vcol[:, ROW["conv_dw"] + 2 * j + c:ROW["conv_dw"] + 2 * j + c + 1]
                        src = hpad[:, c, j:j + T]
                        if j == 0:
                            b = ROW["conv_b"] + c
                            ins = dve.tensor_scalar(convy[:, c, :], src, w, vcol[:, b:b + 1], ALU.mult, ALU.add)
                        else:
                            dve.wait_ge(s_dch, done[c])
                            ins = dve.scalar_tensor_tensor(out=convy[:, c, :], in0=src, scalar=w,
                                                           in1=convy[:, c, :], op0=ALU.mult, op1=ALU.add)
                        if j == CONV_W - 1 and c == 1:
                            ins.then_inc(s_conv, 1)
                        else:
                            done[c] = chain(ins)

            fox(0)
            probs(0)
            fox(1)
            probs(1)
            dve.wait_ge(s_unit, len(UNITS))
            dve.wait_ge(s_uout["convb"], 1)
            dve.tensor_tensor(hpad[:, :, PADC:PADC + T], bank[:, 2, :].rearrange("p (c t) -> p c t", c=2),
                              glu[:, :, :], ALU.mult).then_inc(s_uout["conva"], 1)
            dve.wait_ge(s_uout["conva"], 1)
            select(0)
            select(1)
            link(dve.reciprocal(rcnt[:, :, :], rcnt[:, :, :]))
            dve.wait_ge(s_vcol, 2)
            tap(range(0, 20))
            dsa(0)
            probs(2)
            tap(range(20, CONV_W))
            dve.wait_ge(s_uout["pool"], 1)
            pmean = glu
            src = poolv
            for g, w in enumerate(WINDOWS):
                dst = pooled[g % 2]
                j0 = g // 2
                link(dve.tensor_tensor(dst[:, j0:2, PADP:], src[:, j0:2, PADP:],
                                       src[:, j0:2, PADP - w // 2:PADP + T - w // 2], ALU.add))
                r = slice(DH * (g % 2), DH * (g % 2) + DH)
                link(dve.tensor_tensor(pmean[r, g // 2, :], dst[r, g // 2, PADP:], rcnt[r, g // 2, :], ALU.mult))
                src = dst
            dve.tensor_tensor(pooled[0][:, :, PADP:], pmean[:, :, :], poolv[:, :, PADP:], ALU.subtract)\
                .then_inc(s_poolin, 1)
            dsa(1)
            probs(3)
            dve.wait_ge(s_cT, 1)
            for t in range(TB):
                row_stats(t, bank[:, 6, t * T:(t + 1) * T], BW)
            for t in range(TB):
                inverse_std(t)
            for t in range(TB):
                last = normalise(t, bank[:, 6, t * T:(t + 1) * T], glu[:, t, :])
            last.then_inc(s_cz, 1)

            i = 0
            for dq in range(2):
                g = gates[:, dq, :].rearrange("p (t n c) -> p t n c", t=TB, n=NB)
                for t in range(TB):
                    o = work[:, t, dq * HALF:(dq + 1) * HALF]
                    if i == 0:
                        dve.wait_ge(s_hn, TB)
                    for nb in range(NB):
                        dve.wait_ge(s_up, i + 1)
                        dve.wait_ge(s_gsig, 4 * dq + nb + 1)
                        dst = o if nb == 0 else tmp[:, nb % 2, :]
                        ins = dve.tensor_tensor(dst, bank[:, i % 4, :], g[:, t, nb, :], ALU.mult)
                        if nb:
                            link(ins)
                            dve.tensor_tensor(o, o, tmp[:, nb % 2, :], ALU.add).then_inc(s_mix, 1)
                        else:
                            ins.then_inc(s_mix, 1)
                        i += 1
                        dve.wait_ge(s_mix, i)
            dve.wait_ge(s_mT, 4)

            def residual(t, j):
                dve.wait_ge(s_o, 2 * j + t + 1)
                c = slice(j * HALF, (j + 1) * HALF)
                link(dve.scalar_tensor_tensor(out=work[:, t, c], in0=hn[:, t, c], scalar=ALPHA,
                                              in1=bank[:, 2 * t + j, :], op0=ALU.mult, op1=ALU.add))

            residual(0, 0)
            residual(1, 0)
            for t in range(TB):
                residual(t, 1)
                row_stats(t, work[:, t, :], D)
                inverse_std(t)
                normalise(t, work[:, t, :], work[:, t, :]).then_inc(s_z1, 1)
            for t in range(TB):
                turned_rows(t, s_zT, 4, "ln1_g", "ln1_b", s_h1Td)
            dve.wait_ge(s_rt, 1)
            R = [rt[:, i] for i in range(16)]
            link(dve.tensor_tensor(lg, bank[:, 0, 0:TB * 32].rearrange("p (t n) -> p t n", t=TB)[:, :, 0:NG + NE],
                                   rbias[:, :].unsqueeze(1).broadcast_to([P, TB, NG + NE]), ALU.add))
            order = desc4[:, :].unsqueeze(1).broadcast_to([P, TB, NG])

            def first_max(v, val, hot, s):
                link(dve.tensor_reduce(val, v, AX.X, ALU.max))
                link(dve.tensor_tensor(s, v, val.unsqueeze(2).broadcast_to([P, TB, NG]), ALU.is_equal))
                link(dve.tensor_tensor(s, s, order, ALU.mult))
                link(dve.tensor_reduce(R[15][:, :, 0], s, AX.X, ALU.max))
                link(dve.tensor_tensor(hot, s, R[15][:, :, 0:1].broadcast_to([P, TB, NG]), ALU.is_equal))

            gmax, hotg, le = R[0][:, :, 0], R[1][:, :, 0:NG], R[3][:, :, 0:EPG]
            first_max(lg[:, :, 0:NG], gmax, hotg, R[2][:, :, 0:NG])
            link(dve.tensor_tensor(R[7][:, :, 0:NG], lg[:, :, 0:NG],
                                   R[0][:, :, 0:1].broadcast_to([P, TB, NG]), ALU.subtract))
            hotg4 = hotg.unsqueeze(3).broadcast_to([P, TB, NG, EPG])
            prod = R[2].rearrange("p t (g j) -> p t g j", g=NG)
            link(dve.tensor_tensor(prod, lg[:, :, NG:].rearrange("p t (g j) -> p t g j", g=NG), hotg4, ALU.mult))
            link(dve.tensor_reduce(le, R[2].rearrange("p t (g j) -> p t j g", g=NG), AX.X, ALU.add))
            hot1, hot2 = R[4][:, :, 0:EPG], R[5][:, :, 0:EPG]
            first_max(le, R[0][:, :, 1], hot1, R[6][:, :, 0:EPG])
            link(dve.scalar_tensor_tensor(out=R[6][:, :, 4:8], in0=hot1, scalar=TAKEN, in1=le,
                                          op0=ALU.mult, op1=ALU.add))
            first_max(R[6][:, :, 4:8], R[0][:, :, 2], hot2, R[6][:, :, 0:EPG])
            dve.tensor_tensor(R[7][:, :, NG:NG + 1], R[0][:, :, 2:3], R[0][:, :, 1:2], ALU.subtract)\
                .then_inc(s_re, 1)
            link(dve.tensor_tensor(R[9][:, :, 0:EPG], hot1, hot2, ALU.add))
            dve.tensor_tensor(R[12].rearrange("p t (g j) -> p t g j", g=NG), hotg4,
                              R[9][:, :, 0:EPG].unsqueeze(2).broadcast_to([P, TB, NG, EPG]), ALU.mult)\
                .then_inc(s_mask, 1)
            dve.wait_ge(s_rex, 1)
            link(dve.tensor_reduce(R[10][:, :, 0], R[8][:, :, 0:NG], AX.X, ALU.add))
            link(dve.tensor_scalar(R[10][:, :, 1], R[8][:, :, NG], 1.0, None, ALU.add))
            link(dve.reciprocal(R[10][:, :, 2:4], R[10][:, :, 0:2]))
            link(dve.tensor_tensor(R[10][:, :, 4], R[10][:, :, 2], R[10][:, :, 3], ALU.mult))
            link(dve.tensor_tensor(R[10][:, :, 5], R[10][:, :, 4], R[8][:, :, NG], ALU.mult))
            link(dve.tensor_tensor(R[11][:, :, 0:EPG], hot1, R[10][:, :, 4:5].broadcast_to([P, TB, EPG]), ALU.mult))
            link(dve.tensor_tensor(R[11][:, :, 4:8], hot2, R[10][:, :, 5:6].broadcast_to([P, TB, EPG]), ALU.mult))
            link(dve.tensor_tensor(R[11][:, :, 0:EPG], R[11][:, :, 0:EPG], R[11][:, :, 4:8], ALU.add))
            link(dve.tensor_tensor(R[13].rearrange("p t (g j) -> p t g j", g=NG), hotg4,
                                   R[11][:, :, 0:EPG].unsqueeze(2).broadcast_to([P, TB, NG, EPG]), ALU.mult))
            dve.wait_ge(s_rank, 1)
            ranks = bank[:, 1, 0:2 * NE].rearrange("p (t e) -> p t e", t=TB)
            link(dve.tensor_tensor(R[14], ranks, R[12], ALU.mult))
            slots = slot_no[:, :].unsqueeze(1).broadcast_to([P, 2, CAP])

            def dispatch(it):
                for t in range(TB):
                    r = rankp[:, bass.ds(it, 1), t, :].rearrange("p o e -> p (o e)")
                    last = dve.tensor_tensor(disp[:, t], slots, r.unsqueeze(2).broadcast_to([P, 2, CAP]),
                                             ALU.is_equal)
                last.then_inc(m_disp, 1)

            def pass_ranks(q):
                for t in range(TB):
                    last = dve.tensor_scalar(rankp[:, q * PAIRS:(q + 1) * PAIRS, t, :],
                                             R[14][:, t].rearrange("p (i e) -> p i e", e=2),
                                             -1.0 - CAP * q, None, ALU.add)
                return last

            link(pass_ranks(0))
            dispatch(0)
            dve.memset(npass_f[:, 0:1], 1.0)
            link(dve.tensor_reduce(npass_f[:, 6:7], bank[:, 1, 2 * NE:3 * NE], AX.X, ALU.max))
            for q in range(1, PASSES):
                last = dve.tensor_scalar(npass_f[:, q:q + 1], npass_f[:, 6:7], CAP * q + 0.5, None, ALU.is_gt)
            link(last)
            link(dve.tensor_reduce(npass_f[:, PASSES:PASSES + 1], npass_f[:, 0:PASSES], AX.X, ALU.add))
            dve.tensor_copy(npass_i[:, :], npass_f[:, PASSES:PASSES + 1]).then_inc(s_np, 1)
            dve.memset(rankp[:, PASSES * PAIRS], -1.0)
            for q in range(PASSES):
                if q:
                    pass_ranks(q)
                for t in range(TB):
                    last = dve.tensor_copy(wpair[:, q * PAIRS:(q + 1) * PAIRS, t, :],
                                           R[13][:, t].rearrange("p (i e) -> p i e", e=2))
            link(last)
            dve.wait_ge(s_h1, TB)
            for t in range(TB):
                last = dve.tensor_scalar(acc[:, t, :], work[:, t, :], ALPHA, None, ALU.mult)
            last.then_inc(m_acc, 1)

            def gathered():
                dve.tensor_copy(xg[:, KC // 2:KC, :].rearrange("p k s -> p (k s)"), bank[:, 3, :])\
                    .then_inc(m_xgd, 1)

            dve.wait_ge(m_xg, 1)
            gathered()
            dve.wait_ge(s_np, 1)
            npass = dve.value_load(npass_i[0:1, 0:1], min_val=1, max_val=PASSES)
            with dve.Fori(0, dve.snap(npass * PAIRS)) as it:
                dve.wait_ge(m_disp, it + 1)
                for t in range(TB):
                    w = wpair[:, bass.ds(it, 1), t, :].rearrange("p o e -> p (o e)")
                    last = dve.tensor_tensor(dispw[:, t], disp[:, t],
                                             w.unsqueeze(2).broadcast_to([P, 2, CAP]), ALU.mult)
                last.then_inc(m_dispw, 1)
                dve.wait_ge(m_dispw, it + 1)
                dve.wait_ge(m_xg, it + 1)
                dispatch(it + 1)
                dve.wait_ge(m_u, it + 1)
                dve.wait_ge(m_silu, it + 1)
                dve.tensor_tensor(hexp[:, :], silu_g[:, :], bank[:, 1, :], ALU.mult).then_inc(m_h, 1)
                dve.wait_ge(m_cT, it + 1)
                dve.tensor_copy(comb[:, :], bank[:, 7, 0:TB * P]).then_inc(m_cTo, 1)
                dve.wait_ge(m_hT, it + 1)
                dve.tensor_copy(hexT[:, :], bank[:, 4, :]).then_inc(m_hTo, 1)
                dve.wait_ge(m_y, it + 1)
                dve.tensor_copy(yexp[:, 0:HALF], bank[:, 5, :]).then_inc(m_yd, 1)
                dve.wait_ge(m_xg, it + 2)
                gathered()
                dve.wait_ge(m_acc, it * 4 + 1)
                for i in range(4):
                    t, half = divmod(i, 2)
                    dve.wait_ge(m_c, it * 4 + i + 1)
                    o = acc[:, t, half * HALF:(half + 1) * HALF]
                    dve.tensor_tensor(o, o, bank[:, 7 if i % 2 == 0 else 4, :], ALU.add).then_inc(m_acc, 1)
            dve.wait_ge(m_acc, dve.snap(npass * (4 * PAIRS) + 1))
            dve.wait_ge(s_lnp, 96)
            for t in range(TB):
                row_stats(t, acc[:, t, :], D)
                inverse_std(t)
                link(dve.scalar_tensor_tensor(out=work[:, t, :], in0=acc[:, t, :], scalar=mv[:, t, 0:1],
                                              in1=lnp[:, 0, :], op0=ALU.subtract, op1=ALU.mult))
                dve.scalar_tensor_tensor(out=work[:, t, :], in0=work[:, t, :], scalar=mv[:, t, 4:5],
                                         in1=lnp[:, 1, :], op0=ALU.mult, op1=ALU.add).then_inc(s_fin, 1)


_INS = ["x", "ln_in_g", "ln_in_b", "w_in", "b_forget", "b_gate", "pool_w", "pool_scale", "conv_dw", "conv_b",
        "conv_ln_g", "conv_ln_b", "w_branch", "w_out", "ln1_g", "ln1_b", "router_g", "router_g_b",
        "router_e", "router_e_b", "expert_w_gate", "expert_w_up", "expert_w_down", "ln2_g", "ln2_b"]


def kernel(**inputs):
    import numpy as _np
    import concourse.bacc as _bacc
    from concourse import mybir as _mybir
    from concourse.bass_utils import run_bass_kernel_spmd as _run

    nc = _bacc.Bacc("TRN2", target_bir_lowering=False, num_devices=1)
    arrays, aps = {}, {}
    for name in _INS:
        v = _np.ascontiguousarray(inputs[name])
        arrays[f"in_{name}_dram"] = v
        aps[name] = nc.dram_tensor(f"in_{name}_dram", v.shape, _mybir.dt.from_np(v.dtype),
                                   kind="ExternalInput").ap()
    shape = arrays["in_x_dram"].shape
    out = nc.dram_tensor("out_0_dram", shape, _mybir.dt.float32, kind="ExternalOutput").ap()
    hybrid_trunk_kernel(nc, aps, out)
    r = _run(nc, [arrays], core_ids=[0])
    return r.results[0]["out_0_dram"]
```

```python
import concourse.bass as bass
from concourse import mybir
from contextlib import ExitStack


def hybrid_trunk_kernel(nc: bass.Bass, a: dict, out: bass.AP):
    F32 = mybir.dt.float32
    I32 = mybir.dt.int32
    ALU = mybir.AluOpType
    ACT = mybir.ActivationFunctionType
    AX = mybir.AxisListType

    P = 128
    T, D = a["x"].shape[1], a["x"].shape[2]
    TB = T // P
    KC = D // P
    HALF = 512
    BW = D // 4
    DH = 64
    NH = BW // DH
    CONV_W = a["conv_dw"].shape[1]
    PADC = CONV_W - 1
    PADP = 16
    NB = 4
    NG = a["router_g"].shape[2]
    NE = a["router_e"].shape[2]
    EPG = NE // NG
    DFF = a["expert_w_gate"].shape[3]
    FC = DFF // P
    PAIRS = NE // 2
    BODY = 4
    CAP = 64
    PASSES = T // CAP
    TOPK = min(256, T // 4)
    ROUNDS = TOPK // 8
    NEG = -1e30
    TAKEN = -3e38
    EPS = 1e-5
    ALPHA = 2.0 ** 0.25
    SCALE = float(DH) ** -0.5
    SLOPES = [2.0 ** (-8.0 * (h + 1) / NH) for h in range(NH)]
    WINDOWS = (2, 4, 8, 16)

    sizes = dict(pool=BW, fq=BW, fk=BW, fv=BW, ff=NH, dq=BW, dk=DH, dv=DH, iq=BW, ik=DH, iw=NH,
                 conv=2 * BW, gate=NB * D)
    col, at = {}, 0
    for name, n in sizes.items():
        col[name] = at
        at += n

    x_v = a["x"][0].rearrange("(t p) d -> p t d", p=P)
    w_in = a["w_in"][0].rearrange("(k p) n -> p k n", p=P)
    w_br = a["w_branch"][0].rearrange("n (k p) d -> p (n k) d", p=P)
    w_out = a["w_out"][0].rearrange("(k p) d -> p k d", p=P)
    e_gate = a["expert_w_gate"][0].rearrange("e (k p) f -> p e k f", p=P)
    e_up = a["expert_w_up"][0].rearrange("e (k p) f -> p e k f", p=P)
    e_down = a["expert_w_down"][0].rearrange("e (k p) d -> p e k d", p=P)
    out_v = out[0].rearrange("(t p) d -> p t d", p=P)

    vec_src, ROW, at = [], {}, 0
    for name, src in (("ln_in_g", a["ln_in_g"].rearrange("(c p) -> c p", p=P)),
                      ("ln_in_b", a["ln_in_b"].rearrange("(c p) -> c p", p=P)),
                      ("conv_dw", a["conv_dw"][0].rearrange("w (c p) -> (w c) p", p=P)),
                      ("pool_scale", a["pool_scale"][0].rearrange("(c p) -> c p", p=P)),
                      ("conv_b", a["conv_b"][0].rearrange("(c p) -> c p", p=P)),
                      ("conv_ln_g", a["conv_ln_g"][0].rearrange("(c p) -> c p", p=P)),
                      ("conv_ln_b", a["conv_ln_b"][0].rearrange("(c p) -> c p", p=P)),
                      ("ln1_g", a["ln1_g"][0].rearrange("(c p) -> c p", p=P)),
                      ("ln1_b", a["ln1_b"][0].rearrange("(c p) -> c p", p=P))):
        ROW[name] = at
        vec_src.append((at, src))
        at += src.shape[0]
    NROW = at
    NIN = 2 * KC

    ctx = ExitStack()
    with ctx:
        def sb(name, shape, dt=F32):
            return ctx.enter_context(nc.sbuf_tensor(name, shape, dt))

        def sem(name):
            return ctx.enter_context(nc.semaphore(name))

        SLOTS = 6
        RING = 8
        with ExitStack() as rooms:
            rounded = [rooms.enter_context(nc.sbuf_tensor(f"rounded{i}", [P, KC * HALF], mybir.dt.float32r))
                       for i in range(RING + 3)]
        ring = sb("ring", [P, RING, KC * HALF])
        gates = sb("gates", [P, 2, KC * HALF])
        gflat = gates[:, :, :].rearrange("p a n -> p (a n)")
        xflat = ring[:, SLOTS:RING, :].rearrange("p a n -> p (a n)")
        place = {0: 0, 1: KC * HALF, 2: 0, 3: 0}

        def early(part, shape, rows=P):
            n = 1
            for d in shape:
                n *= d
            at = place[part]
            place[part] += n
            assert place[part] <= (1 if part == 0 else 2) * KC * HALF
            v = (xflat if part == 3 else gflat)[0:rows, at:at + n]
            if len(shape) == 2:
                v = v.rearrange("p (a b) -> p a b", b=shape[1])
            if len(shape) == 3:
                v = v.rearrange("p (a b c) -> p a b c", b=shape[1], c=shape[2])
            return v

        hT = sb("hT", [P, KC, T])
        lnp = sb("lnp", [P, 2, D])
        hn = sb("hn", [P, TB, D])
        work = sb("work", [P, TB, D])
        bgate = early(3, [2, HALF])
        vrows = early(0, [P], NROW)
        vcol = sb("vcol", [P, NROW])
        ident = sb("ident", [P, P])
        tri = sb("tri", [P, 3 * P])
        ln1p = sb("ln1p", [P, 2, D])
        lflat = ln1p[:, :, :].rearrange("p a n -> p (a n)")
        causal = lflat[:, 0:T]
        dist = lflat[:, T:2 * T]
        disti = early(0, [T]).bitcast(I32)
        rcnt = early(3, [2, T])
        slot_no = sb("slot_no", [P, CAP])
        desc4 = sb("desc4", [P, NG])
        bforget = sb("bforget", [P, NH])
        rbias = sb("rbias", [P, NG + NE])
        rw = sb("rw", [P, KC, NG + NE])
        poolw = sb("poolw", [P, 2, DH])
        iqT = early(0, [2, T])
        ikT = early(0, [T])
        dqT = early(3, [2, T])
        dkT = early(3, [T])
        fqT = early(0, [2, T])
        fkT = early(1, [2, T])
        fv = early(1, [TB, BW])
        misc = sb("misc", [P, TB, DH + 2 * NH])
        wflat = work[:, :, :].rearrange("p a n -> p (a n)")
        poolv, *pooled = [wflat[:, i * 2 * (PADP + T):(i + 1) * 2 * (PADP + T)]
                          .rearrange("p (c t) -> p c t", c=2) for i in range(3)]
        glu = early(3, [2, T])
        hpad = early(3, [2, PADC + T])
        convy = early(3, [2, T])
        brT = early(3, [NB, 2, T])
        fs = sb("fs", [P, 6, TB, NH])
        lsb = early(0, [TB, NH, P])
        cq = sb("cq", [P, TB, NH])
        fbias0 = early(1, [NH, P])
        fbias1 = early(1, [NH, T])
        rel = early(0, [NH, T])
        score = [sb(f"score{b}", [P, (b + 1) * P]) for b in range(TB)]
        top8 = sb("top8", [P, 8])
        logit = [lflat[:, 2 * T:D].rearrange("p (h k) -> p h k", h=NH), early(3, [NH, T])]
        alibi = lflat[:, D:2 * D].rearrange("p (h k) -> p h k", h=NH)
        probT = early(3, [2, NH * P])
        tmp = probT
        smx = sb("smx", [P, 2, TB, 3, NH])
        stats = sb("stats", [P, TB, 2, 6])
        mv = sb("mv", [P, TB, 6])
        lgT = early(2, [T])
        lg = early(2, [TB, NG + NE])
        xg = early(2, [KC, P])
        rt = early(2, [16, TB, NE])
        rq = early(2, [5, TB * (NG + NE)])
        rv = early(2, [3, TB * (NG + 1)])
        rankp = early(2, [PASSES * PAIRS + 1, TB, 2])
        wpair = early(2, [PASSES * PAIRS, TB, 2])
        disp = early(2, [TB, 2, CAP])
        dispw = early(2, [TB, 2, CAP])
        comb = early(2, [TB * P])
        silu_g = early(2, [DFF])
        hexp = early(2, [DFF])
        hexT = early(2, [FC * P])
        yexp = early(2, [D])
        npass_f = sb("npass_f", [P, 8])
        npass_i = sb("npass_i", [P, 1], I32)
        acc = hn

        bank = ctx.enter_context(nc.psum_tensor("bank", [P, 8, HALF], F32))

        def pair_bank(i):
            return bank[:, i:i + 2, :].rearrange("p a (j k) -> p (a j) k", j=2)

        s_x = [sem(f"x_loaded{t}") for t in range(TB)]
        s_vin = sem("ln_in_rows_loaded")
        s_vr = sem("other_vector_rows_loaded")
        s_bf = sem("forget_bias_loaded")
        s_small = sem("small_params_loaded")
        s_slot = [sem(f"slot{i}_loaded") for i in range(RING)]
        s_lnp = sem("ln_params_loaded")
        s_bg = [sem(f"bgate{i}_loaded") for i in range(2)]
        s_brlo = sem("branch_split")
        s_wbhi = sem("w_branch_second_half_quarter_rounded")
        s_wblo = [sem(f"w_branch{i}_quarter_rest_rounded") for i in range(2)]
        s_wohi = sem("w_out_quarter_rounded")
        s_wolo = sem("w_out_quarter_rest_rounded")
        s_mTlo = sem("merged_turned_rest_rounded")
        s_const = sem("constants_built")
        s_ppad = sem("pool_rows_padded")
        s_idf = sem("identity_built")
        s_vT = sem("vector_rows_turned")
        s_vcol = sem("vector_columns_ready")
        s_var = sem("row_variance_ready")
        s_std = sem("row_std_ready")
        s_z = sem("x_normalised")
        s_xT = sem("x_turned")
        s_hTa = sem("hT_by_scalar")
        s_hTd = sem("hT_by_vector")
        s_hn = sem("hn_ready")
        UNITS = ["iq", "ikdk", "misc", "dq", "fq", "fk", "fv", "pool", "convb", "conva"]
        s_unit = sem("unit_projected")
        s_uout = {u: sem(f"{u}_out_of_psum") for u in UNITS}
        s_gate = sem("gate_projected")
        s_hThi = sem("hT_rounded")
        s_hTlo = sem("hT_rest_rounded")
        s_hi = sem("gate_quarter_rounded")
        s_lo = [sem("even_gate_quarter_rest_rounded"), sem("odd_gate_quarter_rest_rounded")]
        s_whi = {u: sem(f"{u}_weights_quarter_rounded") for u in ("s_fox", "s_val", "s_conv")}
        s_wlo = {u: sem(f"{u}_weights_quarter_rest_rounded") for u in ("s_fox", "s_val", "s_conv")}
        s_gout = sem("gate_out_of_psum")
        s_gbias = sem("gate_biased")
        s_gsig = sem("gate_sigmoid_done")
        s_idx = sem("indexer_scores_in_psum")
        s_rel = sem("indexer_relu_done")
        s_relu_used = sem("indexer_relu_used")
        s_sel = sem("selection_done")
        s_ls = sem("log_sigmoid_steps")
        s_lsa = sem("log_sigmoid_by_scalar")
        s_lsb = sem("log_sigmoid_spread")
        s_cum = sem("cumulated_in_psum")
        s_cumo = sem("cumulated_out_of_psum")
        s_s = sem("attention_scores_in_psum")
        s_lg = sem("logits_ready")
        s_exp = sem("exponentials_done")
        s_prob = sem("probabilities_ready")
        s_pT = sem("probabilities_turned")
        s_pTo = sem("turned_probabilities_out")
        s_pv = sem("values_weighted")
        s_att = sem("attention_branch_ready")
        s_poolin = sem("pool_means_ready")
        s_poolmm = sem("pool_mixed")
        s_poolo = sem("pool_branch_ready")
        s_glu = sem("glu_padded")
        s_conv = sem("convolution_done")
        s_cT = sem("convolution_turned")
        s_cz = sem("convolution_normalised")
        s_czT = sem("convolution_turned_back")
        s_cbr = sem("convolution_branch_ready")
        s_up = sem("branch_projected")
        s_mix = sem("branch_merged")
        s_mT = sem("merged_turned")
        s_mTo = sem("merged_turned_out")
        s_o = sem("output_projected")
        s_y1 = sem("residual_added")
        s_z1 = sem("layer1_normalised")
        s_zT = sem("layer1_turned")
        s_h1Ta = sem("layer1_turned_by_scalar")
        s_h1Td = sem("layer1_turned_by_vector")
        s_h1 = sem("layer1_output_ready")
        s_rtT = sem("router_logits_by_channel_in_psum")
        s_rtTo = sem("router_logits_by_channel_out")
        s_rt = sem("router_logits_in_psum")
        s_re = sem("router_exp_argument")
        s_rex = sem("router_exp_done")
        s_mask = sem("expert_mask_ready")
        s_rank = sem("ranks_in_psum")
        s_tot = sem("expert_totals_in_psum")
        s_tab = sem("tables_ready")
        s_np = sem("passes_known")
        m_disp = sem("dispatch_ready")
        m_dispw = sem("weighted_dispatch_ready")
        m_xg = sem("tokens_gathered")
        m_xga = sem("gathered_out_by_scalar")
        m_xgd = sem("gathered_out_by_vector")
        m_xg0 = sem("tokens_gathered_first_chunks")
        m_g0 = sem("expert_gate_first_chunks_used")
        m_g = sem("expert_gate_in_psum")
        m_u0 = sem("expert_up_first_chunks_used")
        m_u = sem("expert_up_in_psum")
        m_silu = sem("expert_silu_done")
        m_h = sem("expert_hidden_ready")
        m_hT = sem("expert_hidden_turned")
        m_hTo = sem("expert_hidden_turned_out")
        m_cT = sem("combine_turned")
        m_cTo = sem("combine_turned_out")
        m_y0 = sem("expert_output_first_half_in_psum")
        m_y = sem("expert_output_in_psum")
        m_ya = sem("expert_output_out_by_scalar")
        m_yd = sem("expert_output_out_by_vector")
        m_c = sem("combined_in_psum")
        m_acc = sem("residual_sum_begun_or_added_to")
        m_stat = sem("first_half_statistics_or_residual_begun")
        s_dch = sem("vector_chain")
        s_pch = sem("gpsimd_chain")
        s_ach = sem("scalar_chain")
        s_shift = sem("last_mean_over_std_ready")
        s_zlast = sem("last_half_block_normalised")
        s_fin = sem("output_rows_ready")
        s_fin2 = sem("last_half_block_ready")
        s_out = sem("output_stored")

        block = ctx.enter_context(nc.Block())

        FRONT = {"s_idx": (0, 2), "s_dsa": (1, 4), "s_fox": (2, 1), "s_val": (3, 2), "s_conv": (4, 1),
                 "g0": (2, 1), "g1": (3, 1), "g2": (4, 1), "g3": (2, 1), "g4": (3, 1), "g5": (4, 1),
                 "g6": (2, 1), "g7": (3, 1), "wb0": (4, 1), "wb1": (2, 1), "wo0": (3, 1), "wo1": (0, 1)}
        SLOT = {name: s for name, (s, _) in FRONT.items()}
        FIRST = [0] * RING
        LOADED, BEFORE, last_in = {}, {}, {}
        for name, (s, transfers) in FRONT.items():
            FIRST[s] += 16 * transfers
            LOADED[name] = FIRST[s]
            BEFORE[name] = last_in.get(s)
            last_in[s] = name

        def slot(name, cols=HALF):
            return ring[:, SLOT[name], 0:KC * cols].rearrange("p (k n) -> p k n", n=cols)

        def loaded(eng, name):
            eng.wait_ge(s_slot[SLOT[name]], LOADED[name])

        def rounded_slot(s):
            return rounded[s][:, :].rearrange("p (k n) -> p k n", n=HALF)

        hT_part = [rounded[0][:, i * KC * T:(i + 1) * KC * T].rearrange("p (k t) -> p k t", t=T)
                   for i in range(2)]
        WB_PART = [(1, SLOT["wb0"]), (5, SLOT["wb1"])]
        br_part = [rounded[RING + 2][:, i * KC * T:(i + 1) * KC * T].rearrange("p (n c t) -> p n c t", n=NB, c=2)
                   for i in range(2)]
        WO_PART = [(1, SLOT["wo0"]), (5, SLOT["wo1"])]
        merged_part = [rounded[RING][:, i * KC * T:(i + 1) * KC * T].rearrange("p (k t) -> p k t", t=T)
                       for i in range(2)]
        QUARTER = KC * HALF // 4

        def tile_part(t, i):
            return 1 + 4 * (t % 2) if i == 0 else SLOT[f"g{t}"]

        ROUNDED_AT = {"s_fox": 5, "s_val": 1, "s_conv": 5}

        IDXC, DSAC = BW + 2 * DH, BW + DH + 2 * NH

        USED = {"s_idx": (s_unit, 2), "s_dsa": (s_unit, 4), "s_fox": (s_unit, 6), "s_val": (s_unit, 8),
                "s_conv": (s_unit, 10)}
        USED.update({f"g{t}": (s_gate, 2 * t + 2) for t in range(8)})
        USED.update({f"wb{q}": (s_up, 8 * q + 8) for q in range(2)})

        def slot_free(eng, name):
            if BEFORE[name]:
                eng.wait_ge(*USED[BEFORE[name]])

        def expert_slot(s):
            return ring[:, s, :].rearrange("p (e k n) -> p e k n", e=2, n=HALF)

        def expert_part(pair, part):
            e, h = slice(2 * pair, 2 * pair + 2), part % 2
            if part < 4:
                return (e_gate, e_up)[part // 2][:, e, h * FC:(h + 1) * FC, :]
            return e_down[:, e, :, h * HALF:(h + 1) * HALF]

        PART_USED = (m_g0, m_g, m_u0, m_u, m_y0, m_y)

        def load_part(eng, s, pair, part):
            src = expert_part(pair, part)
            for e in range(2):
                eng.dma_start(expert_slot(s)[:, e], src[:, e]).then_inc(s_slot[s], 8 * 2)

        @block.sync
        def _(sp):
            for t in range(TB):
                sp.dma_start(work[:, t, :], x_v[:, t, :]).then_inc(s_x[t], 16)
            d = slot("s_idx", IDXC)
            n = BW + DH
            sp.dma_start(d[:, :, 0:n], w_in[:, :, col["iq"]:col["iq"] + n]).then_inc(s_slot[0], 16)
            sp.dma_start(d[:, :, n:n + DH], w_in[:, :, col["dk"]:col["dk"] + DH]).then_inc(s_slot[0], 16)
            d = slot("s_dsa", DSAC)
            at = 0
            for name in ("dq", "dv", "iw", "ff"):
                n = sizes[name]
                sp.dma_start(d[:, :, at:at + n], w_in[:, :, col[name]:col[name] + n]).then_inc(s_slot[1], 16)
                at += n
            sp.dma_start(slot("s_fox"), w_in[:, :, col["fq"]:col["fq"] + 2 * BW]).then_inc(s_slot[2], 16)
            v = slot("s_val")
            sp.dma_start(v[:, :, 0:BW], w_in[:, :, col["pool"]:col["pool"] + BW]).then_inc(s_slot[3], 16)
            sp.dma_start(v[:, :, BW:2 * BW], w_in[:, :, col["fv"]:col["fv"] + BW]).then_inc(s_slot[3], 16)
            sp.dma_start(slot("s_conv"), w_in[:, :, col["conv"]:col["conv"] + 2 * BW])\
                .then_inc(s_slot[4], 16)
            def load_bgate(t):
                dq, n = divmod(t, NB)
                if t >= 2:
                    sp.wait_ge(s_gbias, t - 1)
                c = n * D + dq * HALF
                sp.dma_start(bgate[:, t % 2, :],
                             a["b_gate"][0][c:c + HALF].partition_broadcast(P)).then_inc(s_bg[t % 2], 16)

            for t in range(8):
                dq, n = divmod(t, NB)
                slot_free(sp, f"g{t}")
                c = col["gate"] + n * D + dq * HALF
                sp.dma_start(slot(f"g{t}"), w_in[:, :, c:c + HALF]).then_inc(s_slot[SLOT[f"g{t}"]], 16)
                if t:
                    load_bgate(t - 1)
            load_bgate(7)
            for dq in range(2):
                slot_free(sp, f"wb{dq}")
                sp.dma_start(slot(f"wb{dq}"), w_br[:, :, dq * HALF:(dq + 1) * HALF])\
                    .then_inc(s_slot[SLOT[f"wb{dq}"]], 16)

            for j in range(2):
                slot_free(sp, f"wo{j}")
                sp.dma_start(slot(f"wo{j}"), w_out[:, :, j * HALF:(j + 1) * HALF])\
                    .then_inc(s_slot[SLOT[f"wo{j}"]], 16)
            for name in ("wb0", "wb1"):
                sp.wait_ge(*USED[name])
                load_part(sp, SLOT[name], 0, SLOT[name])
            sp.wait_ge(s_mix, 4 * NB)
            for e in range(RING - SLOTS):
                load_part(sp, SLOTS + e, 1, e)
            sp.wait_ge(s_o, 2)
            for e in (1, 3):
                load_part(sp, e, 0, e)
            sp.wait_ge(s_o, 4)
            for e in (0, 5):
                load_part(sp, e, 0, e)

            def load_pairs(body, half, first):
                for n in range(first, BODY * 6):
                    pair, part = divmod(n, 6)
                    before, bpart = divmod(n - RING + BODY * 6, 6)
                    sp.wait_ge(PART_USED[bpart], body * BODY + before - BODY + 1)
                    load_part(sp, n % RING, half * BODY + pair, part)

            load_pairs(0, 0, RING)
            load_pairs(1, 1, 0)
            sp.wait_ge(s_np, 1)
            npass = sp.value_load(npass_i[0:1, 0:1], min_val=1, max_val=PASSES)
            with sp.If(npass > 1):
                with sp.Fori(1, npass) as again:
                    for half in range(2):
                        load_pairs(sp.snap(again * 2 + half), half, 0)
            sp.wait_ge(s_h1, TB)
            sp.dma_start(lnp[:, 0, :], a["ln2_g"][0].partition_broadcast(P)).then_inc(s_lnp, 16)
            sp.dma_start(lnp[:, 1, :], a["ln2_b"][0].partition_broadcast(P)).then_inc(s_lnp, 16)
            sp.wait_ge(s_fin, 1)
            sp.dma_start(out_v[:, 0, :], work[:, 0, :]).then_inc(s_out, 16)
            sp.wait_ge(s_fin, 2)
            sp.dma_start(out_v[:, 1, 0:HALF], work[:, 1, 0:HALF]).then_inc(s_out, 16)
            sp.wait_ge(s_fin2, 1)
            sp.dma_start(out_v[:, 1, HALF:D], work[:, 1, HALF:D]).then_inc(s_out, 16)
            sp.wait_ge(s_out, 16 * 3)

        @block.gpsimd
        def _(pool):
            n = [0]

            def link(ins):
                n[0] += 1
                ins.then_inc(s_pch, 1)
                pool.wait_ge(s_pch, n[0])

            link(pool.memset(ident[:, :], 0.0))
            pool.affine_select(out=ident[:, :], in_=ident[:, :], compare_op=ALU.not_equal, fill=1.0, base=0,
                               pattern=[[-1, P]], channel_multiplier=1).then_inc(s_idf, 1)
            for r, src in vec_src[2:]:
                pool.dma_start(vrows[r:r + src.shape[0], :], src).then_inc(s_vr, 16)
            link(pool.memset(causal[:, :], 0.0))
            link(pool.affine_select(out=causal[:, :], in_=causal[:, :], compare_op=ALU.is_ge, fill=NEG,
                                    base=P, pattern=[[-1, T]], channel_multiplier=1))
            link(pool.iota(disti[:, :], [[-1, T]], base=P, channel_multiplier=1))
            link(pool.tensor_copy(dist[:, :], disti[:, :]))
            link(pool.memset(tri[:, :], 1.0))
            link(pool.affine_select(out=tri[:, :], in_=tri[:, :], compare_op=ALU.is_ge, fill=0.0,
                                    base=-P, pattern=[[1, 3 * P]], channel_multiplier=-1))
            link(pool.iota(disti[:, :], [[1, T]], base=1, channel_multiplier=0))
            for g, w in enumerate(WINDOWS):
                r = slice(DH * (g % 2), DH * (g % 2) + DH)
                link(pool.tensor_scalar(rcnt[r, g // 2, :], disti[r, :], float(w), None, ALU.min))
            link(pool.iota(disti[:, 0:CAP], [[1, CAP]], base=0, channel_multiplier=0))
            link(pool.tensor_copy(slot_no[:, :], disti[:, 0:CAP]))
            link(pool.iota(disti[:, 0:NG], [[-1, NG]], base=NG, channel_multiplier=0))
            link(pool.tensor_copy(desc4[:, :], disti[:, 0:NG]))
            pool.memset(hpad[:, :, 0:PADC], 0.0).then_inc(s_const, 1)

            def affine(t, dst, lnp, done):
                link(pool.tensor_tensor(dst[:, t, :], work[:, t, :], lnp[:, 0, :], ALU.mult))
                pool.tensor_tensor(dst[:, t, :], dst[:, t, :], lnp[:, 1, :], ALU.add).then_inc(done, 1)

            pw = a["pool_w"][0]
            for g in range(4):
                pool.dma_start(poolw[DH * (g % 2):DH * (g % 2) + DH, g // 2, :], pw[g]).then_inc(s_small, 16)
            pool.dma_start(rbias[:, 0:NG], a["router_g_b"][0].partition_broadcast(P)).then_inc(s_small, 16)
            pool.dma_start(rbias[:, NG:NG + NE], a["router_e_b"][0].partition_broadcast(P)).then_inc(s_small, 16)
            pool.dma_start(rw[:, :, 0:NG], a["router_g"][0].rearrange("(k p) n -> p k n", p=P)).then_inc(s_small, 16)
            pool.dma_start(rw[:, :, NG:NG + NE], a["router_e"][0].rearrange("(k p) n -> p k n", p=P))\
                .then_inc(s_small, 16)

            pool.wait_ge(s_lnp, 32)
            for t in range(TB):
                pool.wait_ge(s_z, t + 1)
                affine(t, hn, lnp, s_hn)
            pool.wait_ge(s_xT, TB)
            pool.wait_ge(s_hn, TB)
            pool.memset(poolv[:, :, 0:PADP], 0.0)
            pool.memset(pooled[0][:, :, 0:PADP], 0.0)
            pool.memset(pooled[1][:, :, 0:PADP], 0.0).then_inc(s_ppad, 1)
            for name in ("s_val", "s_conv"):
                for q in range(4):
                    c = slice(q * QUARTER, (q + 1) * QUARTER)
                    pool.wait_ge(s_whi[name], q + 1)
                    pool.tensor_tensor(rounded[SLOT[name]][:, c], ring[:, SLOT[name], c],
                                       rounded[ROUNDED_AT[name]][:, c], ALU.subtract).then_inc(s_wlo[name], 1)

            def tile_rest(t):
                for q in range(4):
                    c = slice(q * QUARTER, (q + 1) * QUARTER)
                    pool.wait_ge(s_hi, 4 * t + q + 1)
                    pool.tensor_tensor(rounded[SLOT[f"g{t}"]][:, c], ring[:, SLOT[f"g{t}"], c],
                                       rounded[tile_part(t, 0)][:, c], ALU.subtract).then_inc(s_lo[1], 1)

            def gate_bias(t):
                dq, nb = divmod(t, NB)
                pool.wait_ge(s_bg[t % 2], 16 * (t // 2 + 1))
                pool.wait_ge(s_gout, 2 * (t + 1))
                g = gates[:, dq, :].rearrange("p (t n c) -> p t n c", t=TB, n=NB)[:, :, nb, :]
                pool.tensor_tensor(g, g, bgate[:, t % 2, :].unsqueeze(1).broadcast_to([P, TB, HALF]),
                                   ALU.add).then_inc(s_gbias, 1)

            for t in range(0, 8, 2):
                tile_rest(t + 1)
                gate_bias(t)
                gate_bias(t + 1)
            for q in range(4):
                c = slice(q * QUARTER, (q + 1) * QUARTER)
                pool.wait_ge(s_wbhi, q + 1)
                pool.tensor_tensor(rounded[SLOT["wb1"]][:, c], ring[:, SLOT["wb1"], c],
                                   rounded[WB_PART[1][0]][:, c], ALU.subtract).then_inc(s_wblo[1], 1)
            for j in range(2):
                for q in range(4):
                    c = slice(q * QUARTER, (q + 1) * QUARTER)
                    pool.wait_ge(s_wohi, 4 * j + q + 1)
                    pool.tensor_tensor(rounded[SLOT[f"wo{j}"]][:, c], ring[:, SLOT[f"wo{j}"], c],
                                       rounded[WO_PART[j][0]][:, c], ALU.subtract).then_inc(s_wolo, 1)
            pool.wait_ge(s_lnp, 64)
            for t in range(TB):
                pool.wait_ge(s_zT, t + 1)
                affine(t, work, ln1p, s_h1)
            pool.wait_ge(s_lnp, 96)
            pool.wait_ge(s_zlast, 1)
            o = work[:, 1, HALF:D]
            link(pool.tensor_tensor(o, o, lnp[:, 0, HALF:D], ALU.mult))
            pool.tensor_tensor(o, o, lnp[:, 1, HALF:D], ALU.add).then_inc(s_fin2, 1)

        @block.scalar
        def _(act):
            nln = [0]

            def root(t):
                nln[0] += 1
                act.wait_ge(s_var, nln[0])
                act.activation(mv[:, t, 3:4], mv[:, t, 2:3], ACT.Sqrt).then_inc(s_std, 1)

            def turned_rows(t, turned, bk, gain, bias, done, k0=0):
                act.wait_ge(turned, t + 1)
                for k in range(k0, k0 + KC // 2):
                    c = k - k0
                    last = act.activation(hT[:, k, t * P:(t + 1) * P],
                                          bank[:, bk + 2 * t + k0 // (KC // 2), c * P:(c + 1) * P],
                                          ACT.Identity, bias=vcol[:, ROW[bias] + k:ROW[bias] + k + 1],
                                          scale=vcol[:, ROW[gain] + k:ROW[gain] + k + 1])
                last.then_inc(done, 1)

            for r, src in vec_src[:2]:
                act.dma_start(vrows[r:r + src.shape[0], :], src).then_inc(s_vin, 16)
            act.dma_start(bforget[:, :], a["b_forget"][0].partition_broadcast(P)).then_inc(s_bf, 16)
            act.dma_start(lnp[:, 0, :], a["ln_in_g"].partition_broadcast(P)).then_inc(s_lnp, 16)
            act.dma_start(lnp[:, 1, :], a["ln_in_b"].partition_broadcast(P)).then_inc(s_lnp, 16)
            root(0)
            root(1)
            act.wait_ge(s_vcol, 1)
            for t in range(TB):
                turned_rows(t, s_xT, 0, "ln_in_g", "ln_in_b", s_hTa)
            unit_bank = {u: 2 + i % 2 for i, u in enumerate(UNITS)}

            def unit(name):
                act.wait_ge(s_unit, UNITS.index(name) + 1)
                return bank[:, unit_bank[name], :].rearrange("p (c t) -> p c t", c=2)

            def relu(b):
                act.wait_ge(s_idx, b + 1)
                if b:
                    act.wait_ge(s_relu_used, b)
                n = (b + 1) * P
                act.activation(rel[:, :, 0:n], pair_bank(4)[:, :, 0:n], ACT.Relu).then_inc(s_rel, 1)

            u = unit("iq")
            act.activation(iqT[:, :, :], u, ACT.Copy).then_inc(s_uout["iq"], 1)
            u = unit("ikdk")
            for src, dst in ((slice(0, DH), ikT), (slice(DH, P), dkT)):
                for half in (slice(0, DH), slice(DH, P)):
                    last = act.activation(dst[half, :], u[src, 0, :], ACT.Copy)
            last.then_inc(s_uout["ikdk"], 1)
            act.wait_ge(s_unit, 2)
            act.wait_ge(s_hTd, TB)
            act.activation(hT_part[0], hT[:, :, :], ACT.Copy).then_inc(s_hThi, 1)

            def unit_rounded(name, used=None):
                if used:
                    act.wait_ge(s_unit, used)
                loaded(act, name)
                for q in range(4):
                    c = slice(q * QUARTER, (q + 1) * QUARTER)
                    act.activation(rounded[ROUNDED_AT[name]][:, c], ring[:, SLOT[name], c], ACT.Copy)\
                        .then_inc(s_whi[name], 1)

            unit_rounded("s_fox")
            u = unit("misc")
            act.activation(misc[:, :, :], u[:, :, 0:DH + 2 * NH], ACT.Copy).then_inc(s_uout["misc"], 1)
            relu(0)
            act.wait_ge(s_ls, 1)
            act.activation(fs[:, 2], fs[:, 1], ACT.Exp, scale=-1.0).then_inc(s_lsa, 1)
            u = unit("dq")
            act.activation(dqT[:, :, :], u, ACT.Copy, scale=SCALE).then_inc(s_uout["dq"], 1)
            act.wait_ge(s_ls, 2)
            act.activation(fs[:, 4], fs[:, 3], ACT.Ln).then_inc(s_lsa, 1)
            relu(1)
            unit_rounded("s_val", 4)

            def tile_rounded(t):
                if t < 2:
                    act.wait_ge(s_unit, (8, 10)[t])
                else:
                    act.wait_ge(s_gate, 2 * (t - 1))
                loaded(act, f"g{t}")
                for q in range(4):
                    c = slice(q * QUARTER, (q + 1) * QUARTER)
                    act.activation(rounded[tile_part(t, 0)][:, c], ring[:, SLOT[f"g{t}"], c], ACT.Copy)\
                        .then_inc(s_hi, 1)

            u = unit("fq")
            act.activation(fqT[:, :, :], u, ACT.Copy, scale=SCALE).then_inc(s_uout["fq"], 1)
            u = unit("fk")
            act.activation(fkT[:, :, :], u, ACT.Copy).then_inc(s_uout["fk"], 1)
            unit_rounded("s_conv", 6)
            u = unit("fv")
            act.activation(fv[:, :, :], u, ACT.Copy).then_inc(s_uout["fv"], 1)

            def exps(i):
                b = i % TB
                n = (b + 1) * P
                act.wait_ge(s_lg, i + 1)
                for hh in range(NH):
                    last = act.activation(logit[b][:, hh, 0:n], logit[b][:, hh, 0:n], ACT.Exp,
                                          bias=smx[:, i // TB, b, 0, hh:hh + 1],
                                          accum_out=smx[:, i // TB, b, 1, hh:hh + 1])
                last.then_inc(s_exp, 1)

            nturn = [0]

            def turned(kc):
                i = nturn[0]
                nturn[0] += 1
                act.wait_ge(s_pT, i + 1)
                need = {1: 1, 2: 1, 3: 2, 4: 3, 5: 3}.get(i)
                if need:
                    act.wait_ge(s_pv, need)
                act.activation(probT[:, kc, :], bank[:, 6, :], ACT.Copy).then_inc(s_pTo, 1)

            def branch(i):
                act.wait_ge(s_pv, 2 * (i + 1))
                act.activation(brT[:, 1 + i], bank[:, 7, :].rearrange("p (j t) -> p j t", j=2),
                               ACT.Copy).then_inc(s_att, 1)

            def gate_out(t, b):
                act.wait_ge(s_gate, 2 * t + b + 1)
                dq, nb = divmod(t, NB)
                g = gates[:, dq, :].rearrange("p (t n c) -> p t n c", t=TB, n=NB)
                act.activation(g[:, b, nb, :], bank[:, b, :], ACT.Copy).then_inc(s_gout, 1)

            exps(0)
            act.wait_ge(s_ppad, 1)
            u = unit("pool")
            act.activation(poolv[:, :, PADP:PADP + T], u, ACT.Copy).then_inc(s_uout["pool"], 1)
            tile_rounded(0)
            exps(1)
            u = unit("convb")
            act.activation(glu[:, :, :], u, ACT.Sigmoid).then_inc(s_uout["convb"], 1)
            tile_rounded(1)
            gate_out(0, 0)
            gate_out(0, 1)
            turned(0)
            tile_rounded(2)
            gate_out(1, 0)
            turned(0)
            gate_out(1, 1)
            turned(1)
            tile_rounded(3)
            gate_out(2, 0)
            branch(0)
            exps(2)
            gate_out(2, 1)
            tile_rounded(4)
            gate_out(3, 0)
            turned(0)
            gate_out(3, 1)
            exps(3)
            tile_rounded(5)
            gate_out(4, 0)
            gate_out(4, 1)
            turned(0)
            tile_rounded(6)
            gate_out(5, 0)
            turned(1)
            gate_out(5, 1)
            branch(1)
            act.wait_ge(s_poolmm, 1)
            for q in range(2):
                r = slice(DH * q, DH * q + DH)
                for j in range(2):
                    c = ROW["pool_scale"] + j
                    last = act.activation(brT[r, 0, j, :], bank[r, 2 + q, j * T:(j + 1) * T],
                                          ACT.Copy, scale=vcol[r, c:c + 1])
            last.then_inc(s_poolo, 1)
            tile_rounded(7)
            gate_out(6, 0)
            gate_out(6, 1)
            root(0)
            root(1)

            def sig(t):
                dq, nb = divmod(t, NB)
                act.wait_ge(s_gbias, t + 1)
                g = gates[:, dq, :].rearrange("p (t n c) -> p t n c", t=TB, n=NB)[:, :, nb, :]
                act.activation(g, g, ACT.Sigmoid).then_inc(s_gsig, 1)

            for t in range(3):
                sig(t)
            gate_out(7, 0)
            act.wait_ge(s_lg, 2 * TB)
            act.wait_ge(s_pT, 3 * TB)
            act.dma_start(ln1p[:, 0, :], a["ln1_g"][0].partition_broadcast(P)).then_inc(s_lnp, 16)
            act.dma_start(ln1p[:, 1, :], a["ln1_b"][0].partition_broadcast(P)).then_inc(s_lnp, 16)
            act.wait_ge(s_czT, 1)
            for c in range(2):
                last = act.activation(brT[:, 3, c, :], bank[:, 7, c * T:(c + 1) * T], ACT.Silu,
                                      bias=vcol[:, ROW["conv_ln_b"] + c:ROW["conv_ln_b"] + c + 1],
                                      scale=vcol[:, ROW["conv_ln_g"] + c:ROW["conv_ln_g"] + c + 1])
            last.then_inc(s_cbr, 1)
            sig(3)
            gate_out(7, 1)
            loaded(act, "wb1")
            for q in range(4):
                c = slice(q * QUARTER, (q + 1) * QUARTER)
                act.activation(rounded[WB_PART[1][0]][:, c], ring[:, SLOT["wb1"], c], ACT.Copy)\
                    .then_inc(s_wbhi, 1)
            for t in range(4, 8):
                sig(t)

            def merged_rounded(i):
                act.wait_ge(s_mT, i + 1)
                act.activation(merged_part[0][:, 2 * i:2 * i + 2, :],
                               bank[:, 4 + i % 2, :].rearrange("p (c t) -> p c t", c=2), ACT.Copy)\
                    .then_inc(s_mTo, 1)

            def w_out_rounded(j, quarters):
                loaded(act, f"wo{j}")
                for q in quarters:
                    c = slice(q * QUARTER, (q + 1) * QUARTER)
                    act.activation(rounded[WO_PART[j][0]][:, c], ring[:, SLOT[f"wo{j}"], c], ACT.Copy)\
                        .then_inc(s_wohi, 1)

            act.wait_ge(s_up, 2 * NB)
            w_out_rounded(0, range(4))
            merged_rounded(0)
            merged_rounded(1)
            act.wait_ge(s_up, 4 * NB)
            w_out_rounded(1, range(0, 2))
            merged_rounded(2)
            w_out_rounded(1, range(2, 4))
            merged_rounded(3)
            root(0)
            turned_rows(0, s_zT, 4, "ln1_g", "ln1_b", s_h1Ta)
            root(1)
            turned_rows(0, s_zT, 4, "ln1_g", "ln1_b", s_h1Ta, KC // 2)
            turned_rows(1, s_zT, 4, "ln1_g", "ln1_b", s_h1Ta)
            act.wait_ge(s_re, 1)
            act.activation(rt[:, 8, :, 0:2 * NG + 1], rt[:, 7, :, 0:2 * NG + 1], ACT.Exp).then_inc(s_rex, 1)
            act.wait_ge(s_np, 1)
            npass = act.value_load(npass_i[0:1, 0:1], min_val=1, max_val=PASSES)
            act.wait_ge(m_xg0, 1)
            act.activation(xg[:, 0:KC // 2, :].rearrange("p k s -> p (k s)"), bank[:, 2, :], ACT.Copy)\
                .then_inc(m_xga, 1)
            with act.Fori(0, act.snap(npass * PAIRS)) as it:
                act.wait_ge(m_g, it + 1)
                act.activation(silu_g[:, :], bank[:, 0, :], ACT.Silu).then_inc(m_silu, 1)
                act.wait_ge(m_xg0, it + 2)
                act.activation(xg[:, 0:KC // 2, :].rearrange("p k s -> p (k s)"), bank[:, 2, :], ACT.Copy)\
                    .then_inc(m_xga, 1)
                act.wait_ge(m_y, it + 1)
                act.activation(yexp[:, HALF:D], bank[:, 6, :], ACT.Copy).then_inc(m_ya, 1)
            root(0)
            root(1)
            act.wait_ge(s_shift, 1)
            act.activation(work[:, 1, HALF:D], acc[:, 1, HALF:D], ACT.Identity, bias=mv[:, 1, 5:6],
                           scale=mv[:, 1, 4:5]).then_inc(s_zlast, 1)

        @block.tensor
        def _(pe):
            def stay_warm(bk, n):
                for _ in range(n):
                    pe.transpose(bank[:, bk, 0:P], ident[:, :], ident[:, :])

            pe.wait_ge(s_idf, 1)
            stay_warm(7, 22)
            pe.wait_ge(s_vin, 32)
            pe.transpose(bank[:, 4, 0:NIN], vrows[0:NIN, :], ident[0:NIN, 0:NIN]).then_inc(s_vT, 1)

            def turn_rows(ready, bk, done):
                for t in range(TB):
                    pe.wait_ge(ready, t + 1)
                    for k in range(KC):
                        c = k % (KC // 2)
                        last = pe.transpose(bank[:, bk + 2 * t + k // (KC // 2), c * P:(c + 1) * P],
                                            work[:, t, k * P:(k + 1) * P], ident[:, :])
                    last.then_inc(done, 1)

            stay_warm(7, 18)
            turn_rows(s_z, 0, s_xT)

            nunit = [0]

            def start_unit():
                i = nunit[0]
                if i >= 2:
                    pe.wait_ge(s_uout[UNITS[i - 2]], 1)
                nunit[0] += 1
                return bank[:, 2 + i % 2, :].rearrange("p (c t) -> p c t", c=2)

            def by_channel(w, c0, width):
                o = start_unit()
                m = min(P, width)
                for c in range((width + P - 1) // P):
                    for k in range(KC):
                        last = pe.matmul(o[0:m, c, :], w[:, k, c0 + c * P:c0 + c * P + m], hT[:, k, :],
                                         start=(k == 0), stop=(k == KC - 1))
                last.then_inc(s_unit, 1)

            def by_token(w, c0, width):
                o = start_unit()
                for t in range(TB):
                    for k in range(KC):
                        last = pe.matmul(o[:, t, 0:width], hT[:, k, t * P:(t + 1) * P],
                                         w[:, k, c0:c0 + width], start=(k == 0), stop=(k == KC - 1))
                last.then_inc(s_unit, 1)

            PRODUCTS = ((0, 0), (0, 1), (1, 0))

            def weight_parts(name):
                return [rounded_slot(ROUNDED_AT[name]), rounded_slot(SLOT[name])]

            def by_channel_parts(w, c0, rest=None):
                o = start_unit()
                for c in range(BW // P):
                    for k in range(KC):
                        if rest and c == 0 and k % 2 == 0:
                            pe.wait_ge(rest, k // 2 + 1)
                        for hpart, wpart in PRODUCTS:
                            last = pe.matmul(o[:, c, :], w[wpart][:, k, c0 + c * P:c0 + (c + 1) * P],
                                             hT_part[hpart][:, k, :], start=(k == 0 and hpart == wpart),
                                             stop=(k == KC - 1 and hpart == 1))
                last.then_inc(s_unit, 1)

            def by_token_parts(w, c0, rest):
                o = start_unit()
                for t in range(TB):
                    for k in range(KC):
                        if t == 0 and k % 2 == 0:
                            pe.wait_ge(rest, k // 2 + 1)
                        for hpart, wpart in PRODUCTS:
                            last = pe.matmul(o[:, t, :], hT_part[hpart][:, k, t * P:(t + 1) * P],
                                             w[wpart][:, k, c0:c0 + BW], start=(k == 0 and hpart == wpart),
                                             stop=(k == KC - 1 and hpart == 1))
                last.then_inc(s_unit, 1)

            def scores(qT, kT, shared, b, done):
                n = (b + 1) * P
                o = pair_bank(4)
                for j in range(2):
                    for par in range(2):
                        r = slice(DH * par, DH * par + DH)
                        k = kT[r, 0:n] if shared else kT[r, j, 0:n]
                        last = pe.matmul(o[:, 2 * par + j, 0:n], qT[r, j, b * P:(b + 1) * P], k,
                                         start=True, stop=True)
                last.then_inc(done, 1)

            stay_warm(7, 20)
            pe.wait_ge(s_hTa, TB)
            pe.wait_ge(s_hTd, TB)
            loaded(pe, "s_idx")
            w = slot("s_idx", IDXC)
            by_channel(w, 0, BW)
            by_channel(w, BW, 2 * DH)
            loaded(pe, "s_dsa")
            w = slot("s_dsa", DSAC)
            by_token(w, BW, DH + 2 * NH)
            pe.wait_ge(s_uout["iq"], 1)
            pe.wait_ge(s_uout["ikdk"], 1)
            scores(iqT, ikT, True, 0, s_idx)
            by_channel(w, 0, BW)
            pe.wait_ge(s_rel, 1)
            scores(iqT, ikT, True, 1, s_idx)
            pe.wait_ge(s_hTlo, 1)
            w = weight_parts("s_fox")
            by_channel_parts(w, 0, s_wlo["s_fox"])
            by_channel_parts(w, BW)
            pe.wait_ge(s_vr, 16 * (len(vec_src) - 2))
            pe.transpose(bank[:, 7, 0:NROW], vrows[:, :], ident[0:NROW, 0:NROW]).then_inc(s_vT, 1)
            pe.wait_ge(s_lsb, 2)
            pe.wait_ge(s_const, 1)
            o = pair_bank(0)
            for hh in range(NH):
                h = 2 * (hh % 2) + hh // 2
                pe.matmul(o[:, hh, :], lsb[:, 0, h, :], tri[:, P:P + T], start=True, stop=False)
                pe.matmul(o[:, hh, :], lsb[:, 1, h, :], tri[:, 0:T], start=False, stop=True)
            pe.matmul(bank[:, 6, 0:NH], tri[:, P:2 * P], fs[:, 5, 0, :], start=True, stop=True)
            pe.matmul(bank[:, 6, NH:2 * NH], tri[:, 2 * P:3 * P], fs[:, 5, 0, :], start=True, stop=False)
            pe.matmul(bank[:, 6, NH:2 * NH], tri[:, P:2 * P], fs[:, 5, 1, :], start=False, stop=True)\
                .then_inc(s_cum, 1)
            w = weight_parts("s_val")
            by_token_parts(w, BW, s_wlo["s_val"])
            pe.wait_ge(s_uout["fq"], 1)
            pe.wait_ge(s_uout["fk"], 1)
            pe.wait_ge(s_rel, 2)
            scores(fqT, fkT, False, 0, s_s)
            by_channel_parts(w, 0)
            pe.wait_ge(s_lg, 1)
            scores(fqT, fkT, False, 1, s_s)
            w = weight_parts("s_conv")
            by_channel_parts(w, BW, s_wlo["s_conv"])
            by_channel_parts(w, 0)

            def gate(t, b):
                w = [rounded_slot(tile_part(t, i)) for i in range(2)]
                if t:
                    pe.wait_ge(s_gout, 2 * (t - 1) + b + 1)
                elif b == 0:
                    pe.wait_ge(s_cumo, 1)
                for k in range(KC):
                    if b == 0 and k % 2 == 0:
                        pe.wait_ge(s_lo[t % 2], 4 * (t // 2) + k // 2 + 1)
                    for hpart, wpart in PRODUCTS:
                        last = pe.matmul(bank[:, b, :], hT_part[hpart][:, k, b * P:(b + 1) * P],
                                         w[wpart][:, k, :], start=(k == 0 and hpart == wpart),
                                         stop=(k == KC - 1 and hpart == 1))
                last.then_inc(s_gate, 1)

            nturn = [0]

            def turn(i, kc):
                if nturn[0] == 0:
                    pe.wait_ge(s_cumo, 1)
                else:
                    pe.wait_ge(s_pTo, nturn[0])
                nturn[0] += 1
                pe.wait_ge(s_prob, i + 1)
                b = i % TB
                for hh in range(NH):
                    last = pe.transpose(bank[:, 6, hh * P:(hh + 1) * P],
                                        logit[b][:, hh, kc * P:(kc + 1) * P], ident[:, :])
                last.then_inc(s_pT, 1)

            def weigh(i, value):
                b = i % TB
                pe.wait_ge(s_pTo, nturn[0])
                if i == 0:
                    pe.wait_ge(s_vcol, 2)
                if i == TB:
                    pe.wait_ge(s_att, 1)
                for hh in range(NH):
                    par, j = hh // 2, hh % 2
                    for kc in range(b + 1):
                        last = pe.matmul(bank[DH * par:DH * par + DH, 7, j * T + b * P:j * T + (b + 1) * P],
                                         value(kc, 2 * j + par), probT[:, kc, hh * P:(hh + 1) * P],
                                         start=(kc == 0), stop=(kc == b))
                last.then_inc(s_pv, 1)

            def fox_v(kc, h):
                return fv[:, kc, h * DH:(h + 1) * DH]

            def dsa_v(kc, h):
                return misc[:, kc, 0:DH]

            gate(0, 0)
            gate(0, 1)
            turn(0, 0)
            gate(1, 0)
            weigh(0, fox_v)
            turn(1, 0)
            gate(1, 1)
            turn(1, 1)
            gate(2, 0)
            weigh(1, fox_v)
            pe.wait_ge(s_lg, 2)
            scores(dqT, dkT, True, 0, s_s)
            gate(2, 1)
            gate(3, 0)
            turn(2, 0)
            gate(3, 1)
            weigh(2, dsa_v)
            pe.wait_ge(s_lg, 3)
            scores(dqT, dkT, True, 1, s_s)
            gate(4, 0)
            gate(4, 1)
            turn(3, 0)
            gate(5, 0)
            turn(3, 1)
            gate(5, 1)
            weigh(3, dsa_v)
            pe.wait_ge(s_poolin, 1)
            pe.wait_ge(s_small, 16 * 8)
            pe.wait_ge(s_uout["conva"], 1)
            for g in range(4):
                r = slice(DH * (g % 2), DH * (g % 2) + DH)
                last = pe.matmul(bank[r, 2 + g % 2, (g // 2) * T:(g // 2 + 1) * T], poolw[r, g // 2, :],
                                 pooled[0][r, g // 2, PADP:PADP + T], start=True, stop=True)
            last.then_inc(s_poolmm, 1)
            gate(6, 0)
            gate(6, 1)
            pe.wait_ge(s_conv, 1)
            pe.wait_ge(s_pTo, 6)
            for t in range(TB):
                for c in range(2):
                    last = pe.transpose(bank[:, 6, t * T + c * P:t * T + (c + 1) * P],
                                        convy[:, c, t * P:(t + 1) * P], ident[:, :])
            last.then_inc(s_cT, 1)
            gate(7, 0)
            pe.wait_ge(s_cz, 1)
            pe.wait_ge(s_att, 2)
            for c in range(2):
                for t in range(TB):
                    last = pe.transpose(bank[:, 7, c * T + t * P:c * T + (t + 1) * P],
                                        glu[:, t, c * P:(c + 1) * P], ident[:, :])
            last.then_inc(s_czT, 1)
            gate(7, 1)

            pe.wait_ge(s_att, 2)
            pe.wait_ge(s_poolo, 1)

            def turn_merged(i):
                pe.wait_ge(s_mix, 8 * (i // 2 + 1))
                if i < 2:
                    pe.wait_ge(s_lg, 4)
                else:
                    pe.wait_ge(s_mTlo, i - 1)
                for kk in range(2):
                    for t in range(TB):
                        k = 2 * i + kk
                        last = pe.transpose(bank[:, 4 + i % 2, kk * T + t * P:kk * T + (t + 1) * P],
                                            work[:, t, k * P:(k + 1) * P], ident[:, :])
                last.then_inc(s_mT, 1)

            def out_part(j, t, k0, k1):
                if k0 == 0:
                    pe.wait_ge(s_mix, 13 + 2 * t + j)
                w = [rounded_slot(i) for i in WO_PART[j]]
                for k in range(k0, k1):
                    if k % 2 == 0:
                        pe.wait_ge(s_mTlo, k // 2 + 1)
                        pe.wait_ge(s_wolo, 4 * j + k // 2 + 1)
                    for mpart, wpart in ((0, 0), (0, 1), (1, 0)):
                        last = pe.matmul(bank[:, 2 * t + j, :], merged_part[mpart][:, k, t * P:(t + 1) * P],
                                         w[wpart][:, k, :], start=(k == 0 and mpart == wpart),
                                         stop=(k == KC - 1 and mpart == 1))
                if k1 == KC:
                    last.then_inc(s_o, 1)

            i = 0
            for dq in range(2):
                w = [rounded_slot(i) for i in WB_PART[dq]]
                for t in range(TB):
                    for n in range(NB):
                        if i < 2:
                            pe.wait_ge(s_gout, 16)
                        if t == 0:
                            pe.wait_ge(s_wblo[dq], n + 1)
                            pe.wait_ge(s_brlo, NB if n == 3 else NB - 1)
                        if i >= 4:
                            pe.wait_ge(s_mix, i - 3)
                        for kc in range(2):
                            for bpart, wpart in ((0, 0), (0, 1), (1, 0)):
                                last = pe.matmul(bank[:, i % 4, :], br_part[bpart][:, n, kc, t * P:(t + 1) * P],
                                                 w[wpart][:, 2 * n + kc, :],
                                                 start=(kc == 0 and bpart == wpart),
                                                 stop=(kc == 1 and bpart == 1))
                        last.then_inc(s_up, 1)
                        i += 1
                    if dq == 1 and t == 0:
                        turn_merged(0)
                        turn_merged(1)
            out_part(0, 0, 0, KC // 2)
            turn_merged(2)
            out_part(0, 1, 0, KC // 2)
            turn_merged(3)
            for t in range(TB):
                out_part(0, t, KC // 2, KC)
            for t in range(TB):
                out_part(1, t, 0, KC)
            turn_rows(s_z1, 4, s_zT)
            for t in range(TB):
                pe.wait_ge(s_h1Ta, t + 2)
                if t:
                    pe.wait_ge(s_h1Td, 1)
                for k in range(KC):
                    last = pe.matmul(bank[0:NG + NE, t, 0:P], rw[:, k, :], hT[:, k, t * P:(t + 1) * P],
                                     start=(k == 0), stop=(k == KC - 1))
                last.then_inc(s_rtT, 1)
            for t in range(TB):
                pe.wait_ge(s_rtTo, t + 1)
                last = pe.transpose(bank[:, 2, t * 32:t * 32 + NG + NE], lgT[0:NG + NE, t * P:(t + 1) * P],
                                    ident[0:NG + NE, 0:NG + NE])
            last.then_inc(s_rt, 1)
            stay_warm(3, 24)
            pe.wait_ge(s_mask, 1)
            mask = rt[:, 12, :, :]
            o = bank[:, 1, 0:TB * NE]
            pe.matmul(o[:, 0:TB * NE], tri[:, P:2 * P], mask.rearrange("p t e -> p (t e)"),
                      start=True, stop=False)
            pe.matmul(o[:, NE:2 * NE], tri[:, 2 * P:3 * P], mask[:, 0, :], start=False, stop=True)\
                .then_inc(s_rank, 1)
            pe.matmul(bank[:, 7, 0:NE], tri[:, 2 * P:3 * P], mask[:, 0, :], start=True, stop=False)
            pe.matmul(bank[:, 7, 0:NE], tri[:, 2 * P:3 * P], mask[:, 1, :], start=False, stop=True)\
                .then_inc(s_tot, 1)

            def gather(chunks):
                for k in chunks:
                    for t in range(TB):
                        last = pe.matmul(bank[:, 2 + k // 4, (k % 4) * P:(k % 4 + 1) * P],
                                         work[:, t, k * P:(k + 1) * P],
                                         disp[:, t].rearrange("p e s -> p (e s)"),
                                         start=(t == 0), stop=(t == TB - 1))
                    if k == KC // 2 - 1:
                        last.then_inc(m_xg0, 1)
                    if k == KC - 1:
                        last.then_inc(m_xg, 1)

            pe.wait_ge(m_disp, 1)
            pe.wait_ge(s_h1, TB)
            gather(range(KC))
            pe.wait_ge(s_np, 1)
            npass = pe.value_load(npass_i[0:1, 0:1], min_val=1, max_val=PASSES)
            with pe.Fori(0, pe.snap(npass * (PAIRS // BODY))) as body:
                for j in range(BODY):
                    it = body * BODY + j

                    def weights(part):
                        load = 6 * j + part
                        s = load % RING
                        each = BODY * 6 // RING
                        pe.wait_ge(s_slot[s], body * (32 * each) + FIRST[s] + 32 * (load // RING + 1))
                        return expert_slot(s)

                    pe.wait_ge(m_xga, it + 1)
                    for part in range(4):
                        if part == 1:
                            pe.wait_ge(m_xgd, it + 1)
                        h = part % 2
                        w = weights(part)
                        for k in range(FC):
                            for e in range(2):
                                last = pe.matmul(bank[CAP * e:CAP * e + CAP, part // 2, :],
                                                 xg[:, FC * h + k, CAP * e:CAP * e + CAP], w[:, e, k, :],
                                                 start=(h == 0 and k == 0), stop=(h == 1 and k == FC - 1))
                        last.then_inc(PART_USED[part], 1)
                    pe.wait_ge(m_dispw, it + 1)
                    pe.wait_ge(m_acc, it * 4 + 1)
                    for t in range(TB):
                        last = pe.transpose(bank[:, 7, t * P:(t + 1) * P],
                                            dispw[:, t].rearrange("p e s -> p (e s)"), ident[:, :])
                    last.then_inc(m_cT, 1)
                    pe.wait_ge(m_disp, it + 2)
                    gather(range(0, 2))
                    pe.wait_ge(m_h, it + 1)
                    for f in range(FC):
                        last = pe.transpose(bank[:, 4, f * P:(f + 1) * P], hexp[:, f * P:(f + 1) * P],
                                            ident[:, :])
                    last.then_inc(m_hT, 1)
                    gather(range(2, 4))
                    pe.wait_ge(m_hTo, it + 1)
                    for half in range(2):
                        w = weights(4 + half)
                        for f in range(FC):
                            for e in range(2):
                                last = pe.matmul(bank[CAP * e:CAP * e + CAP, 5 + half, :],
                                                 hexT[:, f * P + CAP * e:f * P + CAP * e + CAP],
                                                 w[:, e, f, :], start=(f == 0), stop=(f == FC - 1))
                        last.then_inc(PART_USED[4 + half], 1)
                        gather(range(4 + 2 * half, 6 + 2 * half))
                        if half == 0:
                            pe.wait_ge(m_cTo, it + 1)
                            pe.wait_ge(m_yd, it + 1)
                        else:
                            pe.wait_ge(m_ya, it + 1)
                        for t in range(TB):
                            i = 2 * half + t
                            if i >= 2:
                                pe.wait_ge(m_acc, it * 4 + i)
                            pe.matmul(bank[:, 7 if i % 2 == 0 else 4, :], comb[:, t * P:(t + 1) * P],
                                      yexp[:, half * HALF:(half + 1) * HALF], start=True, stop=True)\
                                .then_inc(m_c, 1)

        @block.vector
        def _(dve):
            n = [0]

            def chain(ins):
                n[0] += 1
                ins.then_inc(s_dch, 1)
                return n[0]

            def link(ins):
                dve.wait_ge(s_dch, chain(ins))

            nln = [0]

            def half_stats(t, src, i):
                link(dve.bn_stats(stats[:, t, i, :], src))

            def row_var(t, parts):
                link(dve.bn_aggr(mv[:, t, 0:2], stats[:, t, 0:parts, :]))
                dve.tensor_scalar(mv[:, t, 2:3], mv[:, t, 1:2], EPS, None, ALU.add).then_inc(s_var, 1)

            def row_stats(t, src, width):
                parts = (width + HALF - 1) // HALF
                for i in range(parts):
                    w = width // parts
                    last = dve.bn_stats(stats[:, t, i, :], src[:, i * w:(i + 1) * w])
                link(last)
                row_var(t, parts)

            def inverse_std(t):
                nln[0] += 1
                dve.wait_ge(s_std, nln[0])
                link(dve.reciprocal(mv[:, t, 4:5], mv[:, t, 3:4]))

            def normalise(t, src, dst):
                return dve.tensor_scalar(dst, src, mv[:, t, 0:1], mv[:, t, 4:5], ALU.subtract, ALU.mult)

            for t in range(TB):
                dve.wait_ge(s_x[t], 16)
                row_stats(t, work[:, t, :], D)
            for t in range(TB):
                inverse_std(t)
                normalise(t, work[:, t, :], work[:, t, :]).then_inc(s_z, 1)
            dve.wait_ge(s_vT, 1)
            dve.tensor_copy(vcol[:, 0:NIN], bank[:, 4, 0:NIN]).then_inc(s_vcol, 1)
            dve.wait_ge(s_vcol, 1)

            def turned_rows(t, turned, bk, gain, bias, done):
                dve.wait_ge(turned, t + 1)
                for k in range(KC // 2, KC):
                    c = k - KC // 2
                    last = dve.tensor_scalar(hT[:, k, t * P:(t + 1) * P],
                                             bank[:, bk + 2 * t + 1, c * P:(c + 1) * P],
                                             vcol[:, ROW[gain] + k:ROW[gain] + k + 1],
                                             vcol[:, ROW[bias] + k:ROW[bias] + k + 1], ALU.mult, ALU.add)
                last.then_inc(done, 1)

            for t in range(TB):
                turned_rows(t, s_xT, 0, "ln_in_g", "ln_in_b", s_hTd)
            dve.wait_ge(s_hThi, 1)
            dve.tensor_tensor(hT_part[1], hT[:, :, :], hT_part[0], ALU.subtract).then_inc(s_hTlo, 1)
            for q in range(4):
                c = slice(q * QUARTER, (q + 1) * QUARTER)
                dve.wait_ge(s_whi["s_fox"], q + 1)
                dve.tensor_tensor(rounded[SLOT["s_fox"]][:, c], ring[:, SLOT["s_fox"], c],
                                  rounded[ROUNDED_AT["s_fox"]][:, c], ALU.subtract)\
                    .then_inc(s_wlo["s_fox"], 1)
            dve.wait_ge(s_uout["misc"], 1)
            dve.wait_ge(s_bf, 16)
            link(dve.tensor_tensor(fs[:, 0], misc[:, :, DH + NH:DH + 2 * NH],
                                   bforget[:, :].unsqueeze(1).broadcast_to([P, TB, NH]), ALU.add))
            link(dve.tensor_scalar(fs[:, 1], fs[:, 0], -1.0, None, ALU.mult))
            dve.tensor_tensor(fs[:, 1], fs[:, 0], fs[:, 1], ALU.max).then_inc(s_ls, 1)
            dve.wait_ge(s_lsa, 1)
            dve.tensor_scalar(fs[:, 3], fs[:, 2], 1.0, None, ALU.add).then_inc(s_ls, 1)

            def index_score(b):
                m = (b + 1) * P
                dve.wait_ge(s_rel, b + 1)
                for h in range(NH):
                    hh = 2 * (h % 2) + h // 2
                    w = misc[:, b, DH + h:DH + h + 1]
                    if h == 0:
                        ins = dve.tensor_scalar(score[b][:, :], rel[:, hh, 0:m], w, None, ALU.mult)
                    else:
                        ins = dve.scalar_tensor_tensor(out=score[b][:, :], in0=rel[:, hh, 0:m], scalar=w,
                                                       in1=score[b][:, :], op0=ALU.mult, op1=ALU.add)
                    link(ins)
                dve.tensor_tensor(score[b][:, :], score[b][:, :], causal[:, T - m:T], ALU.add)\
                    .then_inc(s_relu_used, 1)
                dve.wait_ge(s_relu_used, b + 1)

            def select(b):
                s = score[b][:, :]
                for r in range(ROUNDS):
                    link(dve.max(top8[:, :], s))
                    link(dve.match_replace(s, top8[:, :], s, TAKEN))
                link(dve.tensor_scalar(s, s, TAKEN / 2, NEG, ALU.is_gt, ALU.mult))
                link(dve.tensor_tensor(s, s, causal[:, T - (b + 1) * P:T], ALU.add))

            def tile_rest(t):
                for q in range(4):
                    c = slice(q * QUARTER, (q + 1) * QUARTER)
                    dve.wait_ge(s_hi, 4 * t + q + 1)
                    dve.tensor_tensor(rounded[SLOT[f"g{t}"]][:, c], ring[:, SLOT[f"g{t}"], c],
                                      rounded[tile_part(t, 0)][:, c], ALU.subtract).then_inc(s_lo[0], 1)

            dve.wait_ge(s_const, 1)
            index_score(0)
            dve.wait_ge(s_lsa, 2)
            dve.scalar_tensor_tensor(out=fs[:, 5], in0=fs[:, 0], scalar=0.0, in1=fs[:, 4],
                                     op0=ALU.min, op1=ALU.subtract).then_inc(s_lsb, 1)
            dve.wait_ge(s_lsb, 1)
            dve.tensor_copy(lsb[:, :, :, :], fs[:, 5].unsqueeze(3).broadcast_to([P, TB, NH, P]))\
                .then_inc(s_lsb, 1)
            index_score(1)
            select(0)
            link(dve.reciprocal(rcnt[:, :, :], rcnt[:, :, :]))
            dve.wait_ge(s_vT, 2)
            dve.tensor_copy(vcol[:, NIN:NROW], bank[:, 7, NIN:NROW]).then_inc(s_vcol, 1)
            dve.wait_ge(s_cum, 1)
            dve.tensor_copy(cq[:, :, :], bank[:, 6, 0:TB * NH].rearrange("p (t h) -> p t h", t=TB))
            dve.scalar_tensor_tensor(out=fbias0[:, :, :], in0=pair_bank(0)[:, :, 0:P], scalar=-1.0,
                                     in1=causal[:, P:T].unsqueeze(1).broadcast_to([P, NH, P]),
                                     op0=ALU.mult, op1=ALU.add)
            dve.scalar_tensor_tensor(out=fbias1[:, :, :], in0=pair_bank(0), scalar=-1.0,
                                     in1=causal[:, :].unsqueeze(1).broadcast_to([P, NH, T]),
                                     op0=ALU.mult, op1=ALU.add).then_inc(s_cumo, 1)
            dve.wait_ge(s_cumo, 1)

            def negmax(i):
                b = i % TB
                dve.tensor_reduce(smx[:, i // TB, b, 0, :], logit[b][:, :, :], AX.X, ALU.max,
                                  negate=True).then_inc(s_lg, 1)

            def probs(i):
                b = i % TB
                s = smx[:, i // TB, b]
                dve.wait_ge(s_exp, i + 1)
                link(dve.reciprocal(s[:, 2, :], s[:, 1, :]))
                for hh in range(NH):
                    last = dve.tensor_scalar(logit[b][:, hh, :], logit[b][:, hh, :], s[:, 2, hh:hh + 1],
                                             None, ALU.mult)
                last.then_inc(s_prob, 1)

            def fox(b):
                fb = fbias1 if b else fbias0
                m = (b + 1) * P
                dve.wait_ge(s_s, b + 1)
                for hh in range(NH):
                    h = 2 * (hh % 2) + hh // 2
                    last = dve.scalar_tensor_tensor(out=logit[b][:, hh, :], in0=pair_bank(4)[:, hh, 0:m],
                                                    scalar=cq[:, b, h:h + 1], in1=fb[:, hh, :],
                                                    op0=ALU.add, op1=ALU.add)
                link(last)
                negmax(b)

            def dsa(b):
                m = (b + 1) * P
                for hh in range(NH):
                    h = 2 * (hh % 2) + hh // 2
                    last = dve.scalar_tensor_tensor(out=alibi[:, hh, 0:m], in0=dist[:, T - m:T],
                                                    scalar=-SLOPES[h], in1=score[b][:, :],
                                                    op0=ALU.mult, op1=ALU.add)
                link(last)
                dve.wait_ge(s_s, TB + b + 1)
                dve.wait_ge(s_pT, 1 if b == 0 else 3)
                link(dve.tensor_tensor(logit[b][:, :, :], pair_bank(4)[:, :, 0:m], alibi[:, :, 0:m], ALU.add))
                negmax(TB + b)

            done = [0, 0]

            def tap(taps):
                for j in taps:
                    for c in range(2):
                        w = vcol[:, ROW["conv_dw"] + 2 * j + c:ROW["conv_dw"] + 2 * j + c + 1]
                        src = hpad[:, c, j:j + T]
                        if j == 0:
                            b = ROW["conv_b"] + c
                            ins = dve.tensor_scalar(convy[:, c, :], src, w, vcol[:, b:b + 1], ALU.mult, ALU.add)
                        else:
                            dve.wait_ge(s_dch, done[c])
                            ins = dve.scalar_tensor_tensor(out=convy[:, c, :], in0=src, scalar=w,
                                                           in1=convy[:, c, :], op0=ALU.mult, op1=ALU.add)
                        if j == CONV_W - 1 and c == 1:
                            ins.then_inc(s_conv, 1)
                        else:
                            done[c] = chain(ins)

            fox(0)
            probs(0)
            tile_rest(0)
            fox(1)
            probs(1)
            dve.wait_ge(s_unit, len(UNITS))
            dve.wait_ge(s_uout["convb"], 1)
            dve.tensor_tensor(hpad[:, :, PADC:PADC + T], bank[:, 3, :].rearrange("p (c t) -> p c t", c=2),
                              glu[:, :, :], ALU.mult).then_inc(s_uout["conva"], 1)
            dve.wait_ge(s_uout["conva"], 1)
            select(1)
            dve.wait_ge(s_vcol, 2)
            tap(range(0, 5))
            tile_rest(2)
            tap(range(5, 20))
            dsa(0)
            probs(2)
            tile_rest(4)
            tap(range(20, 26))
            dsa(1)
            tap(range(26, 29))
            probs(3)
            tap(range(29, CONV_W))
            dve.wait_ge(s_uout["pool"], 1)
            pmean = glu
            src = poolv
            for g, w in enumerate(WINDOWS):
                dst = pooled[g % 2]
                j0 = g // 2
                link(dve.tensor_tensor(dst[:, j0:2, PADP:], src[:, j0:2, PADP:],
                                       src[:, j0:2, PADP - w // 2:PADP + T - w // 2], ALU.add))
                r = slice(DH * (g % 2), DH * (g % 2) + DH)
                link(dve.tensor_tensor(pmean[r, g // 2, :], dst[r, g // 2, PADP:], rcnt[r, g // 2, :], ALU.mult))
                src = dst
            dve.tensor_tensor(pooled[0][:, :, PADP:], pmean[:, :, :], poolv[:, :, PADP:], ALU.subtract)\
                .then_inc(s_poolin, 1)
            tile_rest(6)

            def split_branch(n):
                link(dve.tensor_copy(br_part[0][:, n], brT[:, n]))
                dve.tensor_tensor(br_part[1][:, n], brT[:, n], br_part[0][:, n], ALU.subtract)\
                    .then_inc(s_brlo, 1)

            dve.wait_ge(s_hn, TB)
            dve.wait_ge(s_att, 2)
            split_branch(1)
            split_branch(2)
            dve.wait_ge(s_poolo, 1)
            split_branch(0)
            dve.wait_ge(s_cT, 1)
            for t in range(TB):
                row_stats(t, bank[:, 6, t * T:(t + 1) * T], BW)
            for t in range(TB):
                inverse_std(t)
            for t in range(TB):
                last = normalise(t, bank[:, 6, t * T:(t + 1) * T], glu[:, t, :])
            last.then_inc(s_cz, 1)
            loaded(dve, "wb0")
            dve.wait_ge(s_gate, 14)
            for q in range(4):
                c = slice(q * QUARTER, (q + 1) * QUARTER)
                link(dve.tensor_copy(rounded[WB_PART[0][0]][:, c], ring[:, SLOT["wb0"], c]))
                dve.tensor_tensor(rounded[SLOT["wb0"]][:, c], ring[:, SLOT["wb0"], c],
                                  rounded[WB_PART[0][0]][:, c], ALU.subtract).then_inc(s_wblo[0], 1)
            dve.wait_ge(s_cbr, 1)
            split_branch(3)

            def merged_rest(i):
                dve.wait_ge(s_mTo, i + 1)
                c = slice(2 * i, 2 * i + 2)
                dve.tensor_tensor(merged_part[1][:, c, :],
                                  bank[:, 4 + i % 2, :].rearrange("p (c t) -> p c t", c=2),
                                  merged_part[0][:, c, :], ALU.subtract).then_inc(s_mTlo, 1)

            i = 0
            for dq in range(2):
                g = gates[:, dq, :].rearrange("p (t n c) -> p t n c", t=TB, n=NB)
                for t in range(TB):
                    o = work[:, t, dq * HALF:(dq + 1) * HALF]
                    if i == 0:
                        dve.wait_ge(s_hn, TB)
                    for nb in range(NB):
                        dve.wait_ge(s_up, i + 1)
                        dve.wait_ge(s_gsig, 4 * dq + nb + 1)
                        dst = o if nb == 0 else tmp[:, nb % 2, :]
                        ins = dve.tensor_tensor(dst, bank[:, i % 4, :], g[:, t, nb, :], ALU.mult)
                        if nb:
                            link(ins)
                            dve.tensor_tensor(o, o, tmp[:, nb % 2, :], ALU.add).then_inc(s_mix, 1)
                        else:
                            ins.then_inc(s_mix, 1)
                        i += 1
                        dve.wait_ge(s_mix, i)
                        if i in (3 * NB + 1, 3 * NB + 2):
                            merged_rest(i - 3 * NB - 1)
            merged_rest(2)
            merged_rest(3)

            def residual(t, j):
                dve.wait_ge(s_o, 2 * j + t + 1)
                c = slice(j * HALF, (j + 1) * HALF)
                link(dve.scalar_tensor_tensor(out=work[:, t, c], in0=hn[:, t, c], scalar=ALPHA,
                                              in1=bank[:, 2 * t + j, :], op0=ALU.mult, op1=ALU.add))

            for t in range(TB):
                residual(t, 0)
                half_stats(t, work[:, t, 0:HALF], 0)
            for t in range(TB):
                residual(t, 1)
                half_stats(t, work[:, t, HALF:D], 1)
                row_var(t, 2)
                inverse_std(t)
                normalise(t, work[:, t, :], work[:, t, :]).then_inc(s_z1, 1)
            turned_rows(1, s_zT, 4, "ln1_g", "ln1_b", s_h1Td)
            for t in range(TB):
                dve.wait_ge(s_rtT, t + 1)
                dve.tensor_copy(lgT[0:NG + NE, t * P:(t + 1) * P], bank[0:NG + NE, t, 0:P]).then_inc(s_rtTo, 1)
            dve.wait_ge(s_rt, 1)
            R = [rt[:, i] for i in range(16)]
            link(dve.tensor_tensor(lg, bank[:, 2, 0:TB * 32].rearrange("p (t n) -> p t n", t=TB)[:, :, 0:NG + NE],
                                   rbias[:, :].unsqueeze(1).broadcast_to([P, TB, NG + NE]), ALU.add))
            assert NG == EPG
            NR = NG + 1
            rows = TB * NR
            order = desc4[:, :].unsqueeze(1).broadcast_to([P, rows, EPG])

            def first_max(v, val, hot, s):
                link(dve.tensor_reduce(val, v, AX.X, ALU.max))
                link(dve.tensor_tensor(s, v, val.unsqueeze(2).broadcast_to([P, rows, EPG]), ALU.is_equal))
                link(dve.tensor_tensor(s, s, order, ALU.mult))
                link(dve.tensor_reduce(rv[:, 2, :], s, AX.X, ALU.max))
                link(dve.tensor_tensor(hot, s, rv[:, 2, :].unsqueeze(2).broadcast_to([P, rows, EPG]),
                                       ALU.is_equal))

            quads = [rq[:, i, :].rearrange("p (r j) -> p r j", j=EPG) for i in range(5)]
            v1 = lg.rearrange("p t (r j) -> p (t r) j", j=EPG)
            v2, hot1, hot2, s4, chosen = quads

            def by_group(q):
                return q.rearrange("p (t r) j -> p t r j", t=TB)[:, :, 1:NR, :]

            first_max(v1, rv[:, 0, :], hot1, s4)
            link(dve.scalar_tensor_tensor(out=v2, in0=hot1, scalar=TAKEN, in1=v1, op0=ALU.mult, op1=ALU.add))
            first_max(v2, rv[:, 1, :], hot2, s4)
            hotg4 = hot1.rearrange("p (t r) j -> p t r j", t=TB)[:, :, 0, :].unsqueeze(3)\
                .broadcast_to([P, TB, NG, EPG])
            link(dve.tensor_tensor(chosen, hot1, hot2, ALU.add))
            dve.tensor_tensor(R[12].rearrange("p t (g j) -> p t g j", g=NG), hotg4, by_group(chosen),
                              ALU.mult).then_inc(s_mask, 1)
            top = rv[:, :, :].rearrange("p i (t r) -> p i t r", t=TB)
            link(dve.tensor_tensor(R[7][:, :, 0:NG], lg[:, :, 0:NG],
                                   top[:, 0, :, 0:1].broadcast_to([P, TB, NG]), ALU.subtract))
            dve.tensor_tensor(R[7][:, :, NG:NG + NR], top[:, 1], top[:, 0], ALU.subtract).then_inc(s_re, 1)
            dve.wait_ge(s_rank, 1)
            ranks = bank[:, 1, 0:2 * NE].rearrange("p (t e) -> p t e", t=TB)
            link(dve.tensor_tensor(R[14], ranks, R[12], ALU.mult))
            slots = slot_no[:, :].unsqueeze(1).broadcast_to([P, 2, CAP])

            def dispatch(it):
                for t in range(TB):
                    r = rankp[:, bass.ds(it, 1), t, :].rearrange("p o e -> p (o e)")
                    last = dve.tensor_tensor(disp[:, t], slots, r.unsqueeze(2).broadcast_to([P, 2, CAP]),
                                             ALU.is_equal)
                last.then_inc(m_disp, 1)

            def pass_ranks(q):
                for t in range(TB):
                    last = dve.tensor_scalar(rankp[:, q * PAIRS:(q + 1) * PAIRS, t, :],
                                             R[14][:, t].rearrange("p (i e) -> p i e", e=2),
                                             -1.0 - CAP * q, None, ALU.add)
                return last

            link(pass_ranks(0))
            dispatch(0)
            dve.wait_ge(s_rex, 1)
            e2 = R[8][:, :, NG + 1:NG + NR]
            link(dve.tensor_reduce(R[10][:, :, 0], R[8][:, :, 0:NG], AX.X, ALU.add))
            link(dve.tensor_scalar(R[10][:, :, 1:NR], e2, 1.0, None, ALU.add))
            link(dve.reciprocal(R[10][:, :, 0:NR], R[10][:, :, 0:NR]))
            link(dve.tensor_tensor(R[9][:, :, 0:NG], R[10][:, :, 1:NR],
                                   R[10][:, :, 0:1].broadcast_to([P, TB, NG]), ALU.mult))
            link(dve.tensor_tensor(R[9][:, :, NG:2 * NG], R[9][:, :, 0:NG], e2, ALU.mult))
            for hot, c in ((hot1, 0), (hot2, NG)):
                link(dve.tensor_tensor(by_group(hot), by_group(hot), R[9][:, :, c:c + NG].unsqueeze(3)
                                       .broadcast_to([P, TB, NG, EPG]), ALU.mult))
            link(dve.tensor_tensor(by_group(hot1), by_group(hot1), by_group(hot2), ALU.add))
            link(dve.tensor_tensor(R[13].rearrange("p t (g j) -> p t g j", g=NG), hotg4, by_group(hot1),
                                   ALU.mult))
            dve.memset(npass_f[:, 0:1], 1.0)
            dve.wait_ge(s_tot, 1)
            link(dve.tensor_reduce(npass_f[:, 6:7], bank[:, 7, 0:NE], AX.X, ALU.max))
            for q in range(1, PASSES):
                last = dve.tensor_scalar(npass_f[:, q:q + 1], npass_f[:, 6:7], CAP * q + 0.5, None, ALU.is_gt)
            link(last)
            link(dve.tensor_reduce(npass_f[:, PASSES:PASSES + 1], npass_f[:, 0:PASSES], AX.X, ALU.add))
            dve.tensor_copy(npass_i[:, :], npass_f[:, PASSES:PASSES + 1]).then_inc(s_np, 1)
            dve.memset(rankp[:, PASSES * PAIRS], -1.0)
            for q in range(PASSES):
                if q:
                    pass_ranks(q)
                for t in range(TB):
                    last = dve.tensor_copy(wpair[:, q * PAIRS:(q + 1) * PAIRS, t, :],
                                           R[13][:, t].rearrange("p (i e) -> p i e", e=2))
            link(last)
            dve.wait_ge(s_h1, TB)
            for t in range(TB):
                dve.tensor_scalar(acc[:, t, :], work[:, t, :], ALPHA, None, ALU.mult)\
                    .then_inc((m_stat, m_acc)[t], 1)

            def gathered():
                dve.tensor_copy(xg[:, KC // 2:KC, :].rearrange("p k s -> p (k s)"), bank[:, 3, :])\
                    .then_inc(m_xgd, 1)

            dve.wait_ge(m_xg, 1)
            gathered()
            dve.wait_ge(s_np, 1)
            npass = dve.value_load(npass_i[0:1, 0:1], min_val=1, max_val=PASSES)
            with dve.Fori(0, dve.snap(npass * PAIRS)) as it:
                dve.wait_ge(m_disp, it + 1)
                for t in range(TB):
                    w = wpair[:, bass.ds(it, 1), t, :].rearrange("p o e -> p (o e)")
                    last = dve.tensor_tensor(dispw[:, t], disp[:, t],
                                             w.unsqueeze(2).broadcast_to([P, 2, CAP]), ALU.mult)
                last.then_inc(m_dispw, 1)
                dve.wait_ge(m_dispw, it + 1)
                dve.wait_ge(m_xg, it + 1)
                dispatch(it + 1)
                dve.wait_ge(m_u, it + 1)
                dve.wait_ge(m_silu, it + 1)
                dve.tensor_tensor(hexp[:, :], silu_g[:, :], bank[:, 1, :], ALU.mult).then_inc(m_h, 1)
                dve.wait_ge(m_cT, it + 1)
                dve.tensor_copy(comb[:, :], bank[:, 7, 0:TB * P]).then_inc(m_cTo, 1)
                dve.wait_ge(m_hT, it + 1)
                dve.tensor_copy(hexT[:, :], bank[:, 4, :]).then_inc(m_hTo, 1)
                dve.wait_ge(m_y0, it + 1)
                dve.tensor_copy(yexp[:, 0:HALF], bank[:, 5, :]).then_inc(m_yd, 1)
                dve.wait_ge(m_acc, it * 4 + 1)
                for i in range(4):
                    half, t = divmod(i, 2)
                    if i == 2:
                        dve.wait_ge(m_xg, it + 2)
                        gathered()
                    dve.wait_ge(m_c, it * 4 + i + 1)
                    o = acc[:, t, half * HALF:(half + 1) * HALF]
                    dve.tensor_tensor(o, o, bank[:, 7 if i % 2 == 0 else 4, :], ALU.add).then_inc(m_acc, 1)
                    if half == 0:
                        dve.wait_ge(m_acc, it * 4 + i + 2)
                        dve.wait_ge(m_stat, it * 2 + i + 1)
                        dve.bn_stats(stats[:, t, 0, :], o).then_inc(m_stat, 1)
            dve.wait_ge(m_acc, dve.snap(npass * (4 * PAIRS) + 1))
            dve.wait_ge(s_lnp, 96)
            dve.wait_ge(m_stat, dve.snap(npass * (2 * PAIRS) + 1))
            for t in range(TB):
                half_stats(t, acc[:, t, HALF:D], 1)
                row_var(t, 2)

            def scaled(t, c):
                link(dve.scalar_tensor_tensor(out=work[:, t, c], in0=acc[:, t, c], scalar=mv[:, t, 0:1],
                                              in1=lnp[:, 0, c], op0=ALU.subtract, op1=ALU.mult))
                dve.scalar_tensor_tensor(out=work[:, t, c], in0=work[:, t, c], scalar=mv[:, t, 4:5],
                                         in1=lnp[:, 1, c], op0=ALU.mult, op1=ALU.add).then_inc(s_fin, 1)

            inverse_std(0)
            inverse_std(1)
            dve.tensor_scalar(mv[:, 1, 5:6], mv[:, 1, 0:1], mv[:, 1, 4:5], -1.0, ALU.mult, ALU.mult)\
                .then_inc(s_shift, 1)
            scaled(0, slice(0, D))
            scaled(1, slice(0, HALF))


_INS = ["x", "ln_in_g", "ln_in_b", "w_in", "b_forget", "b_gate", "pool_w", "pool_scale", "conv_dw", "conv_b",
        "conv_ln_g", "conv_ln_b", "w_branch", "w_out", "ln1_g", "ln1_b", "router_g", "router_g_b",
        "router_e", "router_e_b", "expert_w_gate", "expert_w_up", "expert_w_down", "ln2_g", "ln2_b"]


def kernel(**inputs):
    import numpy as _np
    import concourse.bacc as _bacc
    from concourse import mybir as _mybir
    from concourse.bass_utils import run_bass_kernel_spmd as _run

    nc = _bacc.Bacc("TRN2", target_bir_lowering=False, num_devices=1)
    arrays, aps = {}, {}
    for name in _INS:
        v = _np.ascontiguousarray(inputs[name])
        arrays[f"in_{name}_dram"] = v
        aps[name] = nc.dram_tensor(f"in_{name}_dram", v.shape, _mybir.dt.from_np(v.dtype),
                                   kind="ExternalInput").ap()
    shape = arrays["in_x_dram"].shape
    out = nc.dram_tensor("out_0_dram", shape, _mybir.dt.float32, kind="ExternalOutput").ap()
    hybrid_trunk_kernel(nc, aps, out)
    r = _run(nc, [arrays], core_ids=[0])
    return r.results[0]["out_0_dram"]
```
